# Optimizing a Trainium2 kernel written in Bass

```python
import jax
import jax.numpy as jnp
from jax import lax
import numpy as np
import jax, jax.numpy as jnp

D_MODEL = 1024
BATCH = 1
SEQ = 256
DEPTH = 2

EPS = 1e-6
CONV_WIDTH = 4
LRU_WIDTH = D_MODEL // 2
LRU_BLOCKS = 8
LRU_BLOCK = LRU_WIDTH // LRU_BLOCKS
LRU_C = 8.0
ATT_HEAD_DIM = 64
ATT_Q_HEADS = (D_MODEL // 2) // ATT_HEAD_DIM
ATT_KV_HEADS = 2
ATT_GROUPS = ATT_Q_HEADS // ATT_KV_HEADS
ATT_Q_WIDTH = ATT_Q_HEADS * ATT_HEAD_DIM
ATT_KV_WIDTH = ATT_KV_HEADS * ATT_HEAD_DIM
WINDOW = 128
ROPE_THETA = 10000.0
EVEN_IN_COLS = 2 * LRU_WIDTH + ATT_Q_WIDTH + 2 * ATT_KV_WIDTH
EVEN_MIX_WIDTH = LRU_WIDTH + ATT_Q_WIDTH
D_FF_DENSE = 2816
GDN_HEADS = 8
GDN_HEAD_DIM = 128
GDN_WIDTH = GDN_HEADS * GDN_HEAD_DIM
GDN_CHUNK = 64
ODD_IN_COLS = 4 * GDN_WIDTH + 2 * GDN_HEADS
N_EXPERTS = 8
TOP_K = 2
D_FF_EXPERT = 3584
N_EVEN = (DEPTH + 1) // 2
N_ODD = DEPTH // 2


def rms_norm(x, g):
    xf = x.astype(jnp.float32)
    y = xf * lax.rsqrt(jnp.mean(xf * xf, axis=-1, keepdims=True) + EPS)
    return (y * g.astype(jnp.float32)).astype(x.dtype)

def l2_norm(x):
    return x * lax.rsqrt(jnp.sum(x * x, axis=-1, keepdims=True) + EPS)

def causal_depthwise_conv(x, w):
    seq = x.shape[1]
    xp = jnp.pad(x, ((0, 0), (CONV_WIDTH - 1, 0), (0, 0)))
    return sum(w[j] * xp[:, j:j + seq] for j in range(CONV_WIDTH))

def rope(x, pos):
    half = x.shape[-1] // 2
    inv_freq = ROPE_THETA ** (-jnp.arange(half, dtype=jnp.float32) / half)
    ang = pos.astype(jnp.float32)[:, None] * inv_freq[None, :]
    cos = jnp.cos(ang)[None, :, None, :]
    sin = jnp.sin(ang)[None, :, None, :]
    xf = x.astype(jnp.float32)
    x1, x2 = xf[..., :half], xf[..., half:]
    return jnp.concatenate([x1 * cos - x2 * sin, x2 * cos + x1 * sin], axis=-1)

def swiglu(h, w_gate, w_up, w_down):
    return (jax.nn.silu(h @ w_gate) * (h @ w_up)) @ w_down

def rg_lru(xb, conv_w, conv_b, w_a, b_a, w_i, b_i, lam):
    bsz, seq, _ = xb.shape
    xc = causal_depthwise_conv(xb, conv_w) + conv_b
    xh = xc.reshape(bsz, seq, LRU_BLOCKS, LRU_BLOCK)
    r = jax.nn.sigmoid(jnp.einsum('bshi,hij->bshj', xh, w_a).reshape(bsz, seq, LRU_WIDTH) + b_a)
    gi = jax.nn.sigmoid(jnp.einsum('bshi,hij->bshj', xh, w_i).reshape(bsz, seq, LRU_WIDTH) + b_i)
    log_a = -LRU_C * r * jax.nn.softplus(-lam)
    a = jnp.exp(log_a)
    u = jnp.sqrt(-jnp.expm1(2.0 * log_a)) * (gi * xc)

    def combine(c1, c2):
        a1, b1 = c1
        a2, b2 = c2
        return a1 * a2, a2 * b1 + b2

    _, h = lax.associative_scan(combine, (a, u), axis=1)
    return h

def sliding_window_attention(q, k, v, sinks):
    bsz, seq = q.shape[:2]
    nb = seq // WINDOW
    qb = q.astype(jnp.float32).reshape(bsz, nb, WINDOW, ATT_KV_HEADS, ATT_GROUPS, ATT_HEAD_DIM)

    def with_prev(t):
        tb = t.astype(jnp.float32).reshape(bsz, nb, WINDOW, ATT_KV_HEADS, ATT_HEAD_DIM)
        prev = jnp.pad(tb, ((0, 0), (1, 0), (0, 0), (0, 0), (0, 0)))[:, :-1]
        return jnp.concatenate([prev, tb], axis=2)

    kb, vb = with_prev(k), with_prev(v)
    s = jnp.einsum('bnqhgd,bnkhd->bnhgqk', qb, kb) * (ATT_HEAD_DIM ** -0.5)
    qi = jnp.arange(WINDOW)[:, None] + WINDOW
    kj = jnp.arange(2 * WINDOW)[None, :]
    rel = qi - kj
    band = (rel >= 0) & (rel < WINDOW)
    valid = band[None] & ((jnp.arange(nb)[:, None, None] > 0) | (kj >= WINDOW)[None])
    s = jnp.where(valid[None, :, None, None], s, -1e30)
    sink = sinks.astype(jnp.float32).reshape(ATT_KV_HEADS, ATT_GROUPS)[None, None, :, :, None, None]
    m = jnp.maximum(jnp.max(s, axis=-1, keepdims=True), sink)
    p = jnp.exp(s - m)
    denom = jnp.sum(p, axis=-1, keepdims=True) + jnp.exp(sink - m)
    o = jnp.einsum('bnhgqk,bnkhd->bnqhgd', p / denom, vb)
    return o.reshape(bsz, seq, ATT_Q_WIDTH)

def even_mixer(h, pos, w_in, conv_w, conv_b, w_a, b_a, w_i, b_i, lam, q_norm, k_norm, sinks, w_out):
    bsz, seq, _ = h.shape
    proj = h @ w_in
    cuts = np.cumsum([LRU_WIDTH, LRU_WIDTH, ATT_Q_WIDTH, ATT_KV_WIDTH]).tolist()
    xb, gate, q, k, v = jnp.split(proj, cuts, axis=-1)
    y_lru = rg_lru(xb.astype(jnp.float32), conv_w, conv_b, w_a, b_a, w_i, b_i, lam) \
        * jax.nn.gelu(gate.astype(jnp.float32))
    q = rope(rms_norm(q.reshape(bsz, seq, ATT_Q_HEADS, ATT_HEAD_DIM), q_norm), pos)
    k = rope(rms_norm(k.reshape(bsz, seq, ATT_KV_HEADS, ATT_HEAD_DIM), k_norm), pos)
    v = v.reshape(bsz, seq, ATT_KV_HEADS, ATT_HEAD_DIM)
    y_att = sliding_window_attention(q, k, v, sinks)
    y = jnp.concatenate([y_lru.astype(h.dtype), y_att.astype(h.dtype)], axis=-1)
    return y @ w_out

def gated_deltanet(h, w_in, conv_w, a_log, dt_bias, out_norm, w_out):
    bsz, seq, _ = h.shape
    nc = seq // GDN_CHUNK
    C = GDN_CHUNK
    proj = (h @ w_in).astype(jnp.float32)
    cuts = [3 * GDN_WIDTH, 4 * GDN_WIDTH, 4 * GDN_WIDTH + GDN_HEADS]
    qkv, gate, a_in, b_in = jnp.split(proj, cuts, axis=-1)
    qkv = jax.nn.silu(causal_depthwise_conv(qkv, conv_w.astype(jnp.float32)))
    q, k, v = jnp.split(qkv, 3, axis=-1)
    q = l2_norm(q.reshape(bsz, seq, GDN_HEADS, GDN_HEAD_DIM)) * (GDN_HEAD_DIM ** -0.5)
    k = l2_norm(k.reshape(bsz, seq, GDN_HEADS, GDN_HEAD_DIM))
    v = v.reshape(bsz, seq, GDN_HEADS, GDN_HEAD_DIM)
    beta = jax.nn.sigmoid(b_in)
    g = -jnp.exp(a_log.astype(jnp.float32)) * jax.nn.softplus(a_in + dt_bias.astype(jnp.float32))

    def to_chunks(t):
        return t.reshape(bsz, nc, C, GDN_HEADS, -1).transpose(0, 3, 1, 2, 4)

    qc, kc, vc = to_chunks(q), to_chunks(k), to_chunks(v)
    gc = g.reshape(bsz, nc, C, GDN_HEADS).transpose(0, 3, 1, 2)
    bc = beta.reshape(bsz, nc, C, GDN_HEADS).transpose(0, 3, 1, 2)
    G = jnp.cumsum(gc, axis=-1)
    tri = jnp.tril(jnp.ones((C, C), dtype=bool))
    strict = jnp.tril(jnp.ones((C, C), dtype=bool), -1)
    diff = G[..., :, None] - G[..., None, :]
    decay = jnp.where(tri, jnp.exp(jnp.where(tri, diff, 0.0)), 0.0)
    kk = jnp.einsum('bhnid,bhnjd->bhnij', kc, kc)
    A = jnp.where(strict, bc[..., :, None] * kk * decay, 0.0) + jnp.eye(C, dtype=jnp.float32)
    u = lax.linalg.triangular_solve(A, bc[..., None] * vc, left_side=True, lower=True, unit_diagonal=True)
    w = lax.linalg.triangular_solve(A, bc[..., None] * jnp.exp(G)[..., None] * kc,
                                    left_side=True, lower=True, unit_diagonal=True)
    a_qk = jnp.where(tri, jnp.einsum('bhnid,bhnjd->bhnij', qc, kc) * decay, 0.0)
    q_dec = qc * jnp.exp(G)[..., None]
    k_dec = kc * jnp.exp(G[..., -1:] - G)[..., None]
    g_last = jnp.exp(G[..., -1])
    xs = (jnp.moveaxis(u, 2, 0), jnp.moveaxis(w, 2, 0), jnp.moveaxis(a_qk, 2, 0),
          jnp.moveaxis(q_dec, 2, 0), jnp.moveaxis(k_dec, 2, 0), jnp.moveaxis(g_last, 2, 0))

    def step(state, inp):
        u_c, w_c, a_c, qd_c, kd_c, gl_c = inp
        v_new = u_c - jnp.einsum('bhcd,bhde->bhce', w_c, state)
        o_c = jnp.einsum('bhcd,bhde->bhce', qd_c, state) + jnp.einsum('bhcj,bhje->bhce', a_c, v_new)
        state = state * gl_c[..., None, None] + jnp.einsum('bhcd,bhce->bhde', kd_c, v_new)
        return state, o_c

    s0 = jnp.zeros((bsz, GDN_HEADS, GDN_HEAD_DIM, GDN_HEAD_DIM), jnp.float32)
    _, o = lax.scan(step, s0, xs)
    o = o.transpose(1, 0, 3, 2, 4).reshape(bsz, seq, GDN_HEADS, GDN_HEAD_DIM)
    o = rms_norm(o, out_norm) * jax.nn.silu(gate.reshape(bsz, seq, GDN_HEADS, GDN_HEAD_DIM))
    return o.reshape(bsz, seq, GDN_WIDTH).astype(h.dtype) @ w_out

def moe_swiglu(h, router, w_gate, w_up, w_down):
    bsz, seq, d = h.shape
    t = h.reshape(-1, d)
    logits = (t @ router).astype(jnp.float32)
    top_v, top_i = lax.top_k(logits, TOP_K)
    top_w = jax.nn.softmax(top_v, axis=-1)
    gates = jnp.sum(jax.nn.one_hot(top_i, N_EXPERTS, dtype=jnp.float32) * top_w[..., None], axis=1)
    out = jnp.zeros(t.shape, jnp.float32)
    for e in range(N_EXPERTS):
        y_e = swiglu(t, w_gate[e], w_up[e], w_down[e]).astype(jnp.float32)
        out = out + gates[:, e:e + 1] * y_e
    return out.astype(h.dtype).reshape(bsz, seq, d)

def first_inputs(seed: int = 0) -> dict:
    key = jax.random.key(seed)
    ks = jax.random.split(key, 32)
    f32 = jnp.float32
    D = D_MODEL

    def nrm(k, shape, scale):
        return scale * jax.random.normal(k, shape, f32)

    lru_u = jax.random.uniform(ks[10], (N_EVEN, LRU_WIDTH), f32, minval=0.9, maxval=0.999)
    lru_s = lru_u ** (1.0 / LRU_C)
    dt = jnp.exp(jax.random.uniform(ks[21], (N_ODD, GDN_HEADS), f32,
                                    minval=float(np.log(0.001)), maxval=float(np.log(0.1))))
    return {
        "x": nrm(ks[0], (BATCH, SEQ, D), 1.0),
        "ln_mix": 1.0 + nrm(ks[1], (DEPTH, D), 0.02),
        "ln_ffn": 1.0 + nrm(ks[2], (DEPTH, D), 0.02),
        "e_w_in": nrm(ks[3], (N_EVEN, D, EVEN_IN_COLS), D ** -0.5),
        "e_lru_conv_w": nrm(ks[4], (N_EVEN, CONV_WIDTH, LRU_WIDTH), CONV_WIDTH ** -0.5),
        "e_lru_conv_b": nrm(ks[5], (N_EVEN, LRU_WIDTH), 0.02),
        "e_lru_w_a": nrm(ks[6], (N_EVEN, LRU_BLOCKS, LRU_BLOCK, LRU_BLOCK), LRU_BLOCK ** -0.5),
        "e_lru_b_a": nrm(ks[7], (N_EVEN, LRU_WIDTH), 0.1),
        "e_lru_w_i": nrm(ks[8], (N_EVEN, LRU_BLOCKS, LRU_BLOCK, LRU_BLOCK), LRU_BLOCK ** -0.5),
        "e_lru_b_i": nrm(ks[9], (N_EVEN, LRU_WIDTH), 0.1),
        "e_lru_lambda": jnp.log(lru_s) - jnp.log1p(-lru_s),
        "e_q_norm": 1.0 + nrm(ks[11], (N_EVEN, ATT_HEAD_DIM), 0.02),
        "e_k_norm": 1.0 + nrm(ks[12], (N_EVEN, ATT_HEAD_DIM), 0.02),
        "e_sinks": nrm(ks[13], (N_EVEN, ATT_Q_HEADS), 1.0),
        "e_w_out": nrm(ks[14], (N_EVEN, EVEN_MIX_WIDTH, D), EVEN_MIX_WIDTH ** -0.5),
        "e_ffn_w_gate": nrm(ks[15], (N_EVEN, D, D_FF_DENSE), D ** -0.5),
        "e_ffn_w_up": nrm(ks[16], (N_EVEN, D, D_FF_DENSE), D ** -0.5),
        "e_ffn_w_down": nrm(ks[17], (N_EVEN, D_FF_DENSE, D), D_FF_DENSE ** -0.5),
        "o_w_in": nrm(ks[18], (N_ODD, D, ODD_IN_COLS), D ** -0.5),
        "o_conv_w": nrm(ks[19], (N_ODD, CONV_WIDTH, 3 * GDN_WIDTH), CONV_WIDTH ** -0.5),
        "o_a_log": jnp.log(jax.random.uniform(ks[20], (N_ODD, GDN_HEADS), f32, minval=1.0, maxval=16.0)),
        "o_dt_bias": dt + jnp.log(-jnp.expm1(-dt)),
        "o_out_norm": 1.0 + nrm(ks[22], (N_ODD, GDN_HEAD_DIM), 0.02),
        "o_w_out": nrm(ks[23], (N_ODD, GDN_WIDTH, D), GDN_WIDTH ** -0.5),
        "o_router": nrm(ks[24], (N_ODD, D, N_EXPERTS), D ** -0.5),
        "o_moe_w_gate": nrm(ks[25], (N_ODD, N_EXPERTS, D, D_FF_EXPERT), D ** -0.5),
        "o_moe_w_up": nrm(ks[26], (N_ODD, N_EXPERTS, D, D_FF_EXPERT), D ** -0.5),
        "o_moe_w_down": nrm(ks[27], (N_ODD, N_EXPERTS, D_FF_EXPERT, D), D_FF_EXPERT ** -0.5),
    }

def first_block(x, ln_mix, ln_ffn,
              e_w_in, e_lru_conv_w, e_lru_conv_b, e_lru_w_a, e_lru_b_a, e_lru_w_i, e_lru_b_i,
              e_lru_lambda, e_q_norm, e_k_norm, e_sinks, e_w_out, e_ffn_w_gate, e_ffn_w_up, e_ffn_w_down,
              o_w_in, o_conv_w, o_a_log, o_dt_bias, o_out_norm, o_w_out, o_router,
              o_moe_w_gate, o_moe_w_up, o_moe_w_down):
    pos = jnp.arange(x.shape[1], dtype=jnp.int32)
    h = x
    for layer in range(DEPTH):
        j = layer // 2
        hn = rms_norm(h, ln_mix[layer])
        if layer % 2 == 0:
            h = h + even_mixer(hn, pos, e_w_in[j], e_lru_conv_w[j], e_lru_conv_b[j], e_lru_w_a[j],
                               e_lru_b_a[j], e_lru_w_i[j], e_lru_b_i[j], e_lru_lambda[j],
                               e_q_norm[j], e_k_norm[j], e_sinks[j], e_w_out[j]).astype(h.dtype)
            h = h + swiglu(rms_norm(h, ln_ffn[layer]), e_ffn_w_gate[j], e_ffn_w_up[j],
                           e_ffn_w_down[j]).astype(h.dtype)
        else:
            h = h + gated_deltanet(hn, o_w_in[j], o_conv_w[j], o_a_log[j], o_dt_bias[j],
                                   o_out_norm[j], o_w_out[j]).astype(h.dtype)
            h = h + moe_swiglu(rms_norm(h, ln_ffn[layer]), o_router[j], o_moe_w_gate[j],
                               o_moe_w_up[j], o_moe_w_down[j]).astype(h.dtype)
    return h


HEAD_DIM = 64
N_HEADS = D_MODEL // HEAD_DIM
HEADS_A = (N_HEADS * 3) // 8
HEADS_B = N_HEADS // 4
HEADS_C = N_HEADS - HEADS_A - HEADS_B
D_A = HEADS_A * HEAD_DIM
D_B = HEADS_B * HEAD_DIM
D_C = HEADS_C * HEAD_DIM
D_MIX = D_A + D_B + D_C
D_PROJ = 2 * D_A + 2 * D_B + 3 * D_C
CONV_A_WIDTH = 31
CONV_C_WIDTH = 3
CHUNK = 128
D_FF = 128 * ((8 * D_MODEL // 3 + 127) // 128)
RMS_EPS = 1e-6
LN_EPS = 1e-5
SPLITS = [int(s) for s in np.cumsum([D_A, D_A, D_B, D_B, D_C, D_C, D_C])[:-1]]


def rms_norm_2(x, g):
    xf = x.astype(jnp.float32)
    y = xf * lax.rsqrt(jnp.mean(xf * xf, axis=-1, keepdims=True) + RMS_EPS)
    return (y * g.astype(jnp.float32)).astype(x.dtype)

def layer_norm(x, g, b):
    xf = x.astype(jnp.float32)
    mu = jnp.mean(xf, axis=-1, keepdims=True)
    xc = xf - mu
    var = jnp.mean(xc * xc, axis=-1, keepdims=True)
    y = xc * lax.rsqrt(var + LN_EPS) * g.astype(jnp.float32) + b.astype(jnp.float32)
    return y.astype(x.dtype)

def causal_depthwise_conv_2(x, w):
    k, c = w.shape
    return lax.conv_general_dilated(
        x, w[:, None, :].astype(x.dtype), window_strides=(1,), padding=[(k - 1, 0)],
        dimension_numbers=("NWC", "WIO", "NWC"), feature_group_count=c)

def swiglu_ffn(h, w_gate, w_up, w_down):
    return (jax.nn.silu(h @ w_gate) * (h @ w_up)) @ w_down

def chunked_spatial_gating(u, v, ln_g, ln_b, w_s, b_s):
    bsz, seq, _ = v.shape
    v = layer_norm(v, ln_g, ln_b)
    v = v.reshape(bsz, seq // CHUNK, CHUNK, HEADS_B, HEAD_DIM)
    mask = jnp.tril(jnp.ones((CHUNK, CHUNK), dtype=bool))
    w = jnp.where(mask, w_s, 0).astype(v.dtype)
    s = jnp.einsum("hts,bcshd->bcthd", w, v) + b_s.T.astype(v.dtype)[None, None, :, :, None]
    return u * s.reshape(bsz, seq, D_B)

def second_inputs(seed: int = 0) -> dict:
    key = jax.random.key(seed)
    ks = jax.random.split(key, 24)
    f32 = jnp.float32

    def nrm(k, shape, scale):
        return jax.random.normal(k, shape, f32) * scale

    def gain(k, shape):
        return 1.0 + 0.02 * jax.random.normal(k, shape, f32)

    L = DEPTH
    return {
        "x": jax.random.normal(ks[0], (BATCH, SEQ, D_MODEL), f32),
        "ffn1_norm": gain(ks[1], (L, D_MODEL)),
        "ffn1_w_gate": nrm(ks[2], (L, D_MODEL, D_FF), D_MODEL ** -0.5),
        "ffn1_w_up": nrm(ks[3], (L, D_MODEL, D_FF), D_MODEL ** -0.5),
        "ffn1_w_down": nrm(ks[4], (L, D_FF, D_MODEL), D_FF ** -0.5),
        "mix_norm": gain(ks[5], (L, D_MODEL)),
        "w_in": nrm(ks[6], (L, D_MODEL, D_PROJ), D_MODEL ** -0.5),
        "conv_a_w": nrm(ks[7], (L, CONV_A_WIDTH, D_A), CONV_A_WIDTH ** -0.5),
        "conv_a_b": nrm(ks[8], (L, D_A), 0.02),
        "ln_a_g": gain(ks[9], (L, D_A)),
        "ln_a_b": nrm(ks[10], (L, D_A), 0.02),
        "ln_v_g": gain(ks[11], (L, D_B)),
        "ln_v_b": nrm(ks[12], (L, D_B), 0.02),
        "w_s": nrm(ks[13], (L, HEADS_B, CHUNK, CHUNK), CHUNK ** -0.5),
        "b_s": gain(ks[14], (L, HEADS_B, CHUNK)),
        "conv_c_w": nrm(ks[15], (L, CONV_C_WIDTH, D_C), CONV_C_WIDTH ** -0.5),
        "w_out": nrm(ks[16], (L, D_MIX, D_MODEL), D_MIX ** -0.5),
        "ffn2_norm": gain(ks[17], (L, D_MODEL)),
        "ffn2_w_gate": nrm(ks[18], (L, D_MODEL, D_FF), D_MODEL ** -0.5),
        "ffn2_w_up": nrm(ks[19], (L, D_MODEL, D_FF), D_MODEL ** -0.5),
        "ffn2_w_down": nrm(ks[20], (L, D_FF, D_MODEL), D_FF ** -0.5),
        "final_norm": gain(ks[21], (D_MODEL,)),
    }

def second_block(x, ffn1_norm, ffn1_w_gate, ffn1_w_up, ffn1_w_down, mix_norm, w_in,
              conv_a_w, conv_a_b, ln_a_g, ln_a_b, ln_v_g, ln_v_b, w_s, b_s, conv_c_w,
              w_out, ffn2_norm, ffn2_w_gate, ffn2_w_up, ffn2_w_down, final_norm):
    for l in range(DEPTH):
        h = rms_norm_2(x, ffn1_norm[l])
        x = x + 0.5 * swiglu_ffn(h, ffn1_w_gate[l], ffn1_w_up[l], ffn1_w_down[l])

        h = rms_norm_2(x, mix_norm[l])
        p = h @ w_in[l]
        a_val, a_gate, b_u, b_v, c_b, c_c, c_x = jnp.split(p, SPLITS, axis=-1)

        a = a_val * jax.nn.sigmoid(a_gate)
        a = causal_depthwise_conv_2(a, conv_a_w[l]) + conv_a_b[l]
        a = jax.nn.silu(layer_norm(a, ln_a_g[l], ln_a_b[l]))

        b = chunked_spatial_gating(jax.nn.gelu(b_u), jax.nn.gelu(b_v),
                                   ln_v_g[l], ln_v_b[l], w_s[l], b_s[l])

        c = c_b * causal_depthwise_conv_2(c_c * c_x, conv_c_w[l])

        x = x + jnp.concatenate([a, b, c], axis=-1) @ w_out[l]

        h = rms_norm_2(x, ffn2_norm[l])
        x = x + 0.5 * swiglu_ffn(h, ffn2_w_gate[l], ffn2_w_up[l], ffn2_w_down[l])
    return rms_norm_2(x, final_norm)


_first_inputs = second_inputs


def second_inputs(seed=0):
    import zlib

    import numpy as np

    out = dict(_first_inputs(seed))
    spreads = {}
    factors = {'ffn1_norm': 3.828,
     'conv_a_b': 3.074,
     'ln_a_g': 5.872,
     'ln_a_b': 6.767,
     'ln_v_g': 8.0,
     'ln_v_b': 8.0,
     'b_s': 7.962,
     'ffn2_norm': 6.12,
     'final_norm': 2.752}
    for name, (base, spread) in spreads.items():
        noise = np.random.default_rng([zlib.crc32(name.encode()), seed]).standard_normal(out[name].shape)
        drawn = base * np.exp(spread * noise) if base else spread * noise
        out[name] = __import__('jax').numpy.asarray(drawn.astype(out[name].dtype))
    for name, factor in factors.items():
        out[name] = (out[name] * factor).astype(out[name].dtype)
    return out


_narrow_inputs = second_inputs


def second_inputs(seed=0):

    out = dict(_narrow_inputs(seed))
    wider = {'ln_a_g': 4.61,
     'ln_a_b': 4.0,
     'ln_v_g': 6.16,
     'ln_v_b': 6.71,
     'b_s': 4.76,
     'final_norm': 3.09}
    for name, times in wider.items():
        mean = out[name].mean()
        out[name] = (mean + times * (out[name] - mean)).astype(out[name].dtype)
    return out


def setup_inputs(seed=0):
    out = dict(first_inputs(seed))
    for name, value in second_inputs(seed + 1).items():
        if name != "x":
            out[name + "_2"] = value
    return out


def reference(
    x, ln_mix, ln_ffn, e_w_in, e_lru_conv_w, e_lru_conv_b, e_lru_w_a, e_lru_b_a, e_lru_w_i,
    e_lru_b_i, e_lru_lambda, e_q_norm, e_k_norm, e_sinks, e_w_out, e_ffn_w_gate, e_ffn_w_up,
    e_ffn_w_down, o_w_in, o_conv_w, o_a_log, o_dt_bias, o_out_norm, o_w_out, o_router,
    o_moe_w_gate, o_moe_w_up, o_moe_w_down, ffn1_norm_2, ffn1_w_gate_2, ffn1_w_up_2,
    ffn1_w_down_2, mix_norm_2, w_in_2, conv_a_w_2, conv_a_b_2, ln_a_g_2, ln_a_b_2, ln_v_g_2,
    ln_v_b_2, w_s_2, b_s_2, conv_c_w_2, w_out_2, ffn2_norm_2, ffn2_w_gate_2, ffn2_w_up_2,
    ffn2_w_down_2, final_norm_2,
):
    x = first_block(
        x, ln_mix, ln_ffn, e_w_in, e_lru_conv_w, e_lru_conv_b, e_lru_w_a, e_lru_b_a, e_lru_w_i,
        e_lru_b_i, e_lru_lambda, e_q_norm, e_k_norm, e_sinks, e_w_out, e_ffn_w_gate, e_ffn_w_up,
        e_ffn_w_down, o_w_in, o_conv_w, o_a_log, o_dt_bias, o_out_norm, o_w_out, o_router,
        o_moe_w_gate, o_moe_w_up, o_moe_w_down,
    )
    return second_block(
        x, ffn1_norm_2, ffn1_w_gate_2, ffn1_w_up_2, ffn1_w_down_2, mix_norm_2, w_in_2,
        conv_a_w_2, conv_a_b_2, ln_a_g_2, ln_a_b_2, ln_v_g_2, ln_v_b_2, w_s_2, b_s_2,
        conv_c_w_2, w_out_2, ffn2_norm_2, ffn2_w_gate_2, ffn2_w_up_2, ffn2_w_down_2,
        final_norm_2,
    )


_drawn_inputs = setup_inputs


def setup_inputs(seed=0):
    import zlib

    import numpy as np

    out = dict(_drawn_inputs(seed))
    spreads = {}
    factors = {'e_k_norm': 7.249}
    for name, (base, spread) in spreads.items():
        noise = np.random.default_rng([zlib.crc32(name.encode()), seed]).standard_normal(out[name].shape)
        drawn = base * np.exp(spread * noise) if base else spread * noise
        out[name] = jnp.asarray(drawn.astype(out[name].dtype))
    for name, factor in factors.items():
        out[name] = (out[name] * factor).astype(out[name].dtype)
    return out
```

```python
from contextlib import ExitStack

import numpy as np

import concourse.bass as bass
from concourse import mybir

F32 = mybir.dt.float32
F32R = mybir.dt.float32r
I32 = mybir.dt.int32
ALU = mybir.AluOpType
ACT = mybir.ActivationFunctionType
AX = mybir.AxisListType

P = 128
SEQ, D = 256, 1024
NT = SEQ // P
KT = D // P
HALF = 512
EPS = 1e-6
LN_EPS = 1e-5

LRU = 512
LT = LRU // P
CONV = 4
HQ, HKV, DH = 8, 2, 64
HK = HQ + HKV
LRU_C = 8.0
NEG = -1e30

DFF = 2816
FU = 256
NU = DFF // FU
PIECE = KT * FU

GH = 8
NLEV = 7

NE, FE = 8, 3584
FC = 512
NC = FE // FC

DA, DB, DC = 384, 256, 384
AT = DA // P
TAPS_A, TAPS_C = 31, 3
HB = 4
LAYERS2 = 2


def columns(items):
    at, where = 0, {}
    for name, width in items:
        where[name] = (at, at + width)
        at += width
    return where, at


CONST_COLS, CONST_W = columns([
    ("ident", P), ("upto", P), ("before", P), ("ones", P), ("iota", P), ("level", NLEV * P),
    ("future", P), ("window", 2 * P), ("cos", NT * 32), ("sin", NT * 32), ("eight", NE),
])
SMALL_COLS, SMALL_W = columns([
    ("g0", KT), ("g1", KT), ("g2", KT), ("g3", KT),
    ("lconv_w", LT * CONV), ("lconv_b", LT), ("b_a", LT), ("b_i", LT), ("lam", LT),
    ("qk_gain", HK * DH), ("sinks", NT * HQ), ("w_a", LT * P), ("w_i", LT * P),
    ("oconv_w", 3 * GH * CONV), ("a_log", NT * GH), ("dt_bias", NT * GH), ("out_gain", P),
    ("w_ab", KT * 2 * GH), ("router", KT * NE),
])
SMALL2_COLS, SMALL2_W = columns([
    ("g0", KT), ("g1", KT), ("g2", KT), ("conv_a_w", AT * TAPS_A), ("conv_a_b", AT),
    ("ln_a_g", AT), ("ln_a_b", AT), ("ln_v_g", DB), ("ln_v_b", DB), ("w_s", HB * P), ("b_s", HB),
    ("conv_c_w", AT * TAPS_C),
])

class Signals(dict):

    def __init__(self, nc, ctx):
        super().__init__()
        self.nc, self.ctx = nc, ctx

    def __missing__(self, name):
        self[name] = self.ctx.enter_context(self.nc.semaphore(name))
        return self[name]


def bc(ap, axis, n):
    ap = ap.unsqueeze(axis)
    shape = list(ap.shape)
    shape[axis] = n
    return ap.to_broadcast(shape)


class Place:
    pass


def place(nc, ctx, w):
    m = Place()

    def sb(name, width, dt=F32):
        return ctx.enter_context(nc.sbuf_tensor(name, [P, width], dt))

    def cut(t, at, *dims):
        n = 1
        for d in dims:
            n *= d
        ap = t[:, at:at + n]
        if len(dims) == 2:
            return ap.rearrange("p (a b) -> p a b", b=dims[1])
        if len(dims) == 3:
            return ap.rearrange("p (a b c) -> p a b c", b=dims[1], c=dims[2])
        return ap

    m.w = w
    m.sig = Signals(nc, ctx)
    m.ps = [ctx.enter_context(nc.psum_tensor(f"bank{i}", [P, HALF], F32)) for i in range(8)]
    m.mslot = [sb(f"mslot{i}", KT * HALF) for i in range(4)]
    m.res = cut(sb("res", NT * D), 0, NT, D)
    m.xn = cut(sb("xn", NT * D), 0, NT, D)
    m.xT = cut(sb("xT", KT * SEQ), 0, KT, SEQ)
    consts = sb("consts", CONST_W)
    small = sb("small", SMALL_W)
    small2 = sb("small2", LAYERS2 * SMALL2_W)
    m.consts, m.small, m.small2 = consts, small, small2
    m.c = {n: consts[:, a:b] for n, (a, b) in CONST_COLS.items()}
    m.s = {n: small[:, a:b] for n, (a, b) in SMALL_COLS.items()}
    m.s2 = [{n: small2[:, l * SMALL2_W + a:l * SMALL2_W + b] for n, (a, b) in SMALL2_COLS.items()}
            for l in range(LAYERS2)]
    stats = sb("stats", 32)
    m.ss, m.ms, m.sd, m.rstd = stats[:, 0:2], stats[:, 2:4], stats[:, 4:6], stats[:, 6:8]
    tiny = sb("tiny", 400)
    m.tiny = lambda i, n: tiny[:, i:i + n]
    m.q_int = sb("q_int", 2, I32)
    R = 23600
    with nc.sbuf_tensor("scratch", [P, R], F32) as scratch:
        m.scr = lambda at, *dims: cut(scratch, at, *dims)
    f0 = R - 3 * PIECE
    m.splits = {u: i for i, u in enumerate((1, 4, 6, 7, 9))}
    m.fslot = [m.scr(f0 + i * PIECE, PIECE) for i in range(3)]
    m.whi = [sb(f"weights_hi{i}", PIECE, F32R) for i in range(3)]
    m.wlo = [sb(f"weights_lo{i}", PIECE, F32R) for i in range(3)]
    m.xh, m.xl = cut(sb("x_hi", KT * SEQ, F32R), 0, KT, SEQ), cut(sb("x_lo", KT * SEQ, F32R), 0, KT, SEQ)
    m.hh, m.hl = sb("hidden_hi", HALF, F32R), sb("hidden_lo", HALF, F32R)
    return m



def split_product(pe, out, stationary, moving, start, stop):
    pe.matmul(out, stationary[0], moving[0], start=start, stop=False)
    pe.matmul(out, stationary[0], moving[1], start=False, stop=False)
    return pe.matmul(out, stationary[1], moving[0], start=False, stop=stop)



def mix_blocks(w):
    def cols(t, a, b):
        return t[:, a:b].rearrange("(k p) n -> p k n", p=P), b - a

    e_in, e_out, o_in, o_out = w["e_w_in"][0], w["e_w_out"][0], w["o_w_in"][0], w["o_w_out"][0]
    out = [cols(e_in, 0, 512), cols(e_in, 512, 1024), cols(e_in, 1024, 1536), cols(e_in, 1536, 1792)]
    out += [cols(e_out, 0, 512), cols(e_out, 512, 1024)]
    out += [cols(o_in, 512 * i, 512 * i + 512) for i in range(8)]
    out += [cols(o_out, 0, 512), cols(o_out, 512, 1024)]
    for l in range(LAYERS2):
        w_in, w_out, at = w["w_in_2"][l], w["w_out_2"][l], 0
        for width in (DA, DA, 2 * DB, DC, DC, DC):
            out.append(cols(w_in, at, at + width))
            at += width
        out += [cols(w_out, 0, 512), cols(w_out, 512, 1024)]
    return out


B_EVEN, B_ODD, B_SECOND = 0, 6, 16


def mblock(m, i):
    width = m.blocks[i][1]
    return m.mslot[i % 4][:, 0:KT * width].rearrange("p (k n) -> p k n", n=width)


def load_block(sp, m, i):
    if i >= 4:
        block_used(sp, m, i - 4)
    if i >= B_SECOND and i < B_SECOND + 4:
        sp.wait_ge(m.sig["r_end"], 1)
    sp.dma_start(mblock(m, i), m.blocks[i][0]).then_inc(m.sig[f"m_in{i % 4}"], 16)


def block_used(eng, m, i):
    eng.wait_ge(m.sig[f"m_used{i % 4}"], i // 4 + 1)


def block_in(pe, m, i):
    pe.wait_ge(m.sig[f"m_in{i % 4}"], 16 * (i // 4 + 1))


def ffn_piece(kind, u):
    if isinstance(u, int) and u == 0 and kind != "down":
        return {"gate": 0, "up": 1}[kind]
    if isinstance(u, int) and u == NU - 1 and kind == "down":
        return 3 * NU - 1
    return 3 * u + {"gate": -1, "down": 3, "up": 1}[kind]


KINDS = {"gate": 0, "up": 1, "down": 2}


def ffn_load(sp, m, v, w_gate, w_up, w_down, between):
    s = m.sig
    g = w_gate.rearrange("(k p) f -> p k f", p=P)
    up = w_up.rearrange("(k p) f -> p k f", p=P)
    dn = w_down.rearrange("(k p) n -> p k n", p=P)
    inner = lambda i: m.fslot[i].rearrange("p (k f) -> p k f", k=KT)

    def free(kind, u):
        if isinstance(u, int) and u == 0:
            if v > 0:
                sp.wait_ge(s["f_lo"], 3 * NU * (v - 1) + ffn_piece(kind, NU - 1) + 1)
        elif isinstance(u, int):
            sp.wait_ge(s["f_lo"], 3 * NU * v + ffn_piece(kind, u - 1) + 1)
        elif kind == "down":
            sp.wait_ge(s["f_lo"], 3 * NU * v + 3 * u + 1)
        else:
            sp.wait_ge(s["f_lo"], 3 * NU * v + 3 * u - {"gate": 3, "up": 1}[kind])

    def gate_up(u):
        free("gate", u)
        sp.dma_start(inner(0), g[:, :, bass.ds(u * FU, FU)]).then_inc(s["f_gin"], 16)
        free("up", u)
        sp.dma_start(inner(1), up[:, :, bass.ds(u * FU, FU)]).then_inc(s["f_uin"], 16)

    def down(u):
        free("down", u)
        sp.dma_start(m.fslot[2].rearrange("p (k n) -> p k n", n=D),
                     dn[:, bass.ds(u * (FU // P), FU // P), :]).then_inc(s["f_din"], 16)

    gate_up(0)
    down(0)
    between()
    gate_up(1)
    down(1)
    with sp.Fori(2, NU) as u:
        gate_up(u)
        down(u)



def norm_dve(dve, m, u, gain, split=None):
    s = m.sig
    if u == 0:
        dve.wait_ge(s["x_in"], 16)
        dve.wait_ge(s["small_in"], 16)
    else:
        dve.drain()
    dve.tensor_tensor_reduce(m.xn[:, 0, :], m.res[:, 0, :], m.res[:, 0, :], 1.0, 0.0, ALU.mult, ALU.add,
                             m.ss[:, 0:1])
    dve.drain()
    dve.wait_ge(s["n_ss"], u + 1)
    dve.tensor_scalar(m.ms, m.ss, 1.0 / D, EPS, ALU.mult, ALU.add).then_inc(s["n_ms"], 1)
    dve.wait_ge(s["n_std"], u + 1)
    dve.reciprocal(m.rstd, m.sd).then_inc(s["n_rstd"], 1)
    dve.drain()
    dve.tensor_scalar(m.xn[:, 0, :], m.res[:, 0, :], m.rstd[:, 0:1], None, ALU.mult).then_inc(s["n_xn_d"], 1)
    if gain is None:
        return
    if split is not None:
        split()
        for k in range(KT):
            dve.wait_ge(s["n_xh"], 4 * m.splits[u] + k // 2 + 1)
            last = dve.scalar_tensor_tensor(m.xl[:, k, :], m.ps[k // 2][:, (k % 2) * SEQ:(k % 2 + 1) * SEQ],
                                            gain[:, k:k + 1], m.xh[:, k, :], ALU.mult, ALU.subtract)
        last.then_inc(s["n_xl"], 1)
        return
    for b in (0, 2):
        dve.wait_ge(s["n_tr"], 4 * u + b + 1)
        for k in (2 * b, 2 * b + 1):
            dve.tensor_scalar(m.xT[:, k, :], m.ps[b][:, (k % 2) * SEQ:(k % 2 + 1) * SEQ], gain[:, k:k + 1],
                              None, ALU.mult).then_inc(s["n_xT_d"], 1)


def norm_act(act, m, u, gain, split=None):
    s = m.sig
    if u == 0:
        act.wait_ge(s["x_in"], 16)
        act.wait_ge(s["small_in"], 16)
    else:
        act.wait_ge(s["res_ready"], u)
    act.activation(m.xn[:, 1, :], m.res[:, 1, :], ACT.Square, accum_out=m.ss[:, 1:2]).then_inc(s["n_ss"], 1)
    act.wait_ge(s["n_ms"], u + 1)
    act.activation(m.sd, m.ms, ACT.Sqrt).then_inc(s["n_std"], 1)
    act.wait_ge(s["n_rstd"], u + 1)
    act.activation(m.xn[:, 1, :], m.res[:, 1, :], ACT.Copy, scale=m.rstd[:, 1:2]).then_inc(s["n_xn_a"], 1)
    if gain is None:
        return
    if split is not None:
        split()
        for k in range(KT):
            act.wait_ge(s["n_tr"], 4 * u + k // 2 + 1)
            last = act.activation(m.xh[:, k, :], m.ps[k // 2][:, (k % 2) * SEQ:(k % 2 + 1) * SEQ], ACT.Copy,
                                  scale=gain[:, k:k + 1])
            if k % 2 == 1:
                last.then_inc(s["n_xh"], 1)
        return
    for b in (1, 3):
        act.wait_ge(s["n_tr"], 4 * u + b + 1)
        for k in (2 * b, 2 * b + 1):
            act.activation(m.xT[:, k, :], m.ps[b][:, (k % 2) * SEQ:(k % 2 + 1) * SEQ], ACT.Copy,
                           scale=gain[:, k:k + 1]).then_inc(s["n_xT_a"], 1)


def norm_pe(pe, m, u):
    s = m.sig
    if u == 0:
        pe.wait_ge(s["const_in"], 16)
    pe.wait_ge(s["n_xn_d"], u + 1)
    pe.wait_ge(s["n_xn_a"], u + 1)
    for b in range(4):
        for k in (2 * b, 2 * b + 1):
            for t in range(NT):
                at = (k % 2) * SEQ + t * P
                last = pe.transpose(m.ps[b][:, at:at + P], m.xn[:, t, k * P:(k + 1) * P], m.c["ident"])
        last.then_inc(s["n_tr"], 1)
    if u in m.splits:
        pe.wait_ge(s["n_xl"], m.splits[u] + 1)
    else:
        n = u - sum(i < u for i in m.splits)
        pe.wait_ge(s["n_xT_d"], 4 * n + 4)
        pe.wait_ge(s["n_xT_a"], 4 * n + 4)



def out_pe(pe, m, i, yT):
    s = m.sig
    for half in range(2):
        block_in(pe, m, i + half)
        for t in range(NT):
            for k in range(KT):
                last = pe.matmul(m.ps[4 + 2 * t + half][:, :], yT[:, k, t * P:(t + 1) * P],
                                 mblock(m, i + half)[:, k, :], start=(k == 0), stop=(k == KT - 1))
            if t == NT - 1:
                last.then_inc(s[f"m_used{(i + half) % 4}"], 1)
            else:
                last.then_inc(s["o_done"], 1)


def out_dve(dve, m, i, n, scale=1.0):
    s = m.sig
    for half in range(2):
        for t in range(NT):
            if t == NT - 1:
                block_used(dve, m, i + half)
            else:
                dve.wait_ge(s["o_done"], 2 * n + half + 1)
            r = m.res[:, t, half * HALF:(half + 1) * HALF]
            last = dve.tensor_tensor(r, m.ps[4 + 2 * t + half][:, :], r, ALU.add)
    last.then_inc(s["res_ready"], 1)



def ffn_pe(pe, m, v):
    s, at = m.sig, v * NU

    def parts(kind, n):
        i = KINDS[kind]
        return [t[i][:, :].rearrange("p (k n) -> p k n", n=n) for t in (m.whi, m.wlo)]

    def split_in(kind, u):
        pe.wait_ge(s["f_lo"], 3 * at + ffn_piece(kind, u) + 1)

    def inner(kind, bank, done):
        hi, lo = parts(kind, FU)
        for j in range(FU // P):
            cols = slice(j * P, (j + 1) * P)
            for k in range(KT):
                last = split_product(pe, m.ps[bank][:, j * SEQ:(j + 1) * SEQ], (hi[:, k, cols], lo[:, k, cols]),
                                     (m.xh[:, k, :], m.xl[:, k, :]), start=(k == 0), stop=(k == KT - 1))
        last.then_inc(s[done], 1)

    def gate(u):
        split_in("gate", u)
        if not (v == 0 and isinstance(u, int) and u == 0):
            pe.wait_ge(s["f_silu"], u + at)
        inner("gate", 0, "f_gdone")

    def up(u):
        split_in("up", u)
        if not (v == 0 and isinstance(u, int) and u == 0):
            pe.wait_ge(s["f_h"], u + at)
        inner("up", 1, "f_udone")

    def down(u, first=False, final=False):
        split_in("down", NU - 1 if final else u)
        pe.wait_ge(s["f_h"], u + at + 1)
        hi, lo = parts("down", D)
        hh, hl = (t[:, :].rearrange("p (k t) -> p k t", t=SEQ) for t in (m.hh, m.hl))
        for k in range(FU // P):
            for t in range(NT):
                for half in range(2):
                    cols, tok = slice(half * HALF, (half + 1) * HALF), slice(t * P, (t + 1) * P)
                    last = split_product(pe, m.ps[4 + 2 * t + half][:, :], (hh[:, k, tok], hl[:, k, tok]),
                                         (hi[:, k, cols], lo[:, k, cols]),
                                         start=first and k == 0, stop=final and k == FU // P - 1)
        last.then_inc(s["f_ddone"], 1)

    gate(0)
    up(0)
    gate(1)
    down(0, first=True)
    up(1)
    with pe.Fori(2, NU) as u:
        gate(u)
        down(u - 1)
        up(u)
    down(NU - 1, final=True)


def ffn_parts_free(eng, m, v, kind, u):
    if not (v == 0 and isinstance(u, int) and u == 0):
        eng.wait_ge(m.sig[f"f_{kind[0]}done"], u + v * NU)


def ffn_hi(act, m, v, kind, u):
    i, at = KINDS[kind], v * NU
    act.wait_ge(m.sig[f"f_{kind[0]}in"], (u + at) * 16 + 16)
    ffn_parts_free(act, m, v, kind, u)
    act.activation(m.whi[i][:, :], m.fslot[i], ACT.Copy).then_inc(m.sig["f_hi"], 1)


def ffn_lo(dve, m, v, kind, u):
    i, at = KINDS[kind], v * NU
    dve.wait_ge(m.sig["f_hi"], 3 * at + ffn_piece(kind, u) + 1)
    ffn_parts_free(dve, m, v, kind, u)
    dve.tensor_tensor(m.wlo[i][:, :], m.fslot[i], m.whi[i][:, :], ALU.subtract).then_inc(m.sig["f_lo"], 1)


def ffn_act(act, m, v):
    s, at = m.sig, v * NU
    silu = ffn_silu(m)

    def one(u):
        act.wait_ge(s["f_gdone"], u + at + 1)
        if not (v == 0 and isinstance(u, int) and u == 0):
            act.wait_ge(s["f_h"], u + at)
        act.activation(silu, m.ps[0][:, :], ACT.Silu).then_inc(s["f_silu"], 1)

    one(0)
    ffn_hi(act, m, v, "gate", 1)
    ffn_hi(act, m, v, "down", 0)
    ffn_hi(act, m, v, "up", 1)
    with act.Fori(1, NU - 1) as u:
        one(u)
        ffn_hi(act, m, v, "gate", u + 1)
        ffn_hi(act, m, v, "down", u)
        ffn_hi(act, m, v, "up", u + 1)
    one(NU - 1)
    ffn_hi(act, m, v, "down", NU - 1)


def ffn_silu(m):
    return m.xT.rearrange("p k t -> p (k t)")[:, 0:HALF]


def ffn_dve(dve, m, v, scale):
    s, at = m.sig, v * NU
    silu, h = ffn_silu(m), m.xT.rearrange("p k t -> p (k t)")[:, HALF:2 * HALF]

    def hidden(u):
        dve.wait_ge(s["f_udone"], u + at + 1)
        dve.wait_ge(s["f_silu"], u + at + 1)
        dve.tensor_tensor(h, m.ps[1][:, :], silu, ALU.mult)
        dve.drain()
        if not (v == 0 and isinstance(u, int) and u == 0):
            dve.wait_ge(s["f_ddone"], u + at)
        dve.tensor_copy(m.hh[:, :], h)
        dve.drain()
        dve.tensor_tensor(m.hl[:, :], h, m.hh[:, :], ALU.subtract).then_inc(s["f_h"], 1)

    ffn_lo(dve, m, v, "gate", 1)
    ffn_lo(dve, m, v, "down", 0)
    hidden(0)
    ffn_lo(dve, m, v, "up", 1)
    with dve.Fori(1, NU - 1) as u:
        ffn_lo(dve, m, v, "gate", u + 1)
        ffn_lo(dve, m, v, "down", u)
        hidden(u)
        ffn_lo(dve, m, v, "up", u + 1)
    ffn_lo(dve, m, v, "down", NU - 1)
    hidden(NU - 1)
    dve.wait_ge(s["f_ddone"], at + NU)
    for t in range(NT):
        for half in range(2):
            r = m.res[:, t, half * HALF:(half + 1) * HALF]
            last = dve.scalar_tensor_tensor(r, m.ps[4 + 2 * t + half][:, :], scale, r, ALU.mult, ALU.add)
    last.then_inc(s["res_ready"], 1)


def softplus_head(dve, x, neg, mag):
    dve.tensor_scalar(neg, x, -1.0, None, ALU.mult)
    dve.drain()
    return dve.tensor_tensor(mag, x, neg, ALU.max)


def softplus_tail(dve, x, e, z, z2, p, out):
    dve.tensor_scalar(z2, e, 2.0, None, ALU.add)
    dve.drain()
    dve.reciprocal(p, z2)
    dve.drain()
    dve.tensor_tensor(z, e, p, ALU.mult)
    dve.drain()
    dve.tensor_tensor(z2, z, z, ALU.mult)
    dve.drain()
    dve.tensor_scalar(p, z2, 1.0 / 17, 1.0 / 15, ALU.mult, ALU.add)
    for d in (13, 11, 9, 7, 5, 3, 1):
        dve.drain()
        dve.tensor_tensor(p, p, z2, ALU.mult)
        dve.drain()
        dve.tensor_scalar(p, p, 1.0 / d, None, ALU.add)
    dve.drain()
    dve.tensor_tensor(z, z, p, ALU.mult)
    dve.tensor_scalar(z2, x, 0.0, None, ALU.max)
    dve.drain()
    return dve.scalar_tensor_tensor(out, z, 2.0, z2, ALU.mult, ALU.add)



def steps(names):
    value, seen = {}, []
    for i, name in enumerate(names.split()):
        seen.append(name)
        value[name, seen.count(name)] = i + 1
    return value


E_DVE = steps("lamabs xc ms qk L kTd pev pev nm u2 ylru pn pTd pTd pTd od")
E_ACT = steps("lamexp gl gl sd rs rs rs rs rs rs rs rs qTa qTa a th beta exp pTa pTa pTa oa")


def even_mem(m):
    e = Place()
    e.xc, e.gl, e.rg, e.gi = (m.scr(i * 1024, LT, SEQ) for i in range(4))
    e.aa, e.th, e.hh = (m.scr(i * 1024, LT, SEQ) for i in range(4, 7))
    e.q10 = m.scr(7168, NT, HK * DH)
    e.vs = m.scr(8448, NT, HKV * DH)
    e.sq = m.scr(8704, NT, HK * DH)
    e.t1 = m.scr(8704, NT, HK, 32)
    e.t2 = m.scr(9344, NT, HK, 32)
    e.qr = m.scr(9984, NT, HK * DH)
    e.kd = m.scr(11264, NT, HKV, 2 * DH)
    e.qT = m.scr(11776, HQ // 2, SEQ)
    e.kT = m.scr(12800, HKV, SEQ)
    e.p0 = m.scr(13312, HQ, P)
    e.pT0 = m.scr(14336, HQ, P)
    e.yT = m.scr(15360, KT, SEQ)
    e.p1 = m.xn.rearrange("p t d -> p (t d)").rearrange("p (h k) -> p h k", h=HQ)
    e.pT1 = m.xT.rearrange("p k t -> p (k t)").rearrange("p (n h q) -> p n h q", n=2, h=HQ)
    e.ss, e.sd, e.r = m.tiny(0, 20), m.tiny(20, 20), m.tiny(40, 20)
    e.lneg, e.lmag, e.lexp, e.lz, e.lz2, e.lp, e.c8 = (m.tiny(60 + 4 * i, 4) for i in range(7))
    e.mx, e.nm, e.den, e.es, e.rd = (m.tiny(100 + 16 * i, 16) for i in range(5))
    return e


def even_pe(pe, m):
    s, e, c = m.sig, even_mem(m), m.c
    for i, bank in ((0, 0), (1, 2)):
        block_in(pe, m, i)
        for j in range(LT):
            for k in range(KT):
                last = pe.matmul(m.ps[bank + j // 2][:, (j % 2) * SEQ:(j % 2 + 1) * SEQ],
                                 mblock(m, i)[:, k, j * P:(j + 1) * P], m.xT[:, k, :],
                                 start=(k == 0), stop=(k == KT - 1))
        last.then_inc(s[f"m_used{i}"], 1)
    for i in (2, 3):
        block_in(pe, m, i)
        width = m.blocks[i][1]
        for t in range(NT):
            for k in range(KT):
                last = pe.matmul(m.ps[2 * i + t][:, 0:width], m.xT[:, k, t * P:(t + 1) * P],
                                 mblock(m, i)[:, k, :], start=(k == 0), stop=(k == KT - 1))
        last.then_inc(s[f"m_used{i}"], 1)
    pe.wait_ge(s["e_dve"], E_DVE["xc", 1])
    pe.wait_ge(s["e_act"], E_ACT["gl", 2])
    for bank, name, done in ((0, "w_a", "e_r"), (2, "w_i", "e_i")):
        for j in range(LT):
            last = pe.matmul(m.ps[bank + j // 2][:, (j % 2) * SEQ:(j % 2 + 1) * SEQ],
                             m.s[name][:, j * P:(j + 1) * P], e.xc[:, j, :], start=True, stop=True)
        last.then_inc(s[done], 1)
    pe.wait_ge(s["e_dve"], E_DVE["qk", 1])
    for t in range(NT):
        for j in range(HQ // 2):
            last = pe.transpose(m.ps[4 + t][:, j * P:(j + 1) * P], e.qr[:, t, j * P:(j + 1) * P], c["ident"])
        for j in range(HKV):
            last = pe.transpose(m.ps[6][:, (t * HKV + j) * P:(t * HKV + j + 1) * P], e.kd[:, t, j, :], c["ident"])
    last.then_inc(s["e_qkT"], 1)
    pe.wait_ge(s["e_act"], E_ACT["qTa", 2])
    pe.wait_ge(s["e_dve"], E_DVE["kTd", 1])

    def score(n, h, bank, at):
        rows = slice((h % 2) * DH, (h % 2 + 1) * DH)
        return pe.matmul(m.ps[bank][:, at:at + (n + 1) * P], e.qT[rows, h // 2, n * P:(n + 1) * P],
                         e.kT[rows, h // (HQ // HKV), 0:(n + 1) * P], start=True, stop=True)

    for h in range(HQ):
        last = score(0, h, 4 + h % 2, (h // 2) * P)
    last.then_inc(s["e_sc"], 1)
    for h in range(4):
        last = score(1, h, 6 + h % 2, (h // 2) * 2 * P)
    last.then_inc(s["e_sc"], 1)
    pe.wait_ge(s["e_dve"], E_DVE["pev", 2])
    for h in range(4, HQ):
        last = score(1, h, 4 + h % 2, (h // 2 - 2) * 2 * P)
    last.then_inc(s["e_sc"], 1)
    pe.wait_ge(s["e_dve"], E_DVE["pn", 1])
    for h in range(HQ):
        last = pe.transpose(m.ps[4 + h // 4][:, (h % 4) * P:(h % 4 + 1) * P], e.p0[:, h, :], c["ident"])
        if h % 4 == 3:
            last.then_inc(s["e_pT"], 1)
    for n in range(2):
        for h in range(HQ):
            bank = (6, 7, 0, 1)[2 * n + h // 4]
            last = pe.transpose(m.ps[bank][:, (h % 4) * P:(h % 4 + 1) * P], e.p1[:, h, n * P:(n + 1) * P], c["ident"])
            if h % 4 == 3:
                last.then_inc(s["e_pT"], 1)
    pe.wait_ge(s["e_act"], E_ACT["pTa", 3])
    pe.wait_ge(s["e_dve"], E_DVE["pTd", 3])
    for t in range(NT):
        for h in range(HQ):
            kv = h // (HQ // HKV)
            out = m.ps[2 + t][(h % 2) * DH:(h % 2 + 1) * DH, (h // 2) * P:(h // 2 + 1) * P]
            for n in range(t + 1):
                rhs = e.pT0[:, h, :] if t == 0 else e.pT1[:, n, h, :]
                last = pe.matmul(out, e.vs[:, n, kv * DH:(kv + 1) * DH], rhs, start=(n == 0), stop=(n == t))
        last.then_inc(s["e_o"], 1)
    pe.wait_ge(s["e_act"], E_ACT["oa", 1])
    pe.wait_ge(s["e_dve"], E_DVE["od", 1])
    pe.wait_ge(s["e_dve"], E_DVE["ylru", 1])
    out_pe(pe, m, B_EVEN + 4, e.yT)


def even_act(act, m):
    s, e = m.sig, even_mem(m)
    act.wait_ge(s["e_dve"], E_DVE["lamabs", 1])
    act.activation(e.lexp, e.lmag, ACT.Exp, scale=-1.0).then_inc(s["e_act"], 1)
    block_used(act, m, 1)
    for b in range(2):
        act.activation(e.gl[:, 2 * b:2 * b + 2, :], m.ps[2 + b][:, :].rearrange("p (a t) -> p a t", a=2),
                       ACT.Gelu_apprx_tanh).then_inc(s["e_act"], 1)
    act.wait_ge(s["e_dve"], E_DVE["ms", 1])
    act.activation(e.sd, e.ss, ACT.Sqrt).then_inc(s["e_act"], 1)
    for bank, out, bias, wait in ((0, e.rg, "b_a", "e_r"), (2, e.gi, "b_i", "e_i")):
        act.wait_ge(s[wait], 1)
        for j in range(LT):
            act.activation(out[:, j, :], m.ps[bank + j // 2][:, (j % 2) * SEQ:(j % 2 + 1) * SEQ], ACT.Sigmoid,
                           bias=m.s[bias][:, j:j + 1]).then_inc(s["e_act"], 1)
    act.wait_ge(s["e_qkT"], 1)
    for t in range(NT):
        act.activation(e.qT[:, :, t * P:(t + 1) * P], m.ps[4 + t][:, :].rearrange("p (a t) -> p a t", a=4),
                       ACT.Copy).then_inc(s["e_act"], 1)
    act.wait_ge(s["e_dve"], E_DVE["L", 1])
    act.activation(e.aa, e.rg, ACT.Exp).then_inc(s["e_act"], 1)
    act.activation(e.th, e.rg, ACT.Tanh, scale=-1.0).then_inc(s["e_act"], 1)
    act.wait_ge(s["e_dve"], E_DVE["u2", 1])
    act.activation(e.th, e.hh, ACT.Sqrt).then_inc(s["e_act"], 1)
    act.wait_ge(s["e_dve"], E_DVE["nm", 1])
    act.activation(e.es, e.es, ACT.Exp)
    for t in range(NT):
        for h in range(HQ):
            p = (e.p0, e.p1)[t][:, h, :]
            i = t * HQ + h
            last = act.activation(p, p, ACT.Exp, bias=e.nm[:, i:i + 1], accum_out=e.den[:, i:i + 1])
    last.then_inc(s["e_act"], 1)
    for i, bank in ((1, 4), (3, 6), (5, 0)):
        act.wait_ge(s["e_pT"], i)
        out = e.pT0[:, 0:4, :] if i == 1 else e.pT1[:, i // 4, 0:4, :]
        act.activation(out, m.ps[bank][:, :].rearrange("p (a t) -> p a t", a=4), ACT.Copy).then_inc(s["e_act"], 1)
    act.wait_ge(s["e_o"], 1)
    act.activation(e.yT[:, LT:KT, 0:P], m.ps[2][:, :].rearrange("p (a t) -> p a t", a=4),
                   ACT.Copy).then_inc(s["e_act"], 1)


def even_dve(dve, m):
    s, e, c, sm = m.sig, even_mem(m), m.c, m.s
    dve.tensor_scalar(e.c8, sm["lam"], -1.0, None, ALU.mult)
    dve.drain()
    softplus_head(dve, e.c8, e.lneg, e.lmag).then_inc(s["e_dve"], 1)
    dve.wait_ge(s["e_act"], E_ACT["lamexp", 1])
    softplus_tail(dve, e.c8, e.lexp, e.lz, e.lz2, e.lp, e.lneg)
    dve.drain()
    dve.tensor_scalar(e.c8, e.lneg, -LRU_C, None, ALU.mult)
    block_used(dve, m, 0)
    raw = [m.ps[j // 2][:, (j % 2) * SEQ:(j % 2 + 1) * SEQ] for j in range(LT)]
    w = [sm["lconv_w"][:, j * CONV:(j + 1) * CONV] for j in range(LT)]
    for j in range(LT):
        dve.tensor_scalar(e.xc[:, j, :], raw[j], w[j][:, CONV - 1:CONV], sm["lconv_b"][:, j:j + 1], ALU.mult, ALU.add)
    for lag in range(1, CONV):
        dve.drain()
        for j in range(LT):
            last = dve.scalar_tensor_tensor(e.xc[:, j, lag:SEQ], raw[j][:, 0:SEQ - lag],
                                            w[j][:, CONV - 1 - lag:CONV - lag], e.xc[:, j, lag:SEQ], ALU.mult, ALU.add)
    last.then_inc(s["e_dve"], 1)
    block_used(dve, m, 2)
    block_used(dve, m, 3)
    for t in range(NT):
        dve.tensor_copy(e.q10[:, t, 0:HALF], m.ps[4 + t][:, :])
        dve.tensor_copy(e.q10[:, t, HALF:HK * DH], m.ps[6 + t][:, 0:P])
        dve.tensor_copy(e.vs[:, t, :], m.ps[6 + t][:, P:2 * P])
    dve.drain()
    dve.tensor_tensor(e.sq, e.q10, e.q10, ALU.mult)
    dve.drain()
    dve.tensor_reduce(e.ss, e.sq.rearrange("p t (h d) -> p (t h) d", h=HK), AX.X, ALU.add)
    dve.drain()
    dve.tensor_scalar(e.ss, e.ss, 1.0 / DH, EPS, ALU.mult, ALU.add).then_inc(s["e_dve"], 1)
    dve.wait_ge(s["e_act"], E_ACT["sd", 1])
    dve.reciprocal(e.r, e.sd)
    dve.drain()
    dve.tensor_tensor(e.q10, e.q10, bc(sm["qk_gain"], 1, NT), ALU.mult)
    dve.drain()
    heads = e.q10.rearrange("p t (h d) -> p (t h) d", h=HK)
    dve.tensor_tensor(heads, heads, bc(e.r, 2, DH), ALU.mult)
    dve.drain()
    for t in range(NT):
        x = e.q10[:, t, :].rearrange("p (h a d) -> p h a d", h=HK, a=2)
        o = e.qr[:, t, :].rearrange("p (h a d) -> p h a d", h=HK, a=2)
        cos, sin = (bc(c[n][:, t * 32:(t + 1) * 32], 1, HK) for n in ("cos", "sin"))
        for a, op in ((0, ALU.subtract), (1, ALU.add)):
            dve.tensor_tensor(e.t1[:, t], x[:, :, a, :], cos, ALU.mult)
            dve.tensor_tensor(e.t2[:, t], x[:, :, 1 - a, :], sin, ALU.mult)
            dve.drain()
            dve.tensor_tensor(o[:, :, a, :], e.t1[:, t], e.t2[:, t], op)
            dve.drain()
        k = e.qr[:, t, HALF:HK * DH].rearrange("p (h d) -> p h d", h=HKV)
        last = dve.tensor_copy(e.kd[:, t].rearrange("p h (a d) -> p h a d", a=2), bc(k, 2, 2))
    last.then_inc(s["e_dve"], 1)
    dve.wait_ge(s["e_act"], E_ACT["rs", 2 * LT])
    dve.tensor_tensor(e.rg, e.rg, bc(e.c8, 2, SEQ), ALU.mult).then_inc(s["e_dve"], 1)
    dve.wait_ge(s["e_qkT"], 1)
    dve.tensor_copy(e.kT.rearrange("p h (t k) -> p t h k", t=NT),
                    m.ps[6][:, :].rearrange("p (t h k) -> p t h k", t=NT, h=HKV)).then_inc(s["e_dve"], 1)
    p0 = e.p0.rearrange("p (a b) k -> p b a k", b=2)
    p1 = e.p1.rearrange("p (a b) k -> p b a k", b=2)
    dve.wait_ge(s["e_sc"], 1)
    for b in range(2):
        dve.scalar_tensor_tensor(p0[:, b], m.ps[4 + b][:, :].rearrange("p (a k) -> p a k", a=4), DH ** -0.5,
                                 bc(c["window"][:, P:2 * P], 1, 4), ALU.mult, ALU.add).then_inc(s["e_dve"], 1)
    for half in range(2):
        dve.wait_ge(s["e_sc"], 2 + half)
        for b in range(2):
            bank = (6, 4)[half] + b
            dve.scalar_tensor_tensor(p1[:, b, 2 * half:2 * half + 2], m.ps[bank][:, :].rearrange("p (a k) -> p a k", a=2),
                                     DH ** -0.5, bc(c["window"], 1, 2), ALU.mult, ALU.add)
    dve.drain()
    dve.tensor_reduce(e.mx[:, 0:HQ], e.p0, AX.X, ALU.max)
    dve.tensor_reduce(e.mx[:, HQ:2 * HQ], e.p1, AX.X, ALU.max)
    dve.drain()
    dve.tensor_tensor(e.mx, e.mx, sm["sinks"], ALU.max)
    dve.drain()
    dve.tensor_tensor(e.es, sm["sinks"], e.mx, ALU.subtract)
    dve.tensor_scalar(e.nm, e.mx, -1.0, None, ALU.mult).then_inc(s["e_dve"], 1)
    dve.wait_ge(s["e_act"], E_ACT["a", 1])
    dve.wait_ge(s["e_act"], E_ACT["th", 1])
    dve.tensor_tensor(e.hh, e.aa, e.aa, ALU.mult)
    dve.tensor_tensor(e.gi, e.gi, e.xc, ALU.mult)
    dve.drain()
    dve.scalar_tensor_tensor(e.hh, e.hh, 1.0, e.th, ALU.add, ALU.mult).then_inc(s["e_dve"], 1)
    dve.wait_ge(s["e_act"], E_ACT["beta", 1])
    dve.tensor_tensor(e.gi, e.gi, e.th, ALU.mult)
    dve.drain()
    for j in range(LT):
        dve.tensor_tensor_scan(e.hh[:, j, :], e.aa[:, j, :], e.gi[:, j, :], 0.0, ALU.mult, ALU.add)
    dve.drain()
    dve.tensor_tensor(e.yT[:, 0:LT, :], e.hh, e.gl, ALU.mult).then_inc(s["e_dve"], 1)
    dve.wait_ge(s["e_act"], E_ACT["exp", 1])
    dve.tensor_tensor(e.den, e.den, e.es, ALU.add)
    dve.drain()
    dve.reciprocal(e.rd, e.den)
    dve.drain()
    dve.tensor_tensor(e.p0, e.p0, bc(e.rd[:, 0:HQ], 2, P), ALU.mult)
    dve.tensor_tensor(e.p1, e.p1, bc(e.rd[:, HQ:2 * HQ], 2, 2 * P), ALU.mult)
    dve.drain().then_inc(s["e_dve"], 1)
    for i, bank in ((2, 5), (4, 7), (6, 1)):
        dve.wait_ge(s["e_pT"], i)
        out = e.pT0[:, 4:8, :] if i == 2 else e.pT1[:, i // 2 - 2, 4:8, :]
        dve.tensor_copy(out, m.ps[bank][:, :].rearrange("p (a t) -> p a t", a=4)).then_inc(s["e_dve"], 1)
    dve.wait_ge(s["e_o"], 2)
    dve.tensor_copy(e.yT[:, LT:KT, P:SEQ], m.ps[3][:, :].rearrange("p (a t) -> p a t", a=4)).then_inc(s["e_dve"], 1)
    out_dve(dve, m, B_EVEN + 4, 0)



def odd_mem(m):
    o = Place()
    o.qkvT = m.scr(0, 3 * GH, SEQ)
    o.yT = m.scr(0, KT, SEQ)
    buf = [m.scr(6144 + i * 1024, GH, P) for i in range(17)]
    o.K, o.BK, o.Q, o.QD, o.BGK, o.BV, o.KD, o.knT, o.bkT, o.qnT, o.qdT, o.dec, o.gb, o.TT, o.S = buf[:15]
    o.C = buf[15:17]
    o.LT, o.AT, o.T, o.Y, o.U, o.WT = o.BK, o.Q, o.dec, o.gb, o.bkT, o.qnT
    o.o = m.xn.rearrange("p t (h e) -> p t h e", h=GH)
    o.sg = m.xT.rearrange("p k t -> p (k t)").rearrange("p (t d) -> p t d", t=NT)
    names = "x neg mag ex z z2 p sp ea eb beta g eG ekd ss sd r oss osd orr".split()
    o.v = {n: m.tiny(16 * i, 16) for i, n in enumerate(names)}
    o.ab = m.tiny(320, 32)
    o.G = m.tiny(352, 32)
    return o


def heads4(bank):
    return bank[:, :].rearrange("p (h e) -> p h e", h=4)


def odd_pe(pe, m):
    s, o, c = m.sig, odd_mem(m), m.c
    w_ab = m.s["w_ab"].rearrange("p (k n) -> p k n", k=KT)
    for t in range(NT):
        for k in range(KT):
            last = pe.matmul(m.ps[0][:, t * 16:(t + 1) * 16], m.xT[:, k, t * P:(t + 1) * P], w_ab[:, k, :],
                             start=(k == 0), stop=(k == KT - 1))
    last.then_inc(s["d_ab"], 1)
    for b in range(6):
        i = B_ODD + b
        block_in(pe, m, i)
        if b >= 2:
            pe.wait_ge(s["d_conv"], b - 1)
        for j in range(4):
            for k in range(KT):
                last = pe.matmul(m.ps[2 + 2 * (b % 2) + j // 2][:, (j % 2) * SEQ:(j % 2 + 1) * SEQ],
                                 mblock(m, i)[:, k, j * P:(j + 1) * P], m.xT[:, k, :],
                                 start=(k == 0), stop=(k == KT - 1))
        last.then_inc(s[f"m_used{i % 4}"], 1)
        if b == 2:
            pe.wait_ge(s["d_g"], 1)
            pe.matmul(m.ps[1][:, 0:16], c["upto"], o.v["g"], start=True, stop=True)
            pe.matmul(m.ps[1][:, 16:32], c["ones"], o.v["g"], start=True, stop=True).then_inc(s["d_G"], 1)
    pe.wait_ge(s["d_Gs"], 1)
    for half in range(2):
        i = B_ODD + 6 + half
        block_in(pe, m, i)
        for t in range(NT):
            for k in range(KT):
                last = pe.matmul(m.ps[((6, 7), (0, 1))[half][t]][:, :], m.xT[:, k, t * P:(t + 1) * P],
                                 mblock(m, i)[:, k, :], start=(k == 0), stop=(k == KT - 1))
        last.then_inc(s[f"m_used{i % 4}"], 1)
    for t in range(NT):
        pe.wait_ge(s["d_conv"], 6)
        pe.wait_ge(s["d_gb"], t + 1)
        if t == 1:
            pe.wait_ge(s["d_oev"], 1)
        for h in range(GH):
            last = pe.matmul(m.ps[2 + h // 4][:, (h % 4) * P:(h % 4 + 1) * P], o.gb[:, h, :], c["upto"],
                             start=True, stop=True)
        last.then_inc(s["d_Gb"], 1)
        pe.wait_ge(s["d_silu"], 6)
        if t == 0:
            pe.wait_ge(s["d_sg"], 1)
        else:
            pe.wait_ge(s["d_Sa"], 1)
        for part, bank in ((0, 4), (1, 6), (2, 0)):
            for h in range(GH):
                last = pe.transpose(m.ps[bank + h // 4][:, (h % 4) * P:(h % 4 + 1) * P],
                                    o.qkvT[:, part * GH + h, t * P:(t + 1) * P], c["ident"])
            last.then_inc(s["d_tr"], 1)
        pe.wait_ge(s["d_tok"], t + 1)
        back = [(o.K, 4), (o.BK, 6), (o.Q, 0)]
        if t == 1:
            pe.wait_ge(s["d_pool"], 2)
            back.append((o.QD, 2))
        for src, bank in back:
            for h in range(GH):
                last = pe.transpose(m.ps[bank + h // 4][:, (h % 4) * P:(h % 4 + 1) * P], src[:, h, :], c["ident"])
            last.then_inc(s["d_tr2"], 1)
        pe.wait_ge(s["d_tr2a"], 2 * t + 2)
        pe.wait_ge(s["d_tr2d"], t + 1)
        for rhs, bank in ((o.bkT, 4), (o.qnT, 6)):
            for h in range(GH):
                last = pe.matmul(m.ps[bank + h // 4][:, (h % 4) * P:(h % 4 + 1) * P], o.knT[:, h, :], rhs[:, h, :],
                                 start=True, stop=True)
            last.then_inc(s["d_kk"], 1)
        pe.wait_ge(s["d_T0"], t + 1)
        for h in range(GH):
            last = pe.transpose(m.ps[h // 4][:, (h % 4) * P:(h % 4 + 1) * P], o.TT[:, h, :], c["ident"])
            if h % 4 == 3:
                last.then_inc(s["d_T0p"], 1)
        for k in range(1, NLEV):
            n = 2 * ((NLEV - 1) * t + k - 1)
            pe.wait_ge(s["d_C"], (NLEV - 1) * t + k)
            for g in range(2):
                if k == 1:
                    pe.wait_ge(s["d_T0a"], 2 * t + g + 1)
                else:
                    pe.wait_ge(s["d_Zd"], n - 2 + g + 1)
                for h in range(4 * g, 4 * g + 4):
                    last = pe.matmul(m.ps[g][:, (h % 4) * P:(h % 4 + 1) * P], o.C[k % 2][:, h, :], o.T[:, h, :],
                                     start=True, stop=True)
                last.then_inc(s["d_Y"], 1)
            for g in range(2):
                pe.wait_ge(s["d_Yc"], n + g + 1)
                for h in range(4 * g, 4 * g + 4):
                    cols = slice((h % 4) * P, (h % 4 + 1) * P)
                    if k < NLEV - 1:
                        pe.matmul(m.ps[2 + g][:, cols], o.TT[:, h, :], o.Y[:, h, :], start=True, stop=True)
                    last = pe.matmul(m.ps[4 + g][:, cols], o.Y[:, h, :], o.TT[:, h, :], start=True, stop=True)
                last.then_inc(s["d_Z"], 1)
        pe.wait_ge(s["d_Zd"], 2 * (NLEV - 1) * (t + 1))
        for h in range(GH):
            last = pe.matmul(m.ps[h // 4][:, (h % 4) * P:(h % 4 + 1) * P], o.TT[:, h, :], o.BV[:, h, :],
                             start=True, stop=True)
        last.then_inc(s["d_U"], 1)
        if t == 1:
            for h in range(GH):
                last = pe.matmul(m.ps[6 + h // 4][:, (h % 4) * P:(h % 4 + 1) * P], o.BGK[:, h, :], o.TT[:, h, :],
                                 start=True, stop=True)
            last.then_inc(s["d_W"], 1)
            pe.wait_ge(s["d_Wa"], 1)
            for h in range(GH):
                last = pe.matmul(m.ps[4 + h // 4][:, (h % 4) * P:(h % 4 + 1) * P], o.WT[:, h, :], o.S[:, h, :],
                                 start=True, stop=True)
            last.then_inc(s["d_WS"], 1)
            pe.wait_ge(s["d_VN"], 1)
        else:
            pe.wait_ge(s["d_Ua"], 1)
        for h in range(GH):
            cols = slice((h % 4) * P, (h % 4 + 1) * P)
            if t == 1:
                pe.matmul(m.ps[2 + h // 4][:, cols], o.qdT[:, h, :], o.S[:, h, :], start=True, stop=False)
            last = pe.matmul(m.ps[2 + h // 4][:, cols], o.AT[:, h, :], o.U[:, h, :], start=(t == 0), stop=True)
        last.then_inc(s["d_O"], 1)
        if t == 0:
            for h in range(GH):
                last = pe.matmul(m.ps[4 + h // 4][:, (h % 4) * P:(h % 4 + 1) * P], o.KD[:, h, :], o.U[:, h, :],
                                 start=True, stop=True)
            last.then_inc(s["d_S"], 1)
    for t in range(NT):
        pe.wait_ge(s["d_on"], t + 1)
        for h in range(GH):
            last = pe.transpose(m.ps[4 * (1 - t) + h // 4][:, (h % 4) * P:(h % 4 + 1) * P],
                                o.o[:, t, h, :], c["ident"])
        last.then_inc(s["d_otr"], 1)
    pe.wait_ge(s["d_ota"], 2)
    pe.wait_ge(s["d_otd"], 2)
    out_pe(pe, m, B_ODD + 8, o.yT)


def odd_pool(pool, m):
    s, o, v = m.sig, odd_mem(m), odd_mem(m).v
    for t in range(NT):
        pool.wait_ge(s["d_tok"], t + 1)
        pool.wait_ge(s["d_eG"], 1)
        th = slice(t * GH, (t + 1) * GH)
        if t == 0:
            pool.tensor_tensor(o.KD, o.K, bc(v["ekd"][:, th], 2, P), ALU.mult).then_inc(s["d_pool"], 1)
        else:
            pool.tensor_tensor(o.BGK, o.BK, bc(v["eG"][:, th], 2, P), ALU.mult)
            pool.tensor_tensor(o.QD, o.Q, bc(v["eG"][:, th], 2, P), ALU.mult)
            pool.drain().then_inc(s["d_pool"], 1)
        pool.wait_ge(s["d_LT"], t + 1)
        for k in range(1, NLEV):
            if (NLEV - 1) * t + k > 2:
                pool.wait_ge(s["d_Y"], 2 * ((NLEV - 1) * t + k - 2))
            pool.tensor_tensor(o.C[k % 2], o.LT, bc(m.c["level"][:, k * P:(k + 1) * P], 1, GH),
                               ALU.mult).then_inc(s["d_C"], 1)


def odd_norm_act(act, m, o, t):
    act.wait_ge(m.sig["d_oss"], t + 1)
    th = slice(t * GH, (t + 1) * GH)
    act.activation(o.v["osd"][:, th], o.v["oss"][:, th], ACT.Sqrt).then_inc(m.sig["d_osd"], 1)


def odd_act(act, m):
    s, o, v = m.sig, odd_mem(m), odd_mem(m).v
    act.wait_ge(s["d_gabs"], 1)
    act.activation(v["ex"], v["mag"], ACT.Exp, scale=-1.0)
    act.activation(v["ea"], m.s["a_log"], ACT.Exp)
    act.activation(v["eb"].rearrange("p (t h) -> p t h", t=NT), o.ab.rearrange("p (t n) -> p t n", t=NT)[:, :, GH:16],
                   ACT.Exp, scale=-1.0)
    act.drain().then_inc(s["d_gexp"], 1)
    for b in range(6):
        act.wait_ge(s["d_conv"], b + 1)
        x = o.qkvT[:, 4 * b:4 * b + 4, :]
        act.activation(x, x, ACT.Silu).then_inc(s["d_silu"], 1)
    for half in range(2):
        block_used(act, m, B_ODD + 6 + half)
    for half in range(2):
        for t in range(NT):
            act.activation(o.sg[:, t, half * HALF:(half + 1) * HALF], m.ps[((6, 7), (0, 1))[half][t]][:, :], ACT.Silu)
    act.drain().then_inc(s["d_sg"], 1)
    act.wait_ge(s["d_Gs"], 1)
    act.activation(v["eG"], o.G[:, 0:16], ACT.Exp)
    act.activation(v["ekd"], o.G[:, 16:32], ACT.Exp)
    act.drain().then_inc(s["d_eG"], 1)
    for t in range(NT):
        act.wait_ge(s["d_diff"], t + 1)
        act.activation(o.dec, o.dec, ACT.Exp).then_inc(s["d_dec"], 1)
        act.wait_ge(s["d_tr"], 3 * t + 1)
        for g in range(2):
            act.activation(o.Q[:, 4 * g:4 * g + 4, :], heads4(m.ps[4 + g]), ACT.Copy).then_inc(s["d_Qa"], 1)
        act.wait_ge(s["d_ms"], t + 1)
        act.activation(v["sd"], v["ss"], ACT.Sqrt).then_inc(s["d_sd"], 1)
        for i, (out, bank) in enumerate(((o.knT, 4), (o.qnT, 0))):
            act.wait_ge(s["d_tr2"], 3 * t + 1 + 2 * i)
            for g in range(2):
                last = act.activation(out[:, 4 * g:4 * g + 4, :], heads4(m.ps[bank + g]), ACT.Copy)
            last.then_inc(s["d_tr2a"], 1)
        for g in range(2):
            act.wait_ge(s["d_T0p"], 2 * t + g + 1)
            act.activation(o.T[:, 4 * g:4 * g + 4, :], heads4(m.ps[g]), ACT.Copy).then_inc(s["d_T0a"], 1)
        for k in range(1, NLEV):
            n = 2 * ((NLEV - 1) * t + k - 1)
            for g in range(2):
                act.wait_ge(s["d_Y"], n + g + 1)
                act.activation(o.Y[:, 4 * g:4 * g + 4, :], heads4(m.ps[g]), ACT.Copy).then_inc(s["d_Yc"], 1)
            if t == 1 and k == 3:
                odd_norm_act(act, m, o, 0)
        act.wait_ge(s["d_U"], t + 1)
        for g in range(2):
            last = act.activation(o.U[:, 4 * g:4 * g + 4, :], heads4(m.ps[g]), ACT.Copy)
        last.then_inc(s["d_Ua"], 1)
        if t == 1:
            act.wait_ge(s["d_W"], 1)
            for g in range(2):
                last = act.activation(o.WT[:, 4 * g:4 * g + 4, :], heads4(m.ps[6 + g]), ACT.Copy)
            last.then_inc(s["d_Wa"], 1)
        act.wait_ge(s["d_O"], t + 1)
        for g in range(2):
            last = act.activation(o.o[:, t, 4 * g:4 * g + 4, :], heads4(m.ps[2 + g]), ACT.Copy)
        last.then_inc(s["d_oev"], 1)
        if t == 0:
            act.wait_ge(s["d_S"], 1)
            for g in range(2):
                last = act.activation(o.S[:, 4 * g:4 * g + 4, :], heads4(m.ps[4 + g]), ACT.Copy)
            last.then_inc(s["d_Sa"], 1)
    odd_norm_act(act, m, o, 1)
    for t in range(NT):
        act.wait_ge(s["d_otr"], t + 1)
        act.activation(o.yT[:, 0:4, t * P:(t + 1) * P], heads4(m.ps[4 * (1 - t)]), ACT.Copy).then_inc(s["d_ota"], 1)


def odd_dve(dve, m):
    s, o, c = m.sig, odd_mem(m), m.c
    v = o.v

    def th(name, t):
        return v[name][:, t * GH:(t + 1) * GH]

    dve.wait_ge(s["d_ab"], 1)
    dve.tensor_copy(o.ab, m.ps[0][:, 0:32])
    dve.drain()
    ab = o.ab.rearrange("p (t n) -> p t n", t=NT)
    dve.tensor_tensor(v["x"].rearrange("p (t h) -> p t h", t=NT), ab[:, :, 0:GH],
                      m.s["dt_bias"].rearrange("p (t h) -> p t h", t=NT), ALU.add)
    dve.drain()
    softplus_head(dve, v["x"], v["neg"], v["mag"]).then_inc(s["d_gabs"], 1)
    dve.wait_ge(s["d_gexp"], 1)
    softplus_tail(dve, v["x"], v["ex"], v["z"], v["z2"], v["p"], v["sp"])
    dve.tensor_scalar(v["eb"], v["eb"], 1.0, None, ALU.add)
    dve.drain()
    dve.reciprocal(v["beta"], v["eb"])
    dve.scalar_tensor_tensor(v["g"], v["ea"], -1.0, v["sp"], ALU.mult, ALU.mult).then_inc(s["d_g"], 1)
    for b in range(6):
        block_used(dve, m, B_ODD + b)
        raw = [m.ps[2 + 2 * (b % 2) + j // 2][:, (j % 2) * SEQ:(j % 2 + 1) * SEQ] for j in range(4)]
        w = [m.s["oconv_w"][:, (4 * b + j) * CONV:(4 * b + j + 1) * CONV] for j in range(4)]
        for j in range(4):
            dve.tensor_scalar(o.qkvT[:, 4 * b + j, :], raw[j], w[j][:, CONV - 1:CONV], None, ALU.mult)
        for lag in range(1, CONV):
            dve.drain()
            for j in range(4):
                x = o.qkvT[:, 4 * b + j, lag:SEQ]
                dve.scalar_tensor_tensor(x, raw[j][:, 0:SEQ - lag], w[j][:, CONV - 1 - lag:CONV - lag], x,
                                         ALU.mult, ALU.add)
        dve.drain().then_inc(s["d_conv"], 1)
        if b == 3:
            dve.wait_ge(s["d_G"], 1)
            dve.tensor_copy(o.G, m.ps[1][:, 0:32])
            dve.drain()
            dve.tensor_tensor(o.G[:, 16:32], o.G[:, 16:32], o.G[:, 0:16], ALU.subtract).then_inc(s["d_Gs"], 1)
            dve.tensor_copy(o.gb, bc(th("g", 0), 2, P)).then_inc(s["d_gb"], 1)
    for t in range(NT):
        dve.wait_ge(s["d_Gb"], t + 1)
        for g in range(2):
            dve.tensor_tensor(o.dec[:, 4 * g:4 * g + 4, :], heads4(m.ps[2 + g]),
                              bc(o.G[:, t * GH + 4 * g:t * GH + 4 * g + 4], 2, P), ALU.subtract)
        dve.drain()
        dve.tensor_tensor(o.dec, o.dec, bc(c["future"], 1, GH), ALU.add).then_inc(s["d_diff"], 1)
        dve.wait_ge(s["d_tr"], 3 * t + 2)
        for g in range(2):
            dve.tensor_copy(o.K[:, 4 * g:4 * g + 4, :], heads4(m.ps[6 + g]))
        dve.drain()
        dve.tensor_tensor(o.BK, o.K, o.K, ALU.mult)
        dve.wait_ge(s["d_Qa"], 2 * t + 2)
        dve.tensor_tensor(o.QD, o.Q, o.Q, ALU.mult)
        dve.drain()
        dve.tensor_reduce(v["ss"][:, GH:16], o.BK, AX.X, ALU.add)
        dve.tensor_reduce(v["ss"][:, 0:GH], o.QD, AX.X, ALU.add)
        dve.drain()
        dve.tensor_scalar(v["ss"], v["ss"], EPS, None, ALU.add).then_inc(s["d_ms"], 1)
        dve.wait_ge(s["d_tr"], 3 * t + 3)
        for g in range(2):
            dve.tensor_tensor(o.BV[:, 4 * g:4 * g + 4, :], heads4(m.ps[g]), bc(th("beta", t)[:, 4 * g:4 * g + 4], 2, P),
                              ALU.mult)
        dve.wait_ge(s["d_sd"], t + 1)
        dve.reciprocal(v["r"], v["sd"])
        dve.drain()
        dve.tensor_scalar(v["r"][:, 0:GH], v["r"][:, 0:GH], P ** -0.5, None, ALU.mult)
        dve.tensor_tensor(o.K, o.K, bc(v["r"][:, GH:16], 2, P), ALU.mult)
        dve.drain()
        dve.tensor_tensor(o.Q, o.Q, bc(v["r"][:, 0:GH], 2, P), ALU.mult)
        dve.tensor_tensor(o.BK, o.K, bc(th("beta", t), 2, P), ALU.mult)
        dve.drain().then_inc(s["d_tok"], 1)
        dve.wait_ge(s["d_tr2"], 3 * t + 2)
        for g in range(2):
            last = dve.tensor_copy(o.bkT[:, 4 * g:4 * g + 4, :], heads4(m.ps[6 + g]))
        if t == 1:
            dve.wait_ge(s["d_tr2"], 7)
            for g in range(2):
                last = dve.tensor_copy(o.qdT[:, 4 * g:4 * g + 4, :], heads4(m.ps[2 + g]))
        last.then_inc(s["d_tr2d"], 1)
        dve.wait_ge(s["d_dec"], t + 1)
        for i, (out, bank) in enumerate(((o.LT, 4), (o.AT, 6))):
            dve.wait_ge(s["d_kk"], 2 * t + i + 1)
            if t == 1 and i == 0:
                dve.wait_ge(s["d_pool"], 2)
            for g in range(2):
                last = dve.tensor_tensor(out[:, 4 * g:4 * g + 4, :], heads4(m.ps[bank + g]),
                                         o.dec[:, 4 * g:4 * g + 4, :], ALU.mult)
            if i == 0:
                last.then_inc(s["d_LT"], 1)
        dve.drain()
        dve.tensor_tensor(o.TT, o.LT, bc(c["level"][:, 0:P], 1, GH), ALU.mult)
        dve.drain()
        dve.tensor_tensor(o.TT, bc(c["ident"], 1, GH), o.TT, ALU.subtract).then_inc(s["d_T0"], 1)
        for k in range(1, NLEV):
            n = 2 * ((NLEV - 1) * t + k - 1)
            for g in range(2):
                dve.wait_ge(s["d_Z"], n + g + 1)
                hs = slice(4 * g, 4 * g + 4)
                if k < NLEV - 1:
                    dve.tensor_tensor(o.T[:, hs, :], o.T[:, hs, :], heads4(m.ps[2 + g]), ALU.subtract)
                dve.tensor_tensor(o.TT[:, hs, :], o.TT[:, hs, :], heads4(m.ps[4 + g]), ALU.subtract)
                dve.drain().then_inc(s["d_Zd"], 1)
            if t == 1 and k == 3:
                odd_norm_dve(dve, m, o, 0)
        if t == 0:
            dve.wait_ge(s["d_U"], 1)
            dve.tensor_copy(o.gb, bc(th("g", 1), 2, P)).then_inc(s["d_gb"], 1)
            dve.wait_ge(s["d_Ua"], 1)
        else:
            dve.wait_ge(s["d_WS"], 1)
            dve.wait_ge(s["d_Ua"], 2)
            for g in range(2):
                hs = slice(4 * g, 4 * g + 4)
                last = dve.tensor_tensor(o.U[:, hs, :], o.U[:, hs, :], heads4(m.ps[4 + g]), ALU.subtract)
            last.then_inc(s["d_VN"], 1)
    odd_norm_dve(dve, m, o, 1)
    for t in range(NT):
        dve.wait_ge(s["d_otr"], t + 1)
        dve.tensor_copy(o.yT[:, 4:8, t * P:(t + 1) * P], heads4(m.ps[4 * (1 - t) + 1])).then_inc(s["d_otd"], 1)
    out_dve(dve, m, B_ODD + 8, 1)


def odd_norm_dve(dve, m, o, t):
    s, x = m.sig, o.o[:, t]
    th = slice(t * GH, (t + 1) * GH)
    dve.wait_ge(s["d_oev"], t + 1)
    dve.tensor_tensor(o.K, x, x, ALU.mult)
    dve.drain()
    dve.tensor_reduce(o.v["oss"][:, th], o.K, AX.X, ALU.add)
    dve.drain()
    dve.tensor_scalar(o.v["oss"][:, th], o.v["oss"][:, th], 1.0 / P, EPS, ALU.mult, ALU.add).then_inc(s["d_oss"], 1)
    dve.tensor_tensor(x, x, bc(m.s["out_gain"], 1, GH), ALU.mult)
    dve.drain()
    dve.tensor_tensor(x, x, o.sg[:, t, :].rearrange("p (h e) -> p h e", h=GH), ALU.mult)
    dve.wait_ge(s["d_osd"], t + 1)
    dve.reciprocal(o.v["orr"][:, th], o.v["osd"][:, th])
    dve.drain()
    dve.tensor_tensor(x, x, bc(o.v["orr"][:, th], 2, P), ALU.mult).then_inc(s["d_on"], 1)



STEPS = 2 * NE + 1


def moe_mem(m):
    r = Place()
    r.oh = m.scr(0, NT, P)
    r.ohg = m.scr(256, NT, P)
    r.ohT = m.scr(512, SEQ)
    r.xgT = m.scr(768, KT, P)
    r.silu = m.scr(1792, FC)
    r.h = m.scr(2304, FC)
    r.hT = m.scr(2816, FC // P, P)
    r.y = m.scr(3328, D)
    r.wg = m.mslot[0].rearrange("p (k n) -> p k n", k=KT)
    r.wu = m.mslot[1].rearrange("p (k n) -> p k n", k=KT)
    r.wd = [m.mslot[2 + i].rearrange("p (k n) -> p k n", k=FC // P) for i in range(2)]
    at = [0]

    def tiny(n):
        at[0] += n
        return m.tiny(at[0] - n, n)

    te = lambda ap: ap.rearrange("p (t e) -> p t e", t=NT)
    r.lg, r.eq, r.sel1, r.sel2, r.sel, r.lg2, r.gate, r.rk1 = (te(tiny(NT * NE)) for _ in range(8))
    r.m1, r.m2, r.best, r.ex, r.w1, r.w2 = (tiny(NT) for _ in range(6))
    r.most, r.over = tiny(1), tiny(1)
    r.rank = te(tiny(NT * STEPS))
    r.gates = te(tiny(NT * STEPS))
    return r


def moe_load(sp, m):
    s, r, w = m.sig, moe_mem(m), m.w
    wg = w["o_moe_w_gate"][0].rearrange("e (k p) f -> e p k f", p=P)
    wu = w["o_moe_w_up"][0].rearrange("e (k p) f -> e p k f", p=P)
    wd = w["o_moe_w_down"][0].rearrange("e (k p) n -> e p k n", p=P)

    def gate_up(q, e, c):
        sp.wait_ge(s["r_gdone"], q * NC + c + 1)
        sp.dma_start(r.wg, wg[bass.ds(e, 1), :, :, bass.ds(c * FC, FC)].rearrange("e p k f -> p (e k) f")).then_inc(s["r_gin"], 16)
        sp.wait_ge(s["r_udone"], q * NC + c + 1)
        sp.dma_start(r.wu, wu[bass.ds(e, 1), :, :, bass.ds(c * FC, FC)].rearrange("e p k f -> p (e k) f")).then_inc(s["r_uin"], 16)

    def down(q, e, c, slot, used):
        sp.wait_ge(s["r_ddone"], used)
        sp.dma_start(r.wd[slot], wd[bass.ds(e, 1), :, bass.ds(c * (FC // P), FC // P), :]
                     .rearrange("e p k n -> p (e k) n")).then_inc(s[f"r_din{slot}"], 16)

    def expert(q, e):
        gate_up(q, e, 0)
        gate_up(q, e, 1)
        down(q, e, 0, 0, q * NC + 1)
        gate_up(q, e, 2)
        down(q, e, 1, 1, q * NC + 1)
        with sp.Fori(1, 3) as j:
            gate_up(q, e, 2 * j + 1)
            down(q, e, 2 * j, 0, q * NC + 2 * j)
            gate_up(q, e, 2 * j + 2)
            down(q, e, 2 * j + 1, 1, q * NC + 2 * j + 1)
        down(q, e, NC - 1, 0, q * NC + NC - 1)

    sp.wait_ge(s["r_q"], 1)
    rounds = sp.value_load(m.q_int[0:1, 1:2], min_val=1, max_val=2)
    with sp.Fori(0, rounds) as n:
        with sp.Fori(0, NE) as e:
            expert(n * NE + e, e)


def moe_steps(eng, m):
    eng.wait_ge(m.sig["r_q"], 1)
    return eng.value_load(m.q_int[0:1, 0:1], min_val=NE, max_val=2 * NE)


def moe_pe(pe, m):
    s, r, c = m.sig, moe_mem(m), m.c
    router = m.s["router"].rearrange("p (k e) -> p k e", k=KT)
    for t in range(NT):
        for k in range(KT):
            last = pe.matmul(m.ps[0][:, t * NE:(t + 1) * NE], m.xT[:, k, t * P:(t + 1) * P], router[:, k, :],
                             start=(k == 0), stop=(k == KT - 1))
    last.then_inc(s["r_lg"], 1)
    pe.wait_ge(s["r_sel"], 1)
    pe.matmul(m.ps[1][:, 0:NE], c["before"], r.sel[:, 0, :], start=True, stop=True)
    pe.matmul(m.ps[1][:, NE:2 * NE], c["ones"], r.sel[:, 0, :], start=True, stop=False)
    pe.matmul(m.ps[1][:, NE:2 * NE], c["before"], r.sel[:, 1, :], start=False, stop=True)
    pe.matmul(m.ps[1][:, 16:24], c["ones"], r.sel[:, 0, :], start=True, stop=False)
    pe.matmul(m.ps[1][:, 16:24], c["ones"], r.sel[:, 1, :], start=False, stop=True).then_inc(s["r_rank"], 1)
    for name in ("r_gdone", "r_udone", "r_ddone"):
        pe.drain().then_inc(s[name], 1)
    steps = moe_steps(pe, m)

    def gather(n):
        pe.wait_ge(s["r_oh"], n + 1)
        for k in range(KT):
            for t in range(NT):
                last = pe.matmul(m.ps[k // 4][:, (k % 4) * P:(k % 4 + 1) * P], m.xn[:, t, k * P:(k + 1) * P],
                                 r.oh[:, t, :], start=(t == 0), stop=(t == NT - 1))
        last.then_inc(s["r_gath"], 1)

    def inner(bank, w, arrived, done, i):
        pe.wait_ge(s[arrived], i * 16 + 16)
        for k in range(KT):
            last = pe.matmul(m.ps[bank][:, :], r.xgT[:, k, :], w[:, k, :], start=(k == 0), stop=(k == KT - 1))
        last.then_inc(s[done], 1)

    def turn(i):
        pe.wait_ge(s["r_h"], i + 2)
        for j in range(FC // P):
            last = pe.transpose(m.ps[2][:, j * P:(j + 1) * P], r.h[:, j * P:(j + 1) * P], c["ident"])
        last.then_inc(s["r_hT"], 1)

    def down(i, slot, uses, first=False, final=False):
        pe.wait_ge(s["r_hTd"], i + 1)
        pe.wait_ge(s[f"r_din{slot}"], uses * 16)
        for k in range(FC // P):
            for half in range(2):
                last = pe.matmul(m.ps[3 + half][:, :], r.hT[:, k, :], r.wd[slot][:, k, half * HALF:(half + 1) * HALF],
                                 start=first and k == 0, stop=final and k == FC // P - 1)
        last.then_inc(s["r_ddone"], 1)

    def chunk(i, slot, uses, first=False):
        pe.wait_ge(s["r_silu"], i)
        inner(0, r.wg, "r_gin", "r_gdone", i)
        turn(i - 1)
        inner(1, r.wu, "r_uin", "r_udone", i)
        down(i - 1, slot, uses, first=first)

    gather(0)
    with pe.Fori(0, steps) as q:
        i = q * NC
        pe.wait_ge(s["r_xga"], q + 1)
        pe.wait_ge(s["r_xgd"], q + 1)
        inner(0, r.wg, "r_gin", "r_gdone", i)
        inner(1, r.wu, "r_uin", "r_udone", i)
        pe.wait_ge(s["r_add"], q + 1)
        for t in range(NT):
            last = pe.transpose(m.ps[7][:, t * P:(t + 1) * P], r.ohg[:, t, :], c["ident"])
        last.then_inc(s["r_ohT"], 1)
        chunk(i + 1, 0, q * 4 + 1, first=True)
        chunk(i + 2, 1, q * 3 + 1)
        with pe.Fori(1, 3) as j:
            chunk(i + 2 * j + 1, 0, q * 4 + j + 1)
            chunk(i + 2 * j + 2, 1, q * 3 + j + 1)
        turn(i + NC - 1)
        down(i + NC - 1, 0, q * 4 + 4, final=True)
        gather(q + 1)
        pe.wait_ge(s["r_ohTa"], q + 1)
        pe.wait_ge(s["r_ya"], q + 1)
        pe.wait_ge(s["r_yd"], q + 1)
        for t in range(NT):
            for half in range(2):
                pe.matmul(m.ps[(5, 6, 7, 2)[2 * t + half]][:, :], r.ohT[:, t * P:(t + 1) * P],
                          r.y[:, half * HALF:(half + 1) * HALF], start=True, stop=True).then_inc(s["r_scat"], 1)
    pe.drain().then_inc(s["r_end"], 1)


def moe_act(act, m):
    s, r = m.sig, moe_mem(m)
    act.wait_ge(s["r_e"], 1)
    act.activation(r.ex, r.ex, ACT.Exp).then_inc(s["r_ed"], 1)
    steps = moe_steps(act, m)

    def gathered(n):
        act.wait_ge(s["r_gath"], n + 1)
        for k in range(4):
            last = act.activation(r.xgT[:, k, :], m.ps[0][:, k * P:(k + 1) * P], ACT.Copy, scale=m.s["g3"][:, k:k + 1])
        last.then_inc(s["r_xga"], 1)

    def silu(i):
        act.wait_ge(s["r_gdone"], i + 2)
        act.wait_ge(s["r_h"], i + 1)
        act.activation(r.silu, m.ps[0][:, :], ACT.Silu).then_inc(s["r_silu"], 1)

    gathered(0)
    with act.Fori(0, steps) as q:
        silu(q * NC)
        act.wait_ge(s["r_ohT"], q + 1)
        act.activation(r.ohT, m.ps[7][:, 0:SEQ], ACT.Copy).then_inc(s["r_ohTa"], 1)
        with act.Fori(1, NC) as c:
            silu(q * NC + c)
        act.wait_ge(s["r_ddone"], q * NC + NC + 1)
        act.activation(r.y[:, 0:HALF], m.ps[3][:, :], ACT.Copy).then_inc(s["r_ya"], 1)
        gathered(q + 1)


def moe_dve(dve, m):
    s, r, c = m.sig, moe_mem(m), m.c
    dve.wait_ge(s["r_lg"], 1)
    dve.tensor_copy(r.lg, m.ps[0][:, 0:NT * NE].rearrange("p (t e) -> p t e", t=NT))
    dve.drain()

    def first_best(x, best, sel):
        dve.tensor_reduce(best, x, AX.X, ALU.max)
        dve.drain()
        dve.tensor_tensor(r.eq, x, bc(best, 2, NE), ALU.is_equal)
        dve.drain()
        dve.tensor_tensor(r.eq, r.eq, bc(c["eight"], 1, NT), ALU.mult)
        dve.drain()
        dve.tensor_reduce(r.best, r.eq, AX.X, ALU.max)
        dve.drain()
        dve.tensor_tensor(sel, r.eq, bc(r.best, 2, NE), ALU.is_equal)
        dve.drain()

    first_best(r.lg, r.m1, r.sel1)
    dve.scalar_tensor_tensor(r.lg2, r.sel1, NEG, r.lg, ALU.mult, ALU.add)
    dve.drain()
    first_best(r.lg2, r.m2, r.sel2)
    dve.tensor_tensor(r.sel, r.sel1, r.sel2, ALU.add).then_inc(s["r_sel"], 1)
    dve.tensor_tensor(r.ex, r.m2, r.m1, ALU.subtract).then_inc(s["r_e"], 1)
    dve.wait_ge(s["r_ed"], 1)
    dve.tensor_scalar(r.w2, r.ex, 1.0, None, ALU.add)
    dve.drain()
    dve.reciprocal(r.w1, r.w2)
    dve.drain()
    dve.tensor_tensor(r.w2, r.ex, r.w1, ALU.mult)
    dve.tensor_tensor(r.sel1, r.sel1, bc(r.w1, 2, NE), ALU.mult)
    dve.drain()
    dve.tensor_tensor(r.sel2, r.sel2, bc(r.w2, 2, NE), ALU.mult)
    dve.drain()
    dve.tensor_tensor(r.gate, r.sel1, r.sel2, ALU.add)
    dve.wait_ge(s["r_rank"], 1)
    dve.scalar_tensor_tensor(r.rk1, m.ps[1][:, 0:NT * NE].rearrange("p (t e) -> p t e", t=NT), 1.0, r.sel,
                             ALU.add, ALU.mult)
    dve.tensor_reduce(r.most, m.ps[1][:, 16:24], AX.X, ALU.max)
    dve.drain()
    for n in range(2):
        cols = slice(n * NE, (n + 1) * NE)
        dve.tensor_scalar(r.rank[:, :, cols], r.rk1, -1.0 - n * P, None, ALU.add)
        dve.tensor_copy(r.gates[:, :, cols], r.gate)
    dve.memset(r.rank[:, :, STEPS - 1:STEPS], -1.0)
    dve.memset(r.gates[:, :, STEPS - 1:STEPS], 0.0)
    dve.tensor_scalar(r.over, r.most, float(P), None, ALU.is_gt)
    dve.drain()
    dve.tensor_scalar(m.q_int[:, 0:1], r.over, float(NE), float(NE), ALU.mult, ALU.add)
    dve.tensor_scalar(m.q_int[:, 1:2], r.over, 1.0, None, ALU.add)
    dve.drain().then_inc(s["r_q"], 1)
    dve.drain().then_inc(s["r_h"], 1)
    dve.drain().then_inc(s["r_add"], 1)

    def one_hot(n):
        for t in range(NT):
            rank, gate = r.rank[:, t, bass.ds(n, 1)], r.gates[:, t, bass.ds(n, 1)]
            dve.tensor_scalar(r.oh[:, t, :], c["iota"], rank, None, ALU.is_equal)
            dve.tensor_scalar(r.ohg[:, t, :], c["iota"], rank, gate, ALU.is_equal, ALU.mult)
        dve.drain().then_inc(s["r_oh"], 1)

    def gathered(n):
        dve.wait_ge(s["r_gath"], n + 1)
        for k in range(4, KT):
            last = dve.tensor_scalar(r.xgT[:, k, :], m.ps[1][:, (k - 4) * P:(k - 3) * P], m.s["g3"][:, k:k + 1],
                                     None, ALU.mult)
        last.then_inc(s["r_xgd"], 1)

    def hidden(i):
        dve.wait_ge(s["r_udone"], i + 2)
        dve.wait_ge(s["r_silu"], i + 1)
        dve.tensor_tensor(r.h, r.silu, m.ps[1][:, :], ALU.mult).then_inc(s["r_h"], 1)

    def turned(i):
        dve.wait_ge(s["r_hT"], i + 1)
        dve.tensor_copy(r.hT, m.ps[2][:, :].rearrange("p (j t) -> p j t", j=FC // P)).then_inc(s["r_hTd"], 1)

    steps = moe_steps(dve, m)
    one_hot(0)
    gathered(0)
    with dve.Fori(0, steps) as q:
        hidden(q * NC)
        with dve.Fori(1, NC) as ch:
            turned(q * NC + ch - 1)
            hidden(q * NC + ch)
        dve.wait_ge(s["r_ohT"], q + 1)
        one_hot(q + 1)
        turned(q * NC + NC - 1)
        dve.wait_ge(s["r_ddone"], q * NC + NC + 1)
        dve.tensor_copy(r.y[:, HALF:D], m.ps[4][:, :]).then_inc(s["r_yd"], 1)
        gathered(q + 1)
        for t in range(NT):
            for half in range(2):
                dve.wait_ge(s["r_scat"], q * 4 + 2 * t + half + 1)
                x = m.res[:, t, half * HALF:(half + 1) * HALF]
                last = dve.tensor_tensor(x, x, m.ps[(5, 6, 7, 2)[2 * t + half]][:, :], ALU.add)
        last.then_inc(s["r_add"], 1)
    dve.drain().then_inc(s["res_ready"], 1)



PAD_A, PAD_C = TAPS_A - 1, TAPS_C - 1


def second_mem(m):
    c = Place()
    c.apad = m.scr(0, AT, PAD_A + SEQ)
    c.sg = m.scr(896, AT, SEQ)
    c.acc = m.scr(1664, AT, SEQ)
    c.g = m.scr(2432, NT, 2 * DB)
    c.ccs, c.cxs, c.cbs = (m.scr(3456 + i * 768, AT, SEQ) for i in range(3))
    c.zpad = m.scr(5760, AT, PAD_C + SEQ)
    c.zt, c.zacc = m.scr(6544, AT, SEQ), m.scr(7312, AT, SEQ)
    c.xh = m.scr(8080, NT, DA)
    c.v = m.scr(8848, NT, DB)
    c.y = m.scr(9360, NT, DB)
    c.ws = m.scr(9872, HB, P)
    c.mixT = m.scr(10384, KT, SEQ)
    c.st = [m.tiny(6 * i, 6) for i in range(4)]
    c.mv = [m.tiny(24 + 2 * i, 2) for i in range(4)]
    c.var, c.sd, c.r = m.tiny(32, 4), m.tiny(36, 4), m.tiny(40, 4)
    return c


def two_banks(m, bank, x, i):
    if i == 0:
        return m.ps[bank][:, :].rearrange("p (a t) -> p a t", a=2), x[:, 0:2, :]
    return m.ps[bank + 1][:, 0:SEQ], x[:, 2, :]


def second_pe(pe, m, l):
    s, c, base = m.sig, second_mem(m), B_SECOND + 8 * l

    def project(j, bank):
        block_in(pe, m, base + j)
        for a in range(AT):
            for k in range(KT):
                last = pe.matmul(m.ps[bank + a // 2][:, (a % 2) * SEQ:(a % 2 + 1) * SEQ],
                                 mblock(m, base + j)[:, k, a * P:(a + 1) * P], m.xT[:, k, :],
                                 start=(k == 0), stop=(k == KT - 1))
        last.then_inc(s[f"m_used{j % 4}"], 1)

    project(0, 0)
    project(1, 2)
    block_in(pe, m, base + 2)
    for t in range(NT):
        for k in range(KT):
            last = pe.matmul(m.ps[4 + t][:, :], m.xT[:, k, t * P:(t + 1) * P], mblock(m, base + 2)[:, k, :],
                             start=(k == 0), stop=(k == KT - 1))
    last.then_inc(s["m_used2"], 1)
    project(3, 6)
    pe.wait_ge(s["c_apad"], l + 1)
    project(4, 0)
    project(5, 2)
    pe.wait_ge(s["c_vl"], l + 1)
    for t in range(NT):
        for h in range(HB):
            at = t * DB + h * 64
            last = pe.matmul(m.ps[4][:, at:at + 64], c.ws[:, h, :], c.v[:, t, h * 64:(h + 1) * 64],
                             start=True, stop=True)
    last.then_inc(s["c_s"], 1)
    pe.wait_ge(s["c_yb"], l + 1)
    for j in range(DB // P):
        for t in range(NT):
            at = j * SEQ + t * P
            last = pe.transpose(m.ps[5][:, at:at + P], c.y[:, t, j * P:(j + 1) * P], m.c["ident"])
    last.then_inc(s["c_ytr"], 1)
    pe.wait_ge(s["c_conv"], l + 1)
    pe.wait_ge(s["c_cev"], 2 * l + 2)
    for t in range(NT):
        for a in range(AT):
            last = pe.transpose(m.ps[t][:, a * P:(a + 1) * P], c.acc[:, a, t * P:(t + 1) * P], m.c["ident"])
        last.then_inc(s["c_tr"], 1)
    for t in range(NT):
        pe.wait_ge(s["c_xh"], 2 * l + t + 1)
        for a in range(AT):
            last = pe.transpose(m.ps[2 + t][:, a * P:(a + 1) * P], c.xh[:, t, a * P:(a + 1) * P], m.c["ident"])
        last.then_inc(s["c_tr2"], 1)
    pe.wait_ge(s["c_ya"], l + 1)
    pe.wait_ge(s["c_ybT"], l + 1)
    pe.wait_ge(s["c_yc"], l + 1)
    out_pe(pe, m, base + 6, c.mixT)


def second_act(act, m, l):
    s, c, base, p = m.sig, second_mem(m), B_SECOND + 8 * l, m.s2[l]
    block_used(act, m, base + 1)
    for i in range(2):
        src, dst = two_banks(m, 2, c.sg, i)
        last = act.activation(dst, src, ACT.Sigmoid)
    last.then_inc(s["c_sg"], 1)
    block_used(act, m, base + 2)
    for t in range(NT):
        last = act.activation(c.g[:, t, :], m.ps[4 + t][:, :], ACT.Gelu_apprx_tanh)
    last.then_inc(s["c_gb"], 1)
    for j, bank, out in ((3, 6, c.cbs), (4, 0, c.ccs), (5, 2, c.cxs)):
        block_used(act, m, base + j)
        for i in range(2):
            src, dst = two_banks(m, bank, out, i)
            last = act.activation(dst, src, ACT.Copy)
        if j > 3:
            last.then_inc(s["c_cev"], 1)
    act.wait_ge(s["c_ms"], 2 * l + 1)
    act.activation(c.sd[:, 0:2], c.var[:, 0:2], ACT.Sqrt).then_inc(s["c_sd"], 1)
    act.wait_ge(s["c_ytr"], l + 1)
    act.activation(c.mixT[:, AT:AT + 2, :], m.ps[5][:, :].rearrange("p (j t) -> p j t", j=2),
                   ACT.Copy).then_inc(s["c_ybT"], 1)
    act.wait_ge(s["c_ms"], 2 * l + 2)
    act.activation(c.sd[:, 2:4], c.var[:, 2:4], ACT.Sqrt).then_inc(s["c_sd"], 1)
    for t in range(NT):
        act.wait_ge(s["c_tr2"], 2 * l + t + 1)
        for a in range(AT):
            last = act.activation(c.mixT[:, a, t * P:(t + 1) * P], m.ps[2 + t][:, a * P:(a + 1) * P], ACT.Silu,
                                  scale=p["ln_a_g"][:, a:a + 1], bias=p["ln_a_b"][:, a:a + 1])
    last.then_inc(s["c_ya"], 1)


def second_dve(dve, m, l):
    s, c, base, p = m.sig, second_mem(m), B_SECOND + 8 * l, m.s2[l]
    dve.memset(c.apad[:, :, 0:PAD_A], 0.0)
    dve.tensor_tensor(c.ws, p["w_s"].rearrange("p (h t) -> p h t", h=HB), bc(m.c["upto"], 1, HB), ALU.mult)
    block_used(dve, m, base)
    dve.wait_ge(s["c_sg"], l + 1)
    for i in range(2):
        src, sg = two_banks(m, 0, c.sg, i)
        dst = c.apad[:, 0:2, PAD_A:] if i == 0 else c.apad[:, 2, PAD_A:]
        dve.tensor_tensor(dst, src, sg, ALU.mult)
    dve.drain().then_inc(s["c_apad"], 1)
    w = p["conv_a_w"].rearrange("p (a i) -> p a i", a=AT)
    for i in range(TAPS_A):
        for a in range(AT):
            x = c.apad[:, a, i:i + SEQ]
            if i == 0:
                dve.tensor_scalar(c.acc[:, a, :], x, w[:, a, 0:1], p["conv_a_b"][:, a:a + 1], ALU.mult, ALU.add)
            else:
                dve.scalar_tensor_tensor(c.acc[:, a, :], x, w[:, a, i:i + 1], c.acc[:, a, :], ALU.mult, ALU.add)
        dve.drain()
        if i == 14:
            second_gate_norm(dve, m, c, l, p)
        if i == 18:
            second_gate_scale(dve, m, c, l, p)
        if i == 26:
            dve.wait_ge(s["c_s"], l + 1)
            for t in range(NT):
                y = c.y[:, t, :].rearrange("p (h d) -> p h d", h=HB)
                dve.tensor_tensor(y, m.ps[4][:, t * DB:(t + 1) * DB].rearrange("p (h d) -> p h d", h=HB),
                                  bc(p["b_s"], 2, 64), ALU.add)
            dve.drain()
            dve.tensor_tensor(c.y, c.y, c.g[:, :, 0:DB], ALU.mult).then_inc(s["c_yb"], 1)
    dve.drain().then_inc(s["c_conv"], 1)
    for t in range(NT):
        dve.wait_ge(s["c_tr"], 2 * l + t + 1)
        dve.bn_stats(c.st[2 + t], m.ps[t][:, 0:DA])
        dve.drain()
        dve.bn_aggr(c.mv[2 + t], c.st[2 + t])
        dve.drain()
        dve.tensor_scalar(c.var[:, 2 + t:3 + t], c.mv[2 + t][:, 1:2], LN_EPS, None, ALU.add)
    dve.drain().then_inc(s["c_ms"], 1)
    dve.wait_ge(s["c_sd"], 2 * l + 2)
    dve.reciprocal(c.r[:, 2:4], c.sd[:, 2:4])
    dve.drain()
    for t in range(NT):
        dve.tensor_scalar(c.xh[:, t, :], m.ps[t][:, 0:DA], c.mv[2 + t][:, 0:1], c.r[:, 2 + t:3 + t],
                          ALU.subtract, ALU.mult).then_inc(s["c_xh"], 1)
    out_dve(dve, m, base + 6, 2 + l)


def second_gate_norm(dve, m, c, l, p):
    dve.wait_ge(m.sig["c_gb"], l + 1)
    for t in range(NT):
        dve.bn_stats(c.st[t], c.g[:, t, DB:2 * DB])
    dve.drain()
    for t in range(NT):
        dve.bn_aggr(c.mv[t], c.st[t])
    dve.drain()
    for t in range(NT):
        dve.tensor_scalar(c.var[:, t:t + 1], c.mv[t][:, 1:2], LN_EPS, None, ALU.add)
    dve.drain().then_inc(m.sig["c_ms"], 1)


def second_gate_scale(dve, m, c, l, p):
    dve.wait_ge(m.sig["c_sd"], 2 * l + 1)
    dve.reciprocal(c.r[:, 0:2], c.sd[:, 0:2])
    dve.drain()
    for t in range(NT):
        dve.tensor_scalar(c.v[:, t, :], c.g[:, t, DB:2 * DB], c.mv[t][:, 0:1], c.r[:, t:t + 1],
                          ALU.subtract, ALU.mult)
    dve.drain()
    dve.tensor_tensor(c.v, c.v, bc(p["ln_v_g"], 1, NT), ALU.mult)
    dve.drain()
    dve.tensor_tensor(c.v, c.v, bc(p["ln_v_b"], 1, NT), ALU.add).then_inc(m.sig["c_vl"], 1)


def second_pool(pool, m, l):
    s, c, p = m.sig, second_mem(m), m.s2[l]
    pool.wait_ge(s["c_cev"], 2 * l + 2)
    pool.memset(c.zpad[:, :, 0:PAD_C], 0.0)
    pool.tensor_tensor(c.zpad[:, :, PAD_C:], c.ccs, c.cxs, ALU.mult)
    pool.drain()
    w = p["conv_c_w"].rearrange("p (a i) -> p a i", a=AT)
    for i in range(TAPS_C):
        out = c.zacc if i == 0 else c.zt
        pool.tensor_tensor(out, c.zpad[:, :, i:i + SEQ], bc(w[:, :, i], 2, SEQ), ALU.mult)
        pool.drain()
        if i:
            pool.tensor_tensor(c.zacc, c.zacc, c.zt, ALU.add)
            pool.drain()
    pool.tensor_tensor(c.mixT[:, AT + 2:KT, :], c.zacc, c.cbs, ALU.mult).then_inc(s["c_yc"], 1)



NAMES = [
    "x", "e_w_in", "e_w_out", "e_ffn_w_gate", "e_ffn_w_up", "e_ffn_w_down", "o_w_in", "o_w_out",
    "o_moe_w_gate", "o_moe_w_up", "o_moe_w_down", "ffn1_w_gate_2", "ffn1_w_up_2", "ffn1_w_down_2",
    "w_in_2", "w_out_2", "ffn2_w_gate_2", "ffn2_w_up_2", "ffn2_w_down_2",
]
STAGES = 99


def start_hi(act, m, v):
    ffn_hi(act, m, v, "gate", 0)
    ffn_hi(act, m, v, "up", 0)


def start_lo(dve, m, v):
    ffn_lo(dve, m, v, "gate", 0)
    ffn_lo(dve, m, v, "up", 0)


def build(nc, w, out):
    with ExitStack() as ctx:
        m = place(nc, ctx, w)
        m.blocks = mix_blocks(w)
        s = m.sig
        gain2 = [[m.s2[l][f"g{i}"] for i in range(3)] for l in range(LAYERS2)]
        block = ctx.enter_context(nc.Block())

        @block.sync
        def _(sp):
            sp.dma_start(m.res, w["x"][0].rearrange("(t p) d -> p t d", p=P)).then_inc(s["x_in"], 16)
            sp.dma_start(m.small[:, :], w["small"]).then_inc(s["small_in"], 16)
            sp.dma_start(m.consts[:, :], w["consts"]).then_inc(s["const_in"], 16)
            for i in range(B_EVEN, B_EVEN + 4):
                load_block(sp, m, i)
            sp.dma_start(m.small2[:, :], w["small2"]).then_inc(s["small2_in"], 16)
            for i in range(B_EVEN + 4, B_ODD):
                load_block(sp, m, i)
            if STAGES >= 2:
                def ahead():
                    for i in range(B_ODD, B_ODD + 4):
                        load_block(sp, m, i)
                ffn_load(sp, m, 0, w["e_ffn_w_gate"][0], w["e_ffn_w_up"][0], w["e_ffn_w_down"][0], ahead)
            if STAGES >= 3:
                for i in range(B_ODD + 4, B_SECOND):
                    load_block(sp, m, i)
            if STAGES >= 4:
                moe_load(sp, m)
            if STAGES >= 5:
                for l in range(LAYERS2):
                    first = B_SECOND + 8 * l

                    def ahead(first=first):
                        for i in range(first, first + 4):
                            load_block(sp, m, i)
                    ffn_load(sp, m, 1 + 2 * l, w["ffn1_w_gate_2"][l], w["ffn1_w_up_2"][l], w["ffn1_w_down_2"][l], ahead)
                    for i in range(first + 4, first + 8):
                        load_block(sp, m, i)
                    ffn_load(sp, m, 2 + 2 * l, w["ffn2_w_gate_2"][l], w["ffn2_w_up_2"][l], w["ffn2_w_down_2"][l],
                             lambda: None)
                sp.wait_ge(s["n_xn_d"], 11)
                sp.dma_start(final_gain(m), w["final"]).then_inc(s["final_in"], 16)
                sp.wait_ge(s["out_ready"], 1)
                src = m.xn
            else:
                sp.wait_ge(s["res_ready"], STAGES)
                src = m.res
            sp.dma_start(out[0].rearrange("(t p) d -> p t d", p=P), src).then_inc(s["out_st"], 16)
            sp.wait_ge(s["out_st"], 16)

        @block.tensor
        def _(pe):
            norm_pe(pe, m, 0)
            even_pe(pe, m)
            if STAGES >= 2:
                norm_pe(pe, m, 1)
                ffn_pe(pe, m, 0)
            if STAGES >= 3:
                norm_pe(pe, m, 2)
                odd_pe(pe, m)
            if STAGES >= 4:
                norm_pe(pe, m, 3)
                moe_pe(pe, m)
            if STAGES >= 5:
                for l in range(LAYERS2):
                    norm_pe(pe, m, 4 + 3 * l)
                    ffn_pe(pe, m, 1 + 2 * l)
                    norm_pe(pe, m, 5 + 3 * l)
                    second_pe(pe, m, l)
                    norm_pe(pe, m, 6 + 3 * l)
                    ffn_pe(pe, m, 2 + 2 * l)

        @block.scalar
        def _(act):
            norm_act(act, m, 0, m.s["g0"])
            even_act(act, m)
            if STAGES >= 2:
                norm_act(act, m, 1, m.s["g1"], lambda: start_hi(act, m, 0))
                ffn_act(act, m, 0)
            if STAGES >= 3:
                norm_act(act, m, 2, m.s["g2"])
                odd_act(act, m)
            if STAGES >= 4:
                norm_act(act, m, 3, m.s["g3"])
                moe_act(act, m)
            if STAGES >= 5:
                for l in range(LAYERS2):
                    norm_act(act, m, 4 + 3 * l, gain2[l][0], lambda: start_hi(act, m, 1 + 2 * l))
                    ffn_act(act, m, 1 + 2 * l)
                    norm_act(act, m, 5 + 3 * l, gain2[l][1])
                    second_act(act, m, l)
                    norm_act(act, m, 6 + 3 * l, gain2[l][2], lambda: start_hi(act, m, 2 + 2 * l))
                    ffn_act(act, m, 2 + 2 * l)
                norm_act(act, m, 10, None)

        @block.vector
        def _(dve):
            norm_dve(dve, m, 0, m.s["g0"])
            even_dve(dve, m)
            if STAGES >= 2:
                norm_dve(dve, m, 1, m.s["g1"], lambda: start_lo(dve, m, 0))
                ffn_dve(dve, m, 0, 1.0)
            if STAGES >= 3:
                norm_dve(dve, m, 2, m.s["g2"])
                odd_dve(dve, m)
            if STAGES >= 4:
                norm_dve(dve, m, 3, m.s["g3"])
                moe_dve(dve, m)
            if STAGES >= 5:
                dve.wait_ge(s["small2_in"], 16)
                for l in range(LAYERS2):
                    norm_dve(dve, m, 4 + 3 * l, gain2[l][0], lambda: start_lo(dve, m, 1 + 2 * l))
                    ffn_dve(dve, m, 1 + 2 * l, 0.5)
                    norm_dve(dve, m, 5 + 3 * l, gain2[l][1])
                    second_dve(dve, m, l)
                    norm_dve(dve, m, 6 + 3 * l, gain2[l][2], lambda: start_lo(dve, m, 2 + 2 * l))
                    ffn_dve(dve, m, 2 + 2 * l, 0.5)
                norm_dve(dve, m, 10, None)
                dve.wait_ge(s["final_in"], 16)
                dve.wait_ge(s["n_xn_a"], 11)
                for t in range(NT):
                    last = dve.tensor_tensor(m.xn[:, t, :], m.xn[:, t, :], final_gain(m), ALU.mult)
                dve.drain().then_inc(s["out_ready"], 1)

        @block.gpsimd
        def _(pool):
            if STAGES >= 3:
                odd_pool(pool, m)
            if STAGES >= 5:
                for l in range(LAYERS2):
                    second_pool(pool, m, l)


def final_gain(m):
    return m.xT.rearrange("p k t -> p (k t)")[:, 0:D]



def constants():
    i = np.arange(P)
    f = np.float32
    half = DH // 2
    inv = (f(10000.0) ** (-np.arange(half, dtype=f) / f(half))).astype(f)
    ang = np.arange(SEQ, dtype=f)[:, None] * inv[None, :]
    turn = lambda a: a.astype(f).reshape(NT, P, half).transpose(1, 0, 2).reshape(P, NT * half)
    level = []
    for k in range(NLEV):
        level.append((((i[None, :] >> k) & 1) == 1) & ((i[:, None] >> k) == (i[None, :] >> k) - 1))
    q, k = i[:, None] + P, np.arange(2 * P)[None, :]
    parts = {
        "ident": np.eye(P, dtype=f),
        "upto": (i[:, None] <= i[None, :]).astype(f),
        "before": (i[:, None] < i[None, :]).astype(f),
        "ones": np.ones((P, P), f),
        "iota": np.broadcast_to(i.astype(f), (P, P)),
        "level": np.concatenate(level, 1).astype(f),
        "future": np.where(i[:, None] <= i[None, :], f(0), f(NEG)),
        "window": np.where((q - k >= 0) & (q - k < P), f(0), f(NEG)),
        "cos": turn(np.cos(ang)), "sin": turn(np.sin(ang)),
        "eight": np.broadcast_to(np.arange(NE, 0, -1).astype(f), (P, NE)),
    }
    return np.concatenate([parts[n] for n in CONST_COLS], 1).astype(f)


def by_partition(a):
    a = a.reshape(-1, a.shape[-1] // P, P)
    return a.transpose(2, 1, 0).reshape(P, -1)


def rows(a, times=1):
    a = np.tile(a.reshape(1, -1), (1, times))
    return np.broadcast_to(a, (P, a.shape[1]))


def block_diagonal(a):
    out = np.zeros((P, LT, P), a.dtype)
    for h in range(a.shape[0]):
        r = slice((h % 2) * 64, (h % 2 + 1) * 64)
        out[r, h // 2, r] = a[h]
    return out.reshape(P, LT * P)


def kernel(**inputs):
    import concourse.bacc as bacc
    from concourse.bass_utils import run_bass_kernel_spmd

    a = {n: np.ascontiguousarray(v) for n, v in inputs.items()}
    parts = {
        "g0": by_partition(a["ln_mix"][0]), "g1": by_partition(a["ln_ffn"][0]),
        "g2": by_partition(a["ln_mix"][1]), "g3": by_partition(a["ln_ffn"][1]),
        "lconv_w": by_partition(a["e_lru_conv_w"][0]), "lconv_b": by_partition(a["e_lru_conv_b"][0]),
        "b_a": by_partition(a["e_lru_b_a"][0]), "b_i": by_partition(a["e_lru_b_i"][0]),
        "lam": by_partition(a["e_lru_lambda"][0]),
        "qk_gain": np.concatenate([rows(a["e_q_norm"][0], HQ), rows(a["e_k_norm"][0], HKV)], 1),
        "sinks": rows(a["e_sinks"][0], NT),
        "w_a": block_diagonal(a["e_lru_w_a"][0]), "w_i": block_diagonal(a["e_lru_w_i"][0]),
        "oconv_w": by_partition(a["o_conv_w"][0]),
        "a_log": rows(a["o_a_log"][0], NT), "dt_bias": rows(a["o_dt_bias"][0], NT),
        "out_gain": rows(a["o_out_norm"][0]),
        "w_ab": a["o_w_in"][0][:, 4096:].reshape(KT, P, 2 * GH).transpose(1, 0, 2).reshape(P, -1),
        "router": a["o_router"][0].reshape(KT, P, NE).transpose(1, 0, 2).reshape(P, -1),
    }
    small = np.concatenate([parts[n] for n in SMALL_COLS], 1)
    small2 = []
    for l in range(LAYERS2):
        parts = {
            "g0": by_partition(a["ffn1_norm_2"][l]), "g1": by_partition(a["mix_norm_2"][l]),
            "g2": by_partition(a["ffn2_norm_2"][l]),
            "conv_a_w": by_partition(a["conv_a_w_2"][l]), "conv_a_b": by_partition(a["conv_a_b_2"][l]),
            "ln_a_g": by_partition(a["ln_a_g_2"][l]), "ln_a_b": by_partition(a["ln_a_b_2"][l]),
            "ln_v_g": rows(a["ln_v_g_2"][l]), "ln_v_b": rows(a["ln_v_b_2"][l]),
            "w_s": a["w_s_2"][l].transpose(2, 0, 1).reshape(P, HB * P), "b_s": a["b_s_2"][l].T,
            "conv_c_w": by_partition(a["conv_c_w_2"][l]),
        }
        small2.append(np.concatenate([parts[n] for n in SMALL2_COLS], 1))

    arrays = {n: a[n] for n in NAMES}
    arrays["small"] = np.ascontiguousarray(small)
    arrays["small2"] = np.ascontiguousarray(np.concatenate(small2, 1))
    arrays["final"] = np.ascontiguousarray(rows(a["final_norm_2"]))
    arrays["consts"] = np.ascontiguousarray(constants())

    nc = bacc.Bacc("TRN2", target_bir_lowering=False, num_devices=1)
    w = {n: nc.dram_tensor(f"in_{n}", v.shape, F32, kind="ExternalInput").ap() for n, v in arrays.items()}
    out = nc.dram_tensor("out_x", (1, SEQ, D), F32, kind="ExternalOutput").ap()
    build(nc, w, out)
    r = run_bass_kernel_spmd(nc, [{f"in_{n}": v for n, v in arrays.items()}], core_ids=[0])
    return r.results[0]["out_x"]
```

```python
from contextlib import ExitStack

import numpy as np

import concourse.bass as bass
from concourse import mybir

F32 = mybir.dt.float32
F32R = mybir.dt.float32r
I32 = mybir.dt.int32
ALU = mybir.AluOpType
ACT = mybir.ActivationFunctionType
AX = mybir.AxisListType

P = 128
SEQ, D = 256, 1024
NT = SEQ // P
KT = D // P
HALF = 512
EPS = 1e-6
LN_EPS = 1e-5

LRU = 512
LT = LRU // P
CONV = 4
HQ, HKV, DH = 8, 2, 64
HK = HQ + HKV
LRU_C = 8.0
NEG = -1e30

DFF = 2816
FU = 256
NU = DFF // FU
PIECE = KT * FU

GH = 8
NLEV = 7

NE, FE = 8, 3584
FC = 512
NC = FE // FC

DA, DB, DC = 384, 256, 384
AT = DA // P
TAPS_A, TAPS_C = 31, 3
HB = 4
LAYERS2 = 2


def columns(items):
    at, where = 0, {}
    for name, width in items:
        where[name] = (at, at + width)
        at += width
    return where, at


CONST_COLS, CONST_W = columns([
    ("ident", P), ("upto", P), ("before", P), ("ones", P), ("iota", P), ("level", NLEV * P),
    ("future", P), ("window", 2 * P), ("cos", NT * 32), ("sin", NT * 32), ("eight", NE),
])
SMALL_COLS, SMALL_W = columns([
    ("g0", KT), ("g1", KT), ("g2", KT), ("g3", KT),
    ("lconv_w", LT * CONV), ("lconv_b", LT), ("b_a", LT), ("b_i", LT), ("lam", LT),
    ("qk_gain", HK * DH), ("sinks", NT * HQ), ("w_a", LT * P), ("w_i", LT * P),
    ("oconv_w", 3 * GH * CONV), ("a_log", NT * GH), ("dt_bias", NT * GH), ("out_gain", P),
    ("w_ab", KT * 2 * GH), ("router", KT * NE),
])
SMALL2_COLS, SMALL2_W = columns([
    ("g0", KT), ("g1", KT), ("g2", KT), ("conv_a_w", AT * TAPS_A), ("conv_a_b", AT),
    ("ln_a_g", AT), ("ln_a_b", AT), ("ln_v_g", DB), ("ln_v_b", DB), ("w_s", HB * P), ("b_s", HB),
    ("conv_c_w", AT * TAPS_C),
])

class Signals(dict):

    def __init__(self, nc, ctx):
        super().__init__()
        self.nc, self.ctx = nc, ctx

    def __missing__(self, name):
        self[name] = self.ctx.enter_context(self.nc.semaphore(name))
        return self[name]


def bc(ap, axis, n):
    ap = ap.unsqueeze(axis)
    shape = list(ap.shape)
    shape[axis] = n
    return ap.to_broadcast(shape)


class Place:
    pass


def place(nc, ctx, w):
    m = Place()

    def sb(name, width, dt=F32):
        return ctx.enter_context(nc.sbuf_tensor(name, [P, width], dt))

    def cut(t, at, *dims):
        n = 1
        for d in dims:
            n *= d
        ap = t[:, at:at + n]
        if len(dims) == 2:
            return ap.rearrange("p (a b) -> p a b", b=dims[1])
        if len(dims) == 3:
            return ap.rearrange("p (a b c) -> p a b c", b=dims[1], c=dims[2])
        return ap

    m.w = w
    m.sig = Signals(nc, ctx)
    m.ps = [ctx.enter_context(nc.psum_tensor(f"bank{i}", [P, HALF], F32)) for i in range(8)]
    m.mslot = [sb(f"mslot{i}", KT * HALF) for i in range(4)]
    m.res = cut(sb("res", NT * D), 0, NT, D)
    m.xn = cut(sb("xn", NT * D), 0, NT, D)
    m.xT = cut(sb("xT", KT * SEQ), 0, KT, SEQ)
    consts = sb("consts", CONST_W)
    small = sb("small", SMALL_W)
    small2 = sb("small2", LAYERS2 * SMALL2_W)
    m.consts, m.small, m.small2 = consts, small, small2
    m.c = {n: consts[:, a:b] for n, (a, b) in CONST_COLS.items()}
    m.s = {n: small[:, a:b] for n, (a, b) in SMALL_COLS.items()}
    m.s2 = [{n: small2[:, l * SMALL2_W + a:l * SMALL2_W + b] for n, (a, b) in SMALL2_COLS.items()}
            for l in range(LAYERS2)]
    stats = sb("stats", 32)
    m.ss, m.ms, m.sd, m.rstd = stats[:, 0:2], stats[:, 2:4], stats[:, 4:6], stats[:, 6:8]
    tiny = sb("tiny", 400)
    m.tiny = lambda i, n: tiny[:, i:i + n]
    m.q_int = sb("q_int", 2, I32)
    R = 23600
    with nc.sbuf_tensor("scratch", [P, R], F32) as scratch:
        m.scr = lambda at, *dims: cut(scratch, at, *dims)
    f0 = R - 3 * PIECE
    m.splits = {u: i for i, u in enumerate((1, 4, 6, 7, 9))}
    m.fslot = [m.scr(f0 + i * PIECE, PIECE) for i in range(3)]
    m.whi = [sb(f"weights_hi{i}", PIECE, F32R) for i in range(3)]
    m.wlo = [sb(f"weights_lo{i}", PIECE, F32R) for i in range(3)]
    m.xh, m.xl = cut(sb("x_hi", KT * SEQ, F32R), 0, KT, SEQ), cut(sb("x_lo", KT * SEQ, F32R), 0, KT, SEQ)
    m.hh, m.hl = sb("hidden_hi", HALF, F32R), sb("hidden_lo", HALF, F32R)
    return m



def split_product(pe, out, stationary, moving, start, stop):
    pe.matmul(out, stationary[0], moving[0], start=start, stop=False)
    pe.matmul(out, stationary[0], moving[1], start=False, stop=False)
    return pe.matmul(out, stationary[1], moving[0], start=False, stop=stop)



def mix_blocks(w):
    def cols(t, a, b):
        return t[:, a:b].rearrange("(k p) n -> p k n", p=P), b - a

    e_in, e_out, o_in, o_out = w["e_w_in"][0], w["e_w_out"][0], w["o_w_in"][0], w["o_w_out"][0]
    out = [cols(e_in, 1024, 1536), cols(e_in, 1536, 1792), cols(e_in, 0, 512), cols(e_in, 512, 1024)]
    out += [cols(e_out, 0, 512), cols(e_out, 512, 1024)]
    out += [cols(o_in, 512 * i, 512 * i + 512) for i in range(8)]
    out += [cols(o_out, 0, 512), cols(o_out, 512, 1024)]
    for l in range(LAYERS2):
        w_in, w_out = w["w_in_2"][l], w["w_out_2"][l]
        where, _ = columns([("a_val", DA), ("a_gate", DA), ("b", 2 * DB), ("c_b", DC), ("c_c", DC), ("c_x", DC)])
        out += [cols(w_in, *where[n]) for n in ("a_val", "a_gate", "c_c", "b", "c_x", "c_b")]
        out += [cols(w_out, 0, 512), cols(w_out, 512, 1024)]
    return out


B_EVEN, B_ODD, B_SECOND = 0, 6, 16


def mblock(m, i):
    width = m.blocks[i][1]
    return m.mslot[i % 4][:, 0:KT * width].rearrange("p (k n) -> p k n", n=width)


def load_block(sp, m, i):
    if i >= 4:
        block_used(sp, m, i - 4)
    if i >= B_SECOND and i < B_SECOND + 4:
        sp.wait_ge(m.sig["r_end"], 1)
    sp.dma_start(mblock(m, i), m.blocks[i][0]).then_inc(m.sig[f"m_in{i % 4}"], 16)


def block_used(eng, m, i):
    eng.wait_ge(m.sig[f"m_used{i % 4}"], i // 4 + 1)


def block_in(pe, m, i):
    pe.wait_ge(m.sig[f"m_in{i % 4}"], 16 * (i // 4 + 1))


def ffn_piece(kind, u):
    if isinstance(u, int) and u == 0 and kind != "down":
        return {"gate": 0, "up": 1}[kind]
    if isinstance(u, int) and u == NU - 1 and kind == "down":
        return 3 * NU - 1
    return 3 * u + {"gate": -1, "down": 3, "up": 1}[kind]


KINDS = {"gate": 0, "up": 1, "down": 2}


def ffn_load(sp, m, v, w_gate, w_up, w_down, between):
    s = m.sig
    g = w_gate.rearrange("(k p) f -> p k f", p=P)
    up = w_up.rearrange("(k p) f -> p k f", p=P)
    dn = w_down.rearrange("(k p) n -> p k n", p=P)
    inner = lambda i: m.fslot[i].rearrange("p (k f) -> p k f", k=KT)

    def free(kind, u):
        if isinstance(u, int) and u == 0:
            if v > 0:
                sp.wait_ge(s["f_lo"], 3 * NU * (v - 1) + ffn_piece(kind, NU - 1) + 1)
        elif isinstance(u, int):
            sp.wait_ge(s["f_lo"], 3 * NU * v + ffn_piece(kind, u - 1) + 1)
        elif kind == "down":
            sp.wait_ge(s["f_lo"], 3 * NU * v + 3 * u + 1)
        else:
            sp.wait_ge(s["f_lo"], 3 * NU * v + 3 * u - {"gate": 3, "up": 1}[kind])

    def gate_up(u):
        free("gate", u)
        sp.dma_start(inner(0), g[:, :, bass.ds(u * FU, FU)]).then_inc(s["f_gin"], 16)
        free("up", u)
        sp.dma_start(inner(1), up[:, :, bass.ds(u * FU, FU)]).then_inc(s["f_uin"], 16)

    def down(u):
        free("down", u)
        sp.dma_start(m.fslot[2].rearrange("p (k n) -> p k n", n=D),
                     dn[:, bass.ds(u * (FU // P), FU // P), :]).then_inc(s["f_din"], 16)

    gate_up(0)
    down(0)
    between()
    gate_up(1)
    down(1)
    with sp.Fori(2, NU) as u:
        gate_up(u)
        down(u)



def norm_dve(dve, m, u, gain, split=None):
    s = m.sig
    if u == 0:
        dve.wait_ge(s["x_in"], 16)
    else:
        dve.drain()
    dve.tensor_tensor_reduce(m.xn[:, 0, :], m.res[:, 0, :], m.res[:, 0, :], 1.0, 0.0, ALU.mult, ALU.add,
                             m.ss[:, 0:1])
    dve.drain()
    dve.wait_ge(s["n_ss"], u + 1)
    dve.tensor_scalar(m.ms, m.ss, 1.0 / D, EPS, ALU.mult, ALU.add).then_inc(s["n_ms"], 1)
    dve.wait_ge(s["n_std"], u + 1)
    dve.reciprocal(m.rstd, m.sd).then_inc(s["n_rstd"], 1)
    dve.drain()
    dve.tensor_scalar(m.xn[:, 0, :], m.res[:, 0, :], m.rstd[:, 0:1], None, ALU.mult).then_inc(s["n_xn_d"], 1)
    if gain is None:
        return
    if split is not None:
        split[0]()
        for k in range(KT):
            dve.wait_ge(s["n_xh"], 4 * m.splits[u] + k // 2 + 1)
            last = dve.scalar_tensor_tensor(m.xl[:, k, :], m.ps[k // 2][:, (k % 2) * SEQ:(k % 2 + 1) * SEQ],
                                            gain[:, k:k + 1], m.xh[:, k, :], ALU.mult, ALU.subtract)
        last.then_inc(s["n_xl"], 1)
        split[1]()
        return
    if u == 0:
        dve.wait_ge(s["small_in"], 16)
    for b in (0, 2):
        dve.wait_ge(s["n_tr"], 4 * u + b + 1)
        for k in (2 * b, 2 * b + 1):
            dve.tensor_scalar(m.xT[:, k, :], m.ps[b][:, (k % 2) * SEQ:(k % 2 + 1) * SEQ], gain[:, k:k + 1],
                              None, ALU.mult).then_inc(s["n_xT_d"], 1)


def norm_act(act, m, u, gain, split=None):
    s = m.sig
    if u == 0:
        act.wait_ge(s["x_in"], 16)
    else:
        act.wait_ge(s["res_ready"], u)
    act.activation(m.xn[:, 1, :], m.res[:, 1, :], ACT.Square, accum_out=m.ss[:, 1:2]).then_inc(s["n_ss"], 1)
    act.wait_ge(s["n_ms"], u + 1)
    act.activation(m.sd, m.ms, ACT.Sqrt).then_inc(s["n_std"], 1)
    act.wait_ge(s["n_rstd"], u + 1)
    act.activation(m.xn[:, 1, :], m.res[:, 1, :], ACT.Copy, scale=m.rstd[:, 1:2]).then_inc(s["n_xn_a"], 1)
    if gain is None:
        return
    if split is not None:
        split[0]()
        for k in range(KT):
            act.wait_ge(s["n_tr"], 4 * u + k // 2 + 1)
            last = act.activation(m.xh[:, k, :], m.ps[k // 2][:, (k % 2) * SEQ:(k % 2 + 1) * SEQ], ACT.Copy,
                                  scale=gain[:, k:k + 1])
            if k % 2 == 1:
                last.then_inc(s["n_xh"], 1)
        split[1]()
        return
    if u == 0:
        act.wait_ge(s["small_in"], 16)
    for b in (1, 3):
        act.wait_ge(s["n_tr"], 4 * u + b + 1)
        for k in (2 * b, 2 * b + 1):
            act.activation(m.xT[:, k, :], m.ps[b][:, (k % 2) * SEQ:(k % 2 + 1) * SEQ], ACT.Copy,
                           scale=gain[:, k:k + 1]).then_inc(s["n_xT_a"], 1)


def norm_pe(pe, m, u):
    s = m.sig
    if u == 0:
        pe.wait_ge(s["ident_in"], 16)
    pe.wait_ge(s["n_xn_d"], u + 1)
    pe.wait_ge(s["n_xn_a"], u + 1)
    for b in range(4):
        for k in (2 * b, 2 * b + 1):
            for t in range(NT):
                at = (k % 2) * SEQ + t * P
                last = pe.transpose(m.ps[b][:, at:at + P], m.xn[:, t, k * P:(k + 1) * P], m.c["ident"])
        last.then_inc(s["n_tr"], 1)
    if u in m.splits:
        pe.wait_ge(s["n_xl"], m.splits[u] + 1)
    else:
        n = u - sum(i < u for i in m.splits)
        pe.wait_ge(s["n_xT_d"], 4 * n + 4)
        pe.wait_ge(s["n_xT_a"], 4 * n + 4)



def out_pe(pe, m, i, yT):
    s = m.sig
    for half in range(2):
        block_in(pe, m, i + half)
        for t in range(NT):
            for k in range(KT):
                last = pe.matmul(m.ps[4 + 2 * t + half][:, :], yT[:, k, t * P:(t + 1) * P],
                                 mblock(m, i + half)[:, k, :], start=(k == 0), stop=(k == KT - 1))
            if t == NT - 1:
                last.then_inc(s[f"m_used{(i + half) % 4}"], 1)
            else:
                last.then_inc(s["o_done"], 1)


def out_dve(dve, m, i, n, scale=1.0):
    s = m.sig
    for half in range(2):
        for t in range(NT):
            if t == NT - 1:
                block_used(dve, m, i + half)
            else:
                dve.wait_ge(s["o_done"], 2 * n + half + 1)
            r = m.res[:, t, half * HALF:(half + 1) * HALF]
            last = dve.tensor_tensor(r, m.ps[4 + 2 * t + half][:, :], r, ALU.add)
    last.then_inc(s["res_ready"], 1)



def ffn_pe(pe, m, v):
    s, at = m.sig, v * NU

    def parts(kind, n):
        i = KINDS[kind]
        return [t[i][:, :].rearrange("p (k n) -> p k n", n=n) for t in (m.whi, m.wlo)]

    def split_in(kind, u):
        pe.wait_ge(s["f_lo"], 3 * at + ffn_piece(kind, u) + 1)

    def inner(kind, bank, done):
        hi, lo = parts(kind, FU)
        for j in range(FU // P):
            cols = slice(j * P, (j + 1) * P)
            for k in range(KT):
                last = split_product(pe, m.ps[bank][:, j * SEQ:(j + 1) * SEQ], (hi[:, k, cols], lo[:, k, cols]),
                                     (m.xh[:, k, :], m.xl[:, k, :]), start=(k == 0), stop=(k == KT - 1))
        last.then_inc(s[done], 1)

    def gate(u):
        split_in("gate", u)
        if not (v == 0 and isinstance(u, int) and u == 0):
            pe.wait_ge(s["f_silu"], u + at)
        inner("gate", 0, "f_gdone")

    def up(u):
        split_in("up", u)
        if not (v == 0 and isinstance(u, int) and u == 0):
            pe.wait_ge(s["f_h"], u + at)
        inner("up", 1, "f_udone")

    def down(u, first=False, final=False):
        split_in("down", NU - 1 if final else u)
        pe.wait_ge(s["f_h"], u + at + 1)
        hi, lo = parts("down", D)
        hh, hl = (t[:, :].rearrange("p (k t) -> p k t", t=SEQ) for t in (m.hh, m.hl))
        for k in range(FU // P):
            for t in range(NT):
                for half in range(2):
                    cols, tok = slice(half * HALF, (half + 1) * HALF), slice(t * P, (t + 1) * P)
                    last = split_product(pe, m.ps[4 + 2 * t + half][:, :], (hh[:, k, tok], hl[:, k, tok]),
                                         (hi[:, k, cols], lo[:, k, cols]),
                                         start=first and k == 0, stop=final and k == FU // P - 1)
        last.then_inc(s["f_ddone"], 1)

    gate(0)
    up(0)
    gate(1)
    down(0, first=True)
    up(1)
    with pe.Fori(2, NU) as u:
        gate(u)
        down(u - 1)
        up(u)
    down(NU - 1, final=True)


def ffn_parts_free(eng, m, v, kind, u):
    if not (v == 0 and isinstance(u, int) and u == 0):
        eng.wait_ge(m.sig[f"f_{kind[0]}done"], u + v * NU)


def ffn_hi(act, m, v, kind, u):
    i, at = KINDS[kind], v * NU
    act.wait_ge(m.sig[f"f_{kind[0]}in"], (u + at) * 16 + 16)
    ffn_parts_free(act, m, v, kind, u)
    act.activation(m.whi[i][:, :], m.fslot[i], ACT.Copy).then_inc(m.sig["f_hi"], 1)


def ffn_lo(dve, m, v, kind, u):
    i, at = KINDS[kind], v * NU
    dve.wait_ge(m.sig["f_hi"], 3 * at + ffn_piece(kind, u) + 1)
    ffn_parts_free(dve, m, v, kind, u)
    dve.tensor_tensor(m.wlo[i][:, :], m.fslot[i], m.whi[i][:, :], ALU.subtract).then_inc(m.sig["f_lo"], 1)


def ffn_act(act, m, v):
    s, at = m.sig, v * NU
    silu = ffn_silu(m)

    def one(u):
        act.wait_ge(s["f_gdone"], u + at + 1)
        if not (v == 0 and isinstance(u, int) and u == 0):
            act.wait_ge(s["f_h"], u + at)
        act.activation(silu, m.ps[0][:, :], ACT.Silu).then_inc(s["f_silu"], 1)

    one(0)
    ffn_hi(act, m, v, "gate", 1)
    ffn_hi(act, m, v, "down", 0)
    ffn_hi(act, m, v, "up", 1)
    with act.Fori(1, NU - 1) as u:
        one(u)
        ffn_hi(act, m, v, "gate", u + 1)
        ffn_hi(act, m, v, "down", u)
        ffn_hi(act, m, v, "up", u + 1)
    one(NU - 1)
    ffn_hi(act, m, v, "down", NU - 1)


def ffn_silu(m):
    return m.xT.rearrange("p k t -> p (k t)")[:, 0:HALF]


def ffn_dve(dve, m, v, scale):
    s, at = m.sig, v * NU
    silu, h = ffn_silu(m), m.xT.rearrange("p k t -> p (k t)")[:, HALF:2 * HALF]

    def hidden(u):
        dve.wait_ge(s["f_udone"], u + at + 1)
        dve.wait_ge(s["f_silu"], u + at + 1)
        dve.tensor_tensor(h, m.ps[1][:, :], silu, ALU.mult)
        dve.drain()
        if not (v == 0 and isinstance(u, int) and u == 0):
            dve.wait_ge(s["f_ddone"], u + at)
        dve.tensor_copy(m.hh[:, :], h)
        dve.drain()
        dve.tensor_tensor(m.hl[:, :], h, m.hh[:, :], ALU.subtract).then_inc(s["f_h"], 1)

    ffn_lo(dve, m, v, "gate", 1)
    ffn_lo(dve, m, v, "down", 0)
    hidden(0)
    ffn_lo(dve, m, v, "up", 1)
    with dve.Fori(1, NU - 1) as u:
        ffn_lo(dve, m, v, "gate", u + 1)
        ffn_lo(dve, m, v, "down", u)
        hidden(u)
        ffn_lo(dve, m, v, "up", u + 1)
    ffn_lo(dve, m, v, "down", NU - 1)
    hidden(NU - 1)
    dve.wait_ge(s["f_ddone"], at + NU)
    for t in range(NT):
        for half in range(2):
            r = m.res[:, t, half * HALF:(half + 1) * HALF]
            last = dve.scalar_tensor_tensor(r, m.ps[4 + 2 * t + half][:, :], scale, r, ALU.mult, ALU.add)
    last.then_inc(s["res_ready"], 1)


def softplus_head(dve, x, neg, mag):
    dve.tensor_scalar(neg, x, -1.0, None, ALU.mult)
    dve.drain()
    return dve.tensor_tensor(mag, x, neg, ALU.max)


def softplus_tail(dve, x, e, z, z2, p, out):
    dve.tensor_scalar(z2, e, 2.0, None, ALU.add)
    dve.drain()
    dve.reciprocal(p, z2)
    dve.drain()
    dve.tensor_tensor(z, e, p, ALU.mult)
    dve.drain()
    dve.tensor_tensor(z2, z, z, ALU.mult)
    dve.drain()
    dve.tensor_scalar(p, z2, 1.0 / 17, 1.0 / 15, ALU.mult, ALU.add)
    for d in (13, 11, 9, 7, 5, 3, 1):
        dve.drain()
        dve.tensor_tensor(p, p, z2, ALU.mult)
        dve.drain()
        dve.tensor_scalar(p, p, 1.0 / d, None, ALU.add)
    dve.drain()
    dve.tensor_tensor(z, z, p, ALU.mult)
    dve.tensor_scalar(z2, x, 0.0, None, ALU.max)
    dve.drain()
    return dve.scalar_tensor_tensor(out, z, 2.0, z2, ALU.mult, ALU.add)



def steps(names):
    value, seen = {}, []
    for i, name in enumerate(names.split()):
        seen.append(name)
        value[name, seen.count(name)] = i + 1
    return value


E_DVE = steps("lamabs ms qk xc kTd pev pev nm L u2 pn ylru pTd pTd pTd od")
E_ACT = steps("lamexp sd qTa qTa gl gl rs rs rs rs rs rs rs rs a th exp beta pTa pTa pTa oa")


def even_mem(m):
    e = Place()
    e.xc, e.gl, e.rg, e.gi = (m.scr(i * 1024, LT, SEQ) for i in range(4))
    e.aa, e.th, e.hh = (m.scr(i * 1024, LT, SEQ) for i in range(4, 7))
    e.q10 = m.scr(7168, NT, HK * DH)
    e.vs = m.scr(8448, NT, HKV * DH)
    e.sq = m.scr(8704, NT, HK * DH)
    e.t1 = m.scr(8704, NT, HK, 32)
    e.t2 = m.scr(9344, NT, HK, 32)
    e.qr = m.scr(9984, NT, HK * DH)
    e.kd = m.scr(11264, NT, HKV, 2 * DH)
    e.qT = m.scr(11776, HQ // 2, SEQ)
    e.kT = m.scr(12800, HKV, SEQ)
    e.p0 = m.scr(13312, HQ, P)
    e.pT0 = m.scr(14336, HQ, P)
    e.yT = m.scr(15360, KT, SEQ)
    e.p1 = m.xn.rearrange("p t d -> p (t d)").rearrange("p (h k) -> p h k", h=HQ)
    e.pT1 = m.xT.rearrange("p k t -> p (k t)").rearrange("p (n h q) -> p n h q", n=2, h=HQ)
    e.ss, e.sd, e.r = m.tiny(0, 20), m.tiny(20, 20), m.tiny(40, 20)
    e.lneg, e.lmag, e.lexp, e.lz, e.lz2, e.lp, e.c8 = (m.tiny(60 + 4 * i, 4) for i in range(7))
    e.mx, e.nm, e.den, e.es, e.rd = (m.tiny(100 + 16 * i, 16) for i in range(5))
    return e


def even_pe(pe, m):
    s, e, c = m.sig, even_mem(m), m.c
    for i in (0, 1):
        block_in(pe, m, i)
        width = m.blocks[i][1]
        for t in range(NT):
            for k in range(KT):
                last = pe.matmul(m.ps[4 + 2 * i + t][:, 0:width], m.xT[:, k, t * P:(t + 1) * P],
                                 mblock(m, i)[:, k, :], start=(k == 0), stop=(k == KT - 1))
        last.then_inc(s[f"m_used{i}"], 1)

    def recurrent(i, bank, parts):
        for j in parts:
            for k in range(KT):
                last = pe.matmul(m.ps[bank + j // 2][:, (j % 2) * SEQ:(j % 2 + 1) * SEQ],
                                 mblock(m, i)[:, k, j * P:(j + 1) * P], m.xT[:, k, :],
                                 start=(k == 0), stop=(k == KT - 1))
        return last

    block_in(pe, m, 2)
    recurrent(2, 0, range(LT)).then_inc(s["m_used2"], 1)
    block_in(pe, m, 3)
    recurrent(3, 2, (0, 1))
    pe.wait_ge(s["e_dve"], E_DVE["qk", 1])
    for t in range(NT):
        for j in range(HQ // 2):
            last = pe.transpose(m.ps[4 + t][:, j * P:(j + 1) * P], e.qr[:, t, j * P:(j + 1) * P], c["ident"])
        for j in range(HKV):
            last = pe.transpose(m.ps[6][:, (t * HKV + j) * P:(t * HKV + j + 1) * P], e.kd[:, t, j, :], c["ident"])
    last.then_inc(s["e_qkT"], 1)
    recurrent(3, 2, (2, 3)).then_inc(s["m_used3"], 1)
    pe.wait_ge(s["e_act"], E_ACT["qTa", 2])
    pe.wait_ge(s["e_dve"], E_DVE["kTd", 1])

    def score(n, h, bank, at):
        rows = slice((h % 2) * DH, (h % 2 + 1) * DH)
        return pe.matmul(m.ps[bank][:, at:at + (n + 1) * P], e.qT[rows, h // 2, n * P:(n + 1) * P],
                         e.kT[rows, h // (HQ // HKV), 0:(n + 1) * P], start=True, stop=True)

    for h in range(HQ):
        last = score(0, h, 4 + h % 2, (h // 2) * P)
    last.then_inc(s["e_sc"], 1)
    for h in range(4):
        last = score(1, h, 6 + h % 2, (h // 2) * 2 * P)
    last.then_inc(s["e_sc"], 1)
    pe.wait_ge(s["e_dve"], E_DVE["pev", 2])
    for h in range(4, HQ):
        last = score(1, h, 4 + h % 2, (h // 2 - 2) * 2 * P)
    last.then_inc(s["e_sc"], 1)
    pe.wait_ge(s["e_dve"], E_DVE["xc", 1])
    pe.wait_ge(s["e_act"], E_ACT["gl", 2])
    for bank, name, done in ((0, "w_a", "e_r"), (2, "w_i", "e_i")):
        for j in range(LT):
            last = pe.matmul(m.ps[bank + j // 2][:, (j % 2) * SEQ:(j % 2 + 1) * SEQ],
                             m.s[name][:, j * P:(j + 1) * P], e.xc[:, j, :], start=True, stop=True)
        last.then_inc(s[done], 1)
    pe.wait_ge(s["e_dve"], E_DVE["pn", 1])
    for h in range(HQ):
        last = pe.transpose(m.ps[4 + h // 4][:, (h % 4) * P:(h % 4 + 1) * P], e.p0[:, h, :], c["ident"])
        if h % 4 == 3:
            last.then_inc(s["e_pT"], 1)
    for n in range(2):
        for h in range(HQ):
            bank = (6, 7, 0, 1)[2 * n + h // 4]
            last = pe.transpose(m.ps[bank][:, (h % 4) * P:(h % 4 + 1) * P], e.p1[:, h, n * P:(n + 1) * P], c["ident"])
            if h % 4 == 3:
                last.then_inc(s["e_pT"], 1)
    pe.wait_ge(s["e_act"], E_ACT["pTa", 3])
    pe.wait_ge(s["e_dve"], E_DVE["pTd", 3])
    for t in range(NT):
        for h in range(HQ):
            kv = h // (HQ // HKV)
            out = m.ps[2 + t][(h % 2) * DH:(h % 2 + 1) * DH, (h // 2) * P:(h // 2 + 1) * P]
            for n in range(t + 1):
                rhs = e.pT0[:, h, :] if t == 0 else e.pT1[:, n, h, :]
                last = pe.matmul(out, e.vs[:, n, kv * DH:(kv + 1) * DH], rhs, start=(n == 0), stop=(n == t))
        last.then_inc(s["e_o"], 1)
    pe.wait_ge(s["e_act"], E_ACT["oa", 1])
    pe.wait_ge(s["e_dve"], E_DVE["od", 1])
    pe.wait_ge(s["e_dve"], E_DVE["ylru", 1])
    out_pe(pe, m, B_EVEN + 4, e.yT)


def even_act(act, m):
    s, e = m.sig, even_mem(m)
    act.wait_ge(s["e_dve"], E_DVE["lamabs", 1])
    act.activation(e.lexp, e.lmag, ACT.Exp, scale=-1.0).then_inc(s["e_act"], 1)
    act.wait_ge(s["e_dve"], E_DVE["ms", 1])
    act.activation(e.sd, e.ss, ACT.Sqrt).then_inc(s["e_act"], 1)
    act.wait_ge(s["e_qkT"], 1)
    for t in range(NT):
        act.activation(e.qT[:, :, t * P:(t + 1) * P], m.ps[4 + t][:, :].rearrange("p (a t) -> p a t", a=4),
                       ACT.Copy).then_inc(s["e_act"], 1)
    block_used(act, m, 3)
    for b in range(2):
        act.activation(e.gl[:, 2 * b:2 * b + 2, :], m.ps[2 + b][:, :].rearrange("p (a t) -> p a t", a=2),
                       ACT.Gelu_apprx_tanh).then_inc(s["e_act"], 1)
    for bank, out, bias, wait in ((0, e.rg, "b_a", "e_r"), (2, e.gi, "b_i", "e_i")):
        act.wait_ge(s[wait], 1)
        for j in range(LT):
            act.activation(out[:, j, :], m.ps[bank + j // 2][:, (j % 2) * SEQ:(j % 2 + 1) * SEQ], ACT.Sigmoid,
                           bias=m.s[bias][:, j:j + 1]).then_inc(s["e_act"], 1)
    act.wait_ge(s["e_dve"], E_DVE["L", 1])
    act.activation(e.aa, e.rg, ACT.Exp).then_inc(s["e_act"], 1)
    act.activation(e.th, e.rg, ACT.Tanh, scale=-1.0).then_inc(s["e_act"], 1)
    act.wait_ge(s["e_dve"], E_DVE["nm", 1])
    act.activation(e.es, e.es, ACT.Exp)
    for t in range(NT):
        for h in range(HQ):
            p = (e.p0, e.p1)[t][:, h, :]
            i = t * HQ + h
            last = act.activation(p, p, ACT.Exp, bias=e.nm[:, i:i + 1], accum_out=e.den[:, i:i + 1])
    last.then_inc(s["e_act"], 1)
    act.wait_ge(s["e_dve"], E_DVE["u2", 1])
    act.activation(e.th, e.hh, ACT.Sqrt).then_inc(s["e_act"], 1)
    for i, bank in ((1, 4), (3, 6), (5, 0)):
        act.wait_ge(s["e_pT"], i)
        out = e.pT0[:, 0:4, :] if i == 1 else e.pT1[:, i // 4, 0:4, :]
        act.activation(out, m.ps[bank][:, :].rearrange("p (a t) -> p a t", a=4), ACT.Copy).then_inc(s["e_act"], 1)
    act.wait_ge(s["e_o"], 1)
    act.activation(e.yT[:, LT:KT, 0:P], m.ps[2][:, :].rearrange("p (a t) -> p a t", a=4),
                   ACT.Copy).then_inc(s["e_act"], 1)


def even_dve(dve, m):
    s, e, c, sm = m.sig, even_mem(m), m.c, m.s
    dve.wait_ge(s["const_in"], 16)
    dve.tensor_scalar(e.c8, sm["lam"], -1.0, None, ALU.mult)
    dve.drain()
    softplus_head(dve, e.c8, e.lneg, e.lmag).then_inc(s["e_dve"], 1)
    dve.wait_ge(s["e_act"], E_ACT["lamexp", 1])
    softplus_tail(dve, e.c8, e.lexp, e.lz, e.lz2, e.lp, e.lneg)
    dve.drain()
    dve.tensor_scalar(e.c8, e.lneg, -LRU_C, None, ALU.mult)
    block_used(dve, m, 0)
    block_used(dve, m, 1)
    for t in range(NT):
        dve.tensor_copy(e.q10[:, t, 0:HALF], m.ps[4 + t][:, :])
        dve.tensor_copy(e.q10[:, t, HALF:HK * DH], m.ps[6 + t][:, 0:P])
        dve.tensor_copy(e.vs[:, t, :], m.ps[6 + t][:, P:2 * P])
    dve.drain()
    dve.tensor_tensor(e.sq, e.q10, e.q10, ALU.mult)
    dve.drain()
    dve.tensor_reduce(e.ss, e.sq.rearrange("p t (h d) -> p (t h) d", h=HK), AX.X, ALU.add)
    dve.drain()
    dve.tensor_scalar(e.ss, e.ss, 1.0 / DH, EPS, ALU.mult, ALU.add).then_inc(s["e_dve"], 1)
    dve.wait_ge(s["e_act"], E_ACT["sd", 1])
    dve.reciprocal(e.r, e.sd)
    dve.drain()
    dve.tensor_tensor(e.q10, e.q10, bc(sm["qk_gain"], 1, NT), ALU.mult)
    dve.drain()
    heads = e.q10.rearrange("p t (h d) -> p (t h) d", h=HK)
    dve.tensor_tensor(heads, heads, bc(e.r, 2, DH), ALU.mult)
    dve.drain()
    for t in range(NT):
        x = e.q10[:, t, :].rearrange("p (h a d) -> p h a d", h=HK, a=2)
        o = e.qr[:, t, :].rearrange("p (h a d) -> p h a d", h=HK, a=2)
        cos, sin = (bc(c[n][:, t * 32:(t + 1) * 32], 1, HK) for n in ("cos", "sin"))
        for a, op in ((0, ALU.subtract), (1, ALU.add)):
            dve.tensor_tensor(e.t1[:, t], x[:, :, a, :], cos, ALU.mult)
            dve.tensor_tensor(e.t2[:, t], x[:, :, 1 - a, :], sin, ALU.mult)
            dve.drain()
            dve.tensor_tensor(o[:, :, a, :], e.t1[:, t], e.t2[:, t], op)
            dve.drain()
        k = e.qr[:, t, HALF:HK * DH].rearrange("p (h d) -> p h d", h=HKV)
        last = dve.tensor_copy(e.kd[:, t].rearrange("p h (a d) -> p h a d", a=2), bc(k, 2, 2))
    last.then_inc(s["e_dve"], 1)
    block_used(dve, m, 2)
    raw = [m.ps[j // 2][:, (j % 2) * SEQ:(j % 2 + 1) * SEQ] for j in range(LT)]
    w = [sm["lconv_w"][:, j * CONV:(j + 1) * CONV] for j in range(LT)]
    for j in range(LT):
        dve.tensor_scalar(e.xc[:, j, :], raw[j], w[j][:, CONV - 1:CONV], sm["lconv_b"][:, j:j + 1], ALU.mult, ALU.add)
    for lag in range(1, CONV):
        dve.drain()
        for j in range(LT):
            last = dve.scalar_tensor_tensor(e.xc[:, j, lag:SEQ], raw[j][:, 0:SEQ - lag],
                                            w[j][:, CONV - 1 - lag:CONV - lag], e.xc[:, j, lag:SEQ], ALU.mult, ALU.add)
    last.then_inc(s["e_dve"], 1)
    dve.wait_ge(s["e_qkT"], 1)
    dve.tensor_copy(e.kT.rearrange("p h (t k) -> p t h k", t=NT),
                    m.ps[6][:, :].rearrange("p (t h k) -> p t h k", t=NT, h=HKV)).then_inc(s["e_dve"], 1)
    p0 = e.p0.rearrange("p (a b) k -> p b a k", b=2)
    p1 = e.p1.rearrange("p (a b) k -> p b a k", b=2)
    dve.wait_ge(s["e_sc"], 1)
    for b in range(2):
        dve.scalar_tensor_tensor(p0[:, b], m.ps[4 + b][:, :].rearrange("p (a k) -> p a k", a=4), DH ** -0.5,
                                 bc(c["window"][:, P:2 * P], 1, 4), ALU.mult, ALU.add).then_inc(s["e_dve"], 1)
    for half in range(2):
        dve.wait_ge(s["e_sc"], 2 + half)
        for b in range(2):
            bank = (6, 4)[half] + b
            dve.scalar_tensor_tensor(p1[:, b, 2 * half:2 * half + 2], m.ps[bank][:, :].rearrange("p (a k) -> p a k", a=2),
                                     DH ** -0.5, bc(c["window"], 1, 2), ALU.mult, ALU.add)
    dve.drain()
    dve.tensor_reduce(e.mx[:, 0:HQ], e.p0, AX.X, ALU.max)
    dve.tensor_reduce(e.mx[:, HQ:2 * HQ], e.p1, AX.X, ALU.max)
    dve.drain()
    dve.tensor_tensor(e.mx, e.mx, sm["sinks"], ALU.max)
    dve.drain()
    dve.tensor_tensor(e.es, sm["sinks"], e.mx, ALU.subtract)
    dve.tensor_scalar(e.nm, e.mx, -1.0, None, ALU.mult).then_inc(s["e_dve"], 1)
    dve.wait_ge(s["e_act"], E_ACT["rs", 2 * LT])
    dve.tensor_tensor(e.rg, e.rg, bc(e.c8, 2, SEQ), ALU.mult).then_inc(s["e_dve"], 1)
    dve.wait_ge(s["e_act"], E_ACT["a", 1])
    dve.wait_ge(s["e_act"], E_ACT["th", 1])
    dve.tensor_tensor(e.hh, e.aa, e.aa, ALU.mult)
    dve.tensor_tensor(e.gi, e.gi, e.xc, ALU.mult)
    dve.drain()
    dve.scalar_tensor_tensor(e.hh, e.hh, 1.0, e.th, ALU.add, ALU.mult).then_inc(s["e_dve"], 1)
    dve.wait_ge(s["e_act"], E_ACT["exp", 1])
    dve.tensor_tensor(e.den, e.den, e.es, ALU.add)
    dve.drain()
    dve.reciprocal(e.rd, e.den)
    dve.drain()
    dve.tensor_tensor(e.p0, e.p0, bc(e.rd[:, 0:HQ], 2, P), ALU.mult)
    dve.tensor_tensor(e.p1, e.p1, bc(e.rd[:, HQ:2 * HQ], 2, 2 * P), ALU.mult)
    dve.drain().then_inc(s["e_dve"], 1)
    dve.wait_ge(s["e_act"], E_ACT["beta", 1])
    dve.tensor_tensor(e.gi, e.gi, e.th, ALU.mult)
    dve.drain()
    for j in range(LT):
        dve.tensor_tensor_scan(e.hh[:, j, :], e.aa[:, j, :], e.gi[:, j, :], 0.0, ALU.mult, ALU.add)
    dve.drain()
    dve.tensor_tensor(e.yT[:, 0:LT, :], e.hh, e.gl, ALU.mult).then_inc(s["e_dve"], 1)
    for i, bank in ((2, 5), (4, 7), (6, 1)):
        dve.wait_ge(s["e_pT"], i)
        out = e.pT0[:, 4:8, :] if i == 2 else e.pT1[:, i // 2 - 2, 4:8, :]
        dve.tensor_copy(out, m.ps[bank][:, :].rearrange("p (a t) -> p a t", a=4)).then_inc(s["e_dve"], 1)
    dve.wait_ge(s["e_o"], 2)
    dve.tensor_copy(e.yT[:, LT:KT, P:SEQ], m.ps[3][:, :].rearrange("p (a t) -> p a t", a=4)).then_inc(s["e_dve"], 1)
    out_dve(dve, m, B_EVEN + 4, 0)



def odd_mem(m):
    o = Place()
    o.qkvT = m.scr(0, 3 * GH, SEQ)
    o.yT = m.scr(0, KT, SEQ)
    buf = [m.scr(6144 + i * 1024, GH, P) for i in range(17)]
    o.K, o.BK, o.Q, o.QD, o.BGK, o.BV, o.KD, o.knT, o.bkT, o.qnT, o.qdT, o.dec, o.gb, o.TT, o.S = buf[:15]
    o.C = buf[15:17]
    o.LT, o.AT, o.T, o.Y, o.U, o.WT = o.BK, o.Q, o.dec, o.gb, o.bkT, o.qnT
    o.o = m.xn.rearrange("p t (h e) -> p t h e", h=GH)
    o.sg = m.xT.rearrange("p k t -> p (k t)").rearrange("p (t d) -> p t d", t=NT)
    names = "x neg mag ex z z2 p sp ea eb beta g eG ekd ss sd r oss osd orr".split()
    o.v = {n: m.tiny(16 * i, 16) for i, n in enumerate(names)}
    o.ab = m.tiny(320, 32)
    o.G = m.tiny(352, 32)
    return o


def heads4(bank):
    return bank[:, :].rearrange("p (h e) -> p h e", h=4)


def odd_pe(pe, m):
    s, o, c = m.sig, odd_mem(m), m.c
    w_ab = m.s["w_ab"].rearrange("p (k n) -> p k n", k=KT)
    for t in range(NT):
        for k in range(KT):
            last = pe.matmul(m.ps[0][:, t * 16:(t + 1) * 16], m.xT[:, k, t * P:(t + 1) * P], w_ab[:, k, :],
                             start=(k == 0), stop=(k == KT - 1))
    last.then_inc(s["d_ab"], 1)
    for b in range(6):
        i = B_ODD + b
        block_in(pe, m, i)
        if b >= 2:
            pe.wait_ge(s["d_conv"], b - 1)
        for j in range(4):
            for k in range(KT):
                last = pe.matmul(m.ps[2 + 2 * (b % 2) + j // 2][:, (j % 2) * SEQ:(j % 2 + 1) * SEQ],
                                 mblock(m, i)[:, k, j * P:(j + 1) * P], m.xT[:, k, :],
                                 start=(k == 0), stop=(k == KT - 1))
        last.then_inc(s[f"m_used{i % 4}"], 1)
        if b == 2:
            pe.wait_ge(s["d_g"], 1)
            pe.matmul(m.ps[1][:, 0:16], c["upto"], o.v["g"], start=True, stop=True)
            pe.matmul(m.ps[1][:, 16:32], c["ones"], o.v["g"], start=True, stop=True).then_inc(s["d_G"], 1)
    pe.wait_ge(s["d_Gs"], 1)
    for half in range(2):
        i = B_ODD + 6 + half
        block_in(pe, m, i)
        for t in range(NT):
            for k in range(KT):
                last = pe.matmul(m.ps[((6, 7), (0, 1))[half][t]][:, :], m.xT[:, k, t * P:(t + 1) * P],
                                 mblock(m, i)[:, k, :], start=(k == 0), stop=(k == KT - 1))
        last.then_inc(s[f"m_used{i % 4}"], 1)
    for t in range(NT):
        pe.wait_ge(s["d_conv"], 6)
        pe.wait_ge(s["d_gb"], t + 1)
        if t == 1:
            pe.wait_ge(s["d_oev"], 1)
        for h in range(GH):
            last = pe.matmul(m.ps[2 + h // 4][:, (h % 4) * P:(h % 4 + 1) * P], o.gb[:, h, :], c["upto"],
                             start=True, stop=True)
        last.then_inc(s["d_Gb"], 1)
        pe.wait_ge(s["d_silu"], 6)
        if t == 0:
            pe.wait_ge(s["d_sg"], 1)
        else:
            pe.wait_ge(s["d_Sa"], 1)
        for part, bank in ((0, 4), (1, 6), (2, 0)):
            for h in range(GH):
                last = pe.transpose(m.ps[bank + h // 4][:, (h % 4) * P:(h % 4 + 1) * P],
                                    o.qkvT[:, part * GH + h, t * P:(t + 1) * P], c["ident"])
            last.then_inc(s["d_tr"], 1)
        pe.wait_ge(s["d_tok"], t + 1)
        back = [(o.K, 4), (o.BK, 6), (o.Q, 0)]
        if t == 1:
            pe.wait_ge(s["d_pool"], 2)
            back.append((o.QD, 2))
        for src, bank in back:
            for h in range(GH):
                last = pe.transpose(m.ps[bank + h // 4][:, (h % 4) * P:(h % 4 + 1) * P], src[:, h, :], c["ident"])
            last.then_inc(s["d_tr2"], 1)
        pe.wait_ge(s["d_tr2a"], 2 * t + 2)
        pe.wait_ge(s["d_tr2d"], t + 1)
        for rhs, bank in ((o.bkT, 4), (o.qnT, 6)):
            for h in range(GH):
                last = pe.matmul(m.ps[bank + h // 4][:, (h % 4) * P:(h % 4 + 1) * P], o.knT[:, h, :], rhs[:, h, :],
                                 start=True, stop=True)
            last.then_inc(s["d_kk"], 1)
        pe.wait_ge(s["d_T0"], t + 1)
        for h in range(GH):
            last = pe.transpose(m.ps[h // 4][:, (h % 4) * P:(h % 4 + 1) * P], o.TT[:, h, :], c["ident"])
            if h % 4 == 3:
                last.then_inc(s["d_T0p"], 1)
        for k in range(1, NLEV):
            n = 2 * ((NLEV - 1) * t + k - 1)
            pe.wait_ge(s["d_C"], (NLEV - 1) * t + k)
            for g in range(2):
                if k == 1:
                    pe.wait_ge(s["d_T0a"], 2 * t + g + 1)
                else:
                    pe.wait_ge(s["d_Zd"], n - 2 + g + 1)
                for h in range(4 * g, 4 * g + 4):
                    last = pe.matmul(m.ps[g][:, (h % 4) * P:(h % 4 + 1) * P], o.C[k % 2][:, h, :], o.T[:, h, :],
                                     start=True, stop=True)
                last.then_inc(s["d_Y"], 1)
            for g in range(2):
                pe.wait_ge(s["d_Yc"], n + g + 1)
                for h in range(4 * g, 4 * g + 4):
                    cols = slice((h % 4) * P, (h % 4 + 1) * P)
                    if k < NLEV - 1:
                        pe.matmul(m.ps[2 + g][:, cols], o.TT[:, h, :], o.Y[:, h, :], start=True, stop=True)
                    last = pe.matmul(m.ps[4 + g][:, cols], o.Y[:, h, :], o.TT[:, h, :], start=True, stop=True)
                last.then_inc(s["d_Z"], 1)
        pe.wait_ge(s["d_Zd"], 2 * (NLEV - 1) * (t + 1))
        for h in range(GH):
            last = pe.matmul(m.ps[h // 4][:, (h % 4) * P:(h % 4 + 1) * P], o.TT[:, h, :], o.BV[:, h, :],
                             start=True, stop=True)
        last.then_inc(s["d_U"], 1)
        if t == 1:
            for h in range(GH):
                last = pe.matmul(m.ps[6 + h // 4][:, (h % 4) * P:(h % 4 + 1) * P], o.BGK[:, h, :], o.TT[:, h, :],
                                 start=True, stop=True)
            last.then_inc(s["d_W"], 1)
            pe.wait_ge(s["d_Wa"], 1)
            for h in range(GH):
                last = pe.matmul(m.ps[4 + h // 4][:, (h % 4) * P:(h % 4 + 1) * P], o.WT[:, h, :], o.S[:, h, :],
                                 start=True, stop=True)
            last.then_inc(s["d_WS"], 1)
            pe.wait_ge(s["d_VN"], 1)
        else:
            pe.wait_ge(s["d_Ua"], 1)
        for h in range(GH):
            cols = slice((h % 4) * P, (h % 4 + 1) * P)
            if t == 1:
                pe.matmul(m.ps[2 + h // 4][:, cols], o.qdT[:, h, :], o.S[:, h, :], start=True, stop=False)
            last = pe.matmul(m.ps[2 + h // 4][:, cols], o.AT[:, h, :], o.U[:, h, :], start=(t == 0), stop=True)
        last.then_inc(s["d_O"], 1)
        if t == 0:
            for h in range(GH):
                last = pe.matmul(m.ps[4 + h // 4][:, (h % 4) * P:(h % 4 + 1) * P], o.KD[:, h, :], o.U[:, h, :],
                                 start=True, stop=True)
            last.then_inc(s["d_S"], 1)
    for t in range(NT):
        pe.wait_ge(s["d_on"], t + 1)
        for h in range(GH):
            last = pe.transpose(m.ps[4 * (1 - t) + h // 4][:, (h % 4) * P:(h % 4 + 1) * P],
                                o.o[:, t, h, :], c["ident"])
        last.then_inc(s["d_otr"], 1)
    pe.wait_ge(s["d_ota"], 2)
    pe.wait_ge(s["d_otd"], 2)
    out_pe(pe, m, B_ODD + 8, o.yT)


def odd_pool(pool, m):
    s, o, v = m.sig, odd_mem(m), odd_mem(m).v
    for t in range(NT):
        pool.wait_ge(s["d_tok"], t + 1)
        pool.wait_ge(s["d_eG"], 1)
        th = slice(t * GH, (t + 1) * GH)
        if t == 0:
            pool.tensor_tensor(o.KD, o.K, bc(v["ekd"][:, th], 2, P), ALU.mult).then_inc(s["d_pool"], 1)
        else:
            pool.tensor_tensor(o.BGK, o.BK, bc(v["eG"][:, th], 2, P), ALU.mult)
            pool.tensor_tensor(o.QD, o.Q, bc(v["eG"][:, th], 2, P), ALU.mult)
            pool.drain().then_inc(s["d_pool"], 1)
        pool.wait_ge(s["d_LT"], t + 1)
        for k in range(1, NLEV):
            if (NLEV - 1) * t + k > 2:
                pool.wait_ge(s["d_Y"], 2 * ((NLEV - 1) * t + k - 2))
            pool.tensor_tensor(o.C[k % 2], o.LT, bc(m.c["level"][:, k * P:(k + 1) * P], 1, GH),
                               ALU.mult).then_inc(s["d_C"], 1)


def odd_norm_act(act, m, o, t):
    act.wait_ge(m.sig["d_oss"], t + 1)
    th = slice(t * GH, (t + 1) * GH)
    act.activation(o.v["osd"][:, th], o.v["oss"][:, th], ACT.Sqrt).then_inc(m.sig["d_osd"], 1)


def odd_act(act, m):
    s, o, v = m.sig, odd_mem(m), odd_mem(m).v
    act.wait_ge(s["d_gabs"], 1)
    act.activation(v["ex"], v["mag"], ACT.Exp, scale=-1.0)
    act.activation(v["ea"], m.s["a_log"], ACT.Exp)
    act.activation(v["eb"].rearrange("p (t h) -> p t h", t=NT), o.ab.rearrange("p (t n) -> p t n", t=NT)[:, :, GH:16],
                   ACT.Exp, scale=-1.0)
    act.drain().then_inc(s["d_gexp"], 1)
    for b in range(6):
        act.wait_ge(s["d_conv"], b + 1)
        x = o.qkvT[:, 4 * b:4 * b + 4, :]
        act.activation(x, x, ACT.Silu).then_inc(s["d_silu"], 1)
    for half in range(2):
        block_used(act, m, B_ODD + 6 + half)
    for half in range(2):
        for t in range(NT):
            act.activation(o.sg[:, t, half * HALF:(half + 1) * HALF], m.ps[((6, 7), (0, 1))[half][t]][:, :], ACT.Silu)
    act.drain().then_inc(s["d_sg"], 1)
    act.wait_ge(s["d_Gs"], 1)
    act.activation(v["eG"], o.G[:, 0:16], ACT.Exp)
    act.activation(v["ekd"], o.G[:, 16:32], ACT.Exp)
    act.drain().then_inc(s["d_eG"], 1)
    for t in range(NT):
        act.wait_ge(s["d_diff"], t + 1)
        act.activation(o.dec, o.dec, ACT.Exp).then_inc(s["d_dec"], 1)
        act.wait_ge(s["d_tr"], 3 * t + 1)
        for g in range(2):
            act.activation(o.Q[:, 4 * g:4 * g + 4, :], heads4(m.ps[4 + g]), ACT.Copy).then_inc(s["d_Qa"], 1)
        act.wait_ge(s["d_ms"], t + 1)
        act.activation(v["sd"], v["ss"], ACT.Sqrt).then_inc(s["d_sd"], 1)
        for i, (out, bank) in enumerate(((o.knT, 4), (o.qnT, 0))):
            act.wait_ge(s["d_tr2"], 3 * t + 1 + 2 * i)
            for g in range(2):
                last = act.activation(out[:, 4 * g:4 * g + 4, :], heads4(m.ps[bank + g]), ACT.Copy)
            last.then_inc(s["d_tr2a"], 1)
        for g in range(2):
            act.wait_ge(s["d_T0p"], 2 * t + g + 1)
            act.activation(o.T[:, 4 * g:4 * g + 4, :], heads4(m.ps[g]), ACT.Copy).then_inc(s["d_T0a"], 1)
        for k in range(1, NLEV):
            n = 2 * ((NLEV - 1) * t + k - 1)
            for g in range(2):
                act.wait_ge(s["d_Y"], n + g + 1)
                act.activation(o.Y[:, 4 * g:4 * g + 4, :], heads4(m.ps[g]), ACT.Copy).then_inc(s["d_Yc"], 1)
            if t == 1 and k == 3:
                odd_norm_act(act, m, o, 0)
        act.wait_ge(s["d_U"], t + 1)
        for g in range(2):
            last = act.activation(o.U[:, 4 * g:4 * g + 4, :], heads4(m.ps[g]), ACT.Copy)
        last.then_inc(s["d_Ua"], 1)
        if t == 1:
            act.wait_ge(s["d_W"], 1)
            for g in range(2):
                last = act.activation(o.WT[:, 4 * g:4 * g + 4, :], heads4(m.ps[6 + g]), ACT.Copy)
            last.then_inc(s["d_Wa"], 1)
        act.wait_ge(s["d_O"], t + 1)
        for g in range(2):
            last = act.activation(o.o[:, t, 4 * g:4 * g + 4, :], heads4(m.ps[2 + g]), ACT.Copy)
        last.then_inc(s["d_oev"], 1)
        if t == 0:
            act.wait_ge(s["d_S"], 1)
            for g in range(2):
                last = act.activation(o.S[:, 4 * g:4 * g + 4, :], heads4(m.ps[4 + g]), ACT.Copy)
            last.then_inc(s["d_Sa"], 1)
    odd_norm_act(act, m, o, 1)
    for t in range(NT):
        act.wait_ge(s["d_otr"], t + 1)
        act.activation(o.yT[:, 0:4, t * P:(t + 1) * P], heads4(m.ps[4 * (1 - t)]), ACT.Copy).then_inc(s["d_ota"], 1)


def odd_dve(dve, m):
    s, o, c = m.sig, odd_mem(m), m.c
    v = o.v

    def th(name, t):
        return v[name][:, t * GH:(t + 1) * GH]

    dve.wait_ge(s["d_ab"], 1)
    dve.tensor_copy(o.ab, m.ps[0][:, 0:32])
    dve.drain()
    ab = o.ab.rearrange("p (t n) -> p t n", t=NT)
    dve.tensor_tensor(v["x"].rearrange("p (t h) -> p t h", t=NT), ab[:, :, 0:GH],
                      m.s["dt_bias"].rearrange("p (t h) -> p t h", t=NT), ALU.add)
    dve.drain()
    softplus_head(dve, v["x"], v["neg"], v["mag"]).then_inc(s["d_gabs"], 1)
    dve.wait_ge(s["d_gexp"], 1)
    softplus_tail(dve, v["x"], v["ex"], v["z"], v["z2"], v["p"], v["sp"])
    dve.tensor_scalar(v["eb"], v["eb"], 1.0, None, ALU.add)
    dve.drain()
    dve.reciprocal(v["beta"], v["eb"])
    dve.scalar_tensor_tensor(v["g"], v["ea"], -1.0, v["sp"], ALU.mult, ALU.mult).then_inc(s["d_g"], 1)
    for b in range(6):
        block_used(dve, m, B_ODD + b)
        raw = [m.ps[2 + 2 * (b % 2) + j // 2][:, (j % 2) * SEQ:(j % 2 + 1) * SEQ] for j in range(4)]
        w = [m.s["oconv_w"][:, (4 * b + j) * CONV:(4 * b + j + 1) * CONV] for j in range(4)]
        for j in range(4):
            dve.tensor_scalar(o.qkvT[:, 4 * b + j, :], raw[j], w[j][:, CONV - 1:CONV], None, ALU.mult)
        for lag in range(1, CONV):
            dve.drain()
            for j in range(4):
                x = o.qkvT[:, 4 * b + j, lag:SEQ]
                dve.scalar_tensor_tensor(x, raw[j][:, 0:SEQ - lag], w[j][:, CONV - 1 - lag:CONV - lag], x,
                                         ALU.mult, ALU.add)
        dve.drain().then_inc(s["d_conv"], 1)
        if b == 3:
            dve.wait_ge(s["d_G"], 1)
            dve.tensor_copy(o.G, m.ps[1][:, 0:32])
            dve.drain()
            dve.tensor_tensor(o.G[:, 16:32], o.G[:, 16:32], o.G[:, 0:16], ALU.subtract).then_inc(s["d_Gs"], 1)
            dve.tensor_copy(o.gb, bc(th("g", 0), 2, P)).then_inc(s["d_gb"], 1)
    for t in range(NT):
        dve.wait_ge(s["d_Gb"], t + 1)
        for g in range(2):
            dve.tensor_tensor(o.dec[:, 4 * g:4 * g + 4, :], heads4(m.ps[2 + g]),
                              bc(o.G[:, t * GH + 4 * g:t * GH + 4 * g + 4], 2, P), ALU.subtract)
        dve.drain()
        dve.tensor_tensor(o.dec, o.dec, bc(c["future"], 1, GH), ALU.add).then_inc(s["d_diff"], 1)
        dve.wait_ge(s["d_tr"], 3 * t + 2)
        for g in range(2):
            dve.tensor_copy(o.K[:, 4 * g:4 * g + 4, :], heads4(m.ps[6 + g]))
        dve.drain()
        dve.tensor_tensor(o.BK, o.K, o.K, ALU.mult)
        dve.wait_ge(s["d_Qa"], 2 * t + 2)
        dve.tensor_tensor(o.QD, o.Q, o.Q, ALU.mult)
        dve.drain()
        dve.tensor_reduce(v["ss"][:, GH:16], o.BK, AX.X, ALU.add)
        dve.tensor_reduce(v["ss"][:, 0:GH], o.QD, AX.X, ALU.add)
        dve.drain()
        dve.tensor_scalar(v["ss"], v["ss"], EPS, None, ALU.add).then_inc(s["d_ms"], 1)
        dve.wait_ge(s["d_tr"], 3 * t + 3)
        for g in range(2):
            dve.tensor_tensor(o.BV[:, 4 * g:4 * g + 4, :], heads4(m.ps[g]), bc(th("beta", t)[:, 4 * g:4 * g + 4], 2, P),
                              ALU.mult)
        dve.wait_ge(s["d_sd"], t + 1)
        dve.reciprocal(v["r"], v["sd"])
        dve.drain()
        dve.tensor_scalar(v["r"][:, 0:GH], v["r"][:, 0:GH], P ** -0.5, None, ALU.mult)
        dve.tensor_tensor(o.K, o.K, bc(v["r"][:, GH:16], 2, P), ALU.mult)
        dve.drain()
        dve.tensor_tensor(o.Q, o.Q, bc(v["r"][:, 0:GH], 2, P), ALU.mult)
        dve.tensor_tensor(o.BK, o.K, bc(th("beta", t), 2, P), ALU.mult)
        dve.drain().then_inc(s["d_tok"], 1)
        dve.wait_ge(s["d_tr2"], 3 * t + 2)
        for g in range(2):
            last = dve.tensor_copy(o.bkT[:, 4 * g:4 * g + 4, :], heads4(m.ps[6 + g]))
        if t == 1:
            dve.wait_ge(s["d_tr2"], 7)
            for g in range(2):
                last = dve.tensor_copy(o.qdT[:, 4 * g:4 * g + 4, :], heads4(m.ps[2 + g]))
        last.then_inc(s["d_tr2d"], 1)
        dve.wait_ge(s["d_dec"], t + 1)
        for i, (out, bank) in enumerate(((o.LT, 4), (o.AT, 6))):
            dve.wait_ge(s["d_kk"], 2 * t + i + 1)
            if t == 1 and i == 0:
                dve.wait_ge(s["d_pool"], 2)
            for g in range(2):
                last = dve.tensor_tensor(out[:, 4 * g:4 * g + 4, :], heads4(m.ps[bank + g]),
                                         o.dec[:, 4 * g:4 * g + 4, :], ALU.mult)
            if i == 0:
                last.then_inc(s["d_LT"], 1)
        dve.drain()
        dve.tensor_tensor(o.TT, o.LT, bc(c["level"][:, 0:P], 1, GH), ALU.mult)
        dve.drain()
        dve.tensor_tensor(o.TT, bc(c["ident"], 1, GH), o.TT, ALU.subtract).then_inc(s["d_T0"], 1)
        for k in range(1, NLEV):
            n = 2 * ((NLEV - 1) * t + k - 1)
            for g in range(2):
                dve.wait_ge(s["d_Z"], n + g + 1)
                hs = slice(4 * g, 4 * g + 4)
                if k < NLEV - 1:
                    dve.tensor_tensor(o.T[:, hs, :], o.T[:, hs, :], heads4(m.ps[2 + g]), ALU.subtract)
                dve.tensor_tensor(o.TT[:, hs, :], o.TT[:, hs, :], heads4(m.ps[4 + g]), ALU.subtract)
                dve.drain().then_inc(s["d_Zd"], 1)
            if t == 1 and k == 3:
                odd_norm_dve(dve, m, o, 0)
        if t == 0:
            dve.wait_ge(s["d_U"], 1)
            dve.tensor_copy(o.gb, bc(th("g", 1), 2, P)).then_inc(s["d_gb"], 1)
            dve.wait_ge(s["d_Ua"], 1)
        else:
            dve.wait_ge(s["d_WS"], 1)
            dve.wait_ge(s["d_Ua"], 2)
            for g in range(2):
                hs = slice(4 * g, 4 * g + 4)
                last = dve.tensor_tensor(o.U[:, hs, :], o.U[:, hs, :], heads4(m.ps[4 + g]), ALU.subtract)
            last.then_inc(s["d_VN"], 1)
    odd_norm_dve(dve, m, o, 1)
    for t in range(NT):
        dve.wait_ge(s["d_otr"], t + 1)
        dve.tensor_copy(o.yT[:, 4:8, t * P:(t + 1) * P], heads4(m.ps[4 * (1 - t) + 1])).then_inc(s["d_otd"], 1)
    out_dve(dve, m, B_ODD + 8, 1)


def odd_norm_dve(dve, m, o, t):
    s, x = m.sig, o.o[:, t]
    th = slice(t * GH, (t + 1) * GH)
    dve.wait_ge(s["d_oev"], t + 1)
    dve.tensor_tensor(o.K, x, x, ALU.mult)
    dve.drain()
    dve.tensor_reduce(o.v["oss"][:, th], o.K, AX.X, ALU.add)
    dve.drain()
    dve.tensor_scalar(o.v["oss"][:, th], o.v["oss"][:, th], 1.0 / P, EPS, ALU.mult, ALU.add).then_inc(s["d_oss"], 1)
    dve.tensor_tensor(x, x, bc(m.s["out_gain"], 1, GH), ALU.mult)
    dve.drain()
    dve.tensor_tensor(x, x, o.sg[:, t, :].rearrange("p (h e) -> p h e", h=GH), ALU.mult)
    dve.wait_ge(s["d_osd"], t + 1)
    dve.reciprocal(o.v["orr"][:, th], o.v["osd"][:, th])
    dve.drain()
    dve.tensor_tensor(x, x, bc(o.v["orr"][:, th], 2, P), ALU.mult).then_inc(s["d_on"], 1)



STEPS = 2 * NE + 1


PAIRS = 3 * NC
PE_AHEAD = 3


def moe_pair(kind, c):
    def place_of(c):
        if kind == "down":
            return PAIRS - 1 if isinstance(c, int) and c == NC - 1 else 3 * c + 4
        if isinstance(c, int) and c == 0:
            return 0 if kind == "gate" else 1
        return 3 * c - 1 if kind == "gate" else 3 * c

    first = 2 * place_of(c if isinstance(c, int) else 1) % 3
    return place_of(c), (first, (first + 1) % 3)


def moe_done(q, kind, c):
    return 2 * (q * PAIRS + moe_pair(kind, c)[0]) + 2 + PE_AHEAD


def moe_mem(m):
    r = Place()
    flat = lambda t: t.rearrange("p k t -> p (k t)")
    r.xgh, r.xgl = (flat(t)[:, 0:KT * P].rearrange("p (k t) -> p k t", k=KT) for t in (m.xh, m.xl))
    free_1, free_2 = 6 * PIECE + KT * P, 6 * PIECE + KT * SEQ + KT * P
    r.y = m.scr(free_1, D)
    r.oh = m.scr(free_2, NT, P)
    r.ohg = m.scr(free_2 + 256, NT, P)
    r.ohT = m.scr(free_2 + 512, SEQ)
    r.silu, r.h = flat(m.xT)[:, 0:FC], flat(m.xT)[:, FC:2 * FC]
    r.hh, r.hl = (t[:, :].rearrange("p (j t) -> p j t", j=FC // P) for t in (m.hh, m.hl))
    r.wg, r.wu = (m.mslot[i].rearrange("p (k n) -> p k n", k=KT) for i in range(2))
    r.wd = [m.mslot[2 + i].rearrange("p (k n) -> p k n", k=FC // P) for i in range(2)]
    at = [0]

    def tiny(n):
        at[0] += n
        return m.tiny(at[0] - n, n)

    te = lambda ap: ap.rearrange("p (t e) -> p t e", t=NT)
    r.lg, r.eq, r.sel1, r.sel2, r.sel, r.lg2, r.gate, r.rk1 = (te(tiny(NT * NE)) for _ in range(8))
    r.m1, r.m2, r.best, r.ex, r.w1, r.w2 = (tiny(NT) for _ in range(6))
    r.most, r.over = tiny(1), tiny(1)
    r.rank = te(tiny(NT * STEPS))
    r.gates = te(tiny(NT * STEPS))
    return r


def moe_load(sp, m):
    s, r, w = m.sig, moe_mem(m), m.w
    wg = w["o_moe_w_gate"][0].rearrange("e (k p) f -> e p k f", p=P)
    wu = w["o_moe_w_up"][0].rearrange("e (k p) f -> e p k f", p=P)
    wd = w["o_moe_w_down"][0].rearrange("e (k p) n -> e p k n", p=P)

    def free(q, pair):
        sp.wait_ge(s["r_lo"], 2 * (q * PAIRS + pair) + 2)

    def gate(e, c):
        sp.dma_start(r.wg, wg[bass.ds(e, 1), :, :, bass.ds(c * FC, FC)].rearrange("e p k f -> p (e k) f")).then_inc(s["r_gin"], 16)

    def up(e, c):
        sp.dma_start(r.wu, wu[bass.ds(e, 1), :, :, bass.ds(c * FC, FC)].rearrange("e p k f -> p (e k) f")).then_inc(s["r_uin"], 16)

    def down(e, c, slot):
        sp.dma_start(r.wd[slot], wd[bass.ds(e, 1), :, bass.ds(c * (FC // P), FC // P), :]
                     .rearrange("e p k n -> p (e k) n")).then_inc(s[f"r_din{slot}"], 16)

    def gate_up(q, e, c):
        free(q, 3 * (c - 1) - 1 if not isinstance(c, int) or c > 1 else 0)
        gate(e, c)
        free(q, 3 * (c - 1) if not isinstance(c, int) or c > 1 else 1)
        up(e, c)

    def later(q, e, c, slot):
        gate_up(q, e, c)
        free(q, 3 * (c - 2) + 4)
        down(e, c, slot)

    def rest(q, e):
        gate_up(q, e, 1)
        with sp.Fori(1, 3) as j:
            later(q, e, 2 * j, 0)
            later(q, e, 2 * j + 1, 1)
        later(q, e, NC - 1, 0)

    def first(before, e):
        free(before, 3 * (NC - 1) - 1)
        gate(e, 0)
        free(before, 3 * (NC - 1))
        up(e, 0)
        free(before, PAIRS - 1)
        down(e, 0, 0)
        down(e, 1, 1)

    for i, load in enumerate((lambda: gate(0, 0), lambda: up(0, 0), lambda: down(0, 0, 0), lambda: down(0, 1, 1))):
        block_used(sp, m, B_SECOND - 4 + i)
        load()
    sp.wait_ge(s["r_q"], 1)
    rounds = sp.value_load(m.q_int[0:1, 1:2], min_val=1, max_val=2)
    with sp.Fori(1, rounds + 1) as n:
        with sp.Fori(0, NE - 1) as e:
            q = (n - 1) * NE + e
            rest(q, e)
            first(q, e + 1)
        rest(n * NE - 1, NE - 1)
        first(n * NE - 1, 0)
    sp.wait_ge(s["r_uin"], 16 * (rounds * (NE * NC) + 1))
    sp.wait_ge(s["r_din0"], 16 * (rounds * (NE * 4) + 1))
    sp.wait_ge(s["r_din1"], 16 * (rounds * (NE * 3) + 1))


def moe_steps(eng, m):
    eng.wait_ge(m.sig["r_q"], 1)
    return eng.value_load(m.q_int[0:1, 0:1], min_val=NE, max_val=2 * NE)


def moe_pe(pe, m):
    s, r, c = m.sig, moe_mem(m), m.c
    router = m.s["router"].rearrange("p (k e) -> p k e", k=KT)
    for t in range(NT):
        for k in range(KT):
            last = pe.matmul(m.ps[0][:, t * NE:(t + 1) * NE], m.xT[:, k, t * P:(t + 1) * P], router[:, k, :],
                             start=(k == 0), stop=(k == KT - 1))
    last.then_inc(s["r_lg"], 1)
    pe.wait_ge(s["r_sel"], 1)
    pe.matmul(m.ps[1][:, 0:NE], c["before"], r.sel[:, 0, :], start=True, stop=True)
    pe.matmul(m.ps[1][:, NE:2 * NE], c["ones"], r.sel[:, 0, :], start=True, stop=False)
    pe.matmul(m.ps[1][:, NE:2 * NE], c["before"], r.sel[:, 1, :], start=False, stop=True)
    pe.matmul(m.ps[1][:, 16:24], c["ones"], r.sel[:, 0, :], start=True, stop=False)
    pe.matmul(m.ps[1][:, 16:24], c["ones"], r.sel[:, 1, :], start=False, stop=True).then_inc(s["r_rank"], 1)
    pe.drain().then_inc(s["r_used"], PE_AHEAD)
    steps = moe_steps(pe, m)

    def gather(n):
        pe.wait_ge(s["r_oh"], n + 1)
        for k in range(KT):
            for t in range(NT):
                last = pe.matmul(m.ps[k // 4][:, (k % 4) * P:(k % 4 + 1) * P], m.xn[:, t, k * P:(k + 1) * P],
                                 r.oh[:, t, :], start=(t == 0), stop=(t == NT - 1))
        last.then_inc(s["r_gath"], 1)

    def pieces(q, kind, c, k, halves=(0, 1)):
        pair, places = moe_pair(kind, c)
        for half in halves:
            n = 2 * (q * PAIRS + pair) + half
            pe.wait_ge(s["r_lo"], n + 1)
            yield half, [t[places[half]][:, :].rearrange("p (k n) -> p k n", k=k) for t in (m.whi, m.wlo)]

    def inner(q, bank, kind, c, halves=(0, 1)):
        for half, (hi, lo) in pieces(q, kind, c, KT // 2, halves):
            for j in range(KT // 2):
                k = half * KT // 2 + j
                last = split_product(pe, m.ps[bank][:, :], (r.xgh[:, k, :], r.xgl[:, k, :]),
                                     (hi[:, j, :], lo[:, j, :]), start=(k == 0), stop=(k == KT - 1))
            last.then_inc(s["r_used"], 1)

    def turn(i):
        pe.wait_ge(s["r_h"], i + 2)
        for j in range(FC // P):
            last = pe.transpose(m.ps[2][:, j * P:(j + 1) * P], r.h[:, j * P:(j + 1) * P], c["ident"])
        last.then_inc(s["r_hT"], 1)

    def down(q, ch, first=False, final=False):
        pe.wait_ge(s["r_hTd"], q * NC + ch + 1)
        for half, (hi, lo) in pieces(q, "down", ch, FC // P // 2):
            for j in range(FC // P // 2):
                k = half * FC // P // 2 + j
                for side in range(2):
                    cols = slice(side * HALF, (side + 1) * HALF)
                    last = split_product(pe, m.ps[3 + side][:, :], (r.hh[:, k, :], r.hl[:, k, :]),
                                         (hi[:, j, cols], lo[:, j, cols]),
                                         start=first and k == 0, stop=final and k == FC // P - 1)
            last.then_inc(s["r_used"], 1)

    def chunk(q, ch, first=False):
        pe.wait_ge(s["r_silu"], q * NC + ch)
        inner(q, 0, "gate", ch)
        turn(q * NC + ch - 1)
        inner(q, 1, "up", ch)
        down(q, ch - 1, first=first)

    def bring_back():
        for t in range(NT):
            for half in range(2):
                pe.matmul(m.ps[(5, 6, 7, 2)[2 * t + half]][:, :], r.ohT[:, t * P:(t + 1) * P],
                          r.y[:, half * HALF:(half + 1) * HALF], start=True, stop=True).then_inc(s["r_scat"], 1)

    gather(0)
    pe.wait_ge(s["r_xgd"], 1)
    inner(0, 0, "gate", 0)
    with pe.Fori(0, steps) as q:
        inner(q, 1, "up", 0)
        pe.wait_ge(s["r_add"], q + 1)
        for t in range(NT):
            last = pe.transpose(m.ps[7][:, t * P:(t + 1) * P], r.ohg[:, t, :], c["ident"])
        last.then_inc(s["r_ohT"], 1)
        chunk(q, 1, first=True)
        with pe.Fori(2, NC) as ch:
            chunk(q, ch)
        pe.wait_ge(s["r_silu"], q * NC + NC)
        turn(q * NC + NC - 1)
        gather(q + 1)
        down(q, NC - 1, final=True)
        pe.wait_ge(s["r_xgd"], q + 2)
        inner(q + 1, 0, "gate", 0, halves=(0,))
        pe.wait_ge(s["r_ohTa"], q + 1)
        pe.wait_ge(s["r_ya"], q + 1)
        pe.wait_ge(s["r_yd"], q + 1)
        bring_back()
        inner(q + 1, 0, "gate", 0, halves=(1,))
    pe.drain().then_inc(s["r_end"], 1)


def moe_act(act, m):
    s, r = m.sig, moe_mem(m)
    act.wait_ge(s["r_e"], 1)
    act.activation(r.ex, r.ex, ACT.Exp).then_inc(s["r_ed"], 1)
    steps = moe_steps(act, m)

    def gathered(n):
        act.wait_ge(s["r_gath"], n + 1)
        for k in range(KT):
            last = act.activation(r.xgh[:, k, :], m.ps[k // 4][:, (k % 4) * P:(k % 4 + 1) * P], ACT.Copy,
                                  scale=m.s["g3"][:, k:k + 1])
            if k % 4 == 3:
                last.then_inc(s["r_xga"], 1)

    def hi(q, kind, c, raw, arrived, chunks, halves=(0, 1)):
        pair, places = moe_pair(kind, c)
        act.wait_ge(s[arrived], chunks * 16)
        for half in halves:
            act.wait_ge(s["r_used"], 2 * (q * PAIRS + pair) + half - 2 + PE_AHEAD)
            act.activation(m.whi[places[half]][:, :], raw[:, half * PIECE:(half + 1) * PIECE],
                           ACT.Copy).then_inc(s["r_hi"], 1)

    def gate(q, c, halves=(0, 1)):
        hi(q, "gate", c, m.mslot[0], "r_gin", q * NC + c + 1, halves)

    def up(q, c):
        hi(q, "up", c, m.mslot[1], "r_uin", q * NC + c + 1)

    def silu(q, c):
        act.wait_ge(s["r_used"], moe_done(q, "gate", c))
        act.wait_ge(s["r_h"], q * NC + c + 1)
        act.activation(r.silu, m.ps[0][:, :], ACT.Silu).then_inc(s["r_silu"], 1)

    def chunk(q, c, slot, chunks):
        gate(q, c)
        up(q, c)
        silu(q, c)
        hi(q, "down", c - 1, m.mslot[2 + slot], f"r_din{slot}", chunks)

    gathered(0)
    gate(0, 0)
    with act.Fori(0, steps) as q:
        up(q, 0)
        silu(q, 0)
        gate(q, 1)
        act.wait_ge(s["r_ohT"], q + 1)
        act.activation(r.ohT, m.ps[7][:, 0:SEQ], ACT.Copy).then_inc(s["r_ohTa"], 1)
        up(q, 1)
        silu(q, 1)
        hi(q, "down", 0, m.mslot[2], "r_din0", q * 4 + 1)
        chunk(q, 2, 1, q * 3 + 1)
        with act.Fori(1, 3) as j:
            chunk(q, 2 * j + 1, 0, q * 4 + j + 1)
            chunk(q, 2 * j + 2, 1, q * 3 + j + 1)
        hi(q, "down", NC - 1, m.mslot[2], "r_din0", q * 4 + 4)
        gate(q + 1, 0, halves=(0,))
        gathered(q + 1)
        gate(q + 1, 0, halves=(1,))
        act.wait_ge(s["r_used"], moe_done(q, "down", NC - 1))
        act.activation(r.y[:, 0:HALF], m.ps[3][:, :], ACT.Copy).then_inc(s["r_ya"], 1)
    act.wait_ge(s["r_end"], 1)


def moe_dve(dve, m):
    s, r, c = m.sig, moe_mem(m), m.c
    dve.wait_ge(s["r_lg"], 1)
    dve.tensor_copy(r.lg, m.ps[0][:, 0:NT * NE].rearrange("p (t e) -> p t e", t=NT))
    dve.drain()

    def first_best(x, best, sel):
        dve.tensor_reduce(best, x, AX.X, ALU.max)
        dve.drain()
        dve.tensor_tensor(r.eq, x, bc(best, 2, NE), ALU.is_equal)
        dve.drain()
        dve.tensor_tensor(r.eq, r.eq, bc(c["eight"], 1, NT), ALU.mult)
        dve.drain()
        dve.tensor_reduce(r.best, r.eq, AX.X, ALU.max)
        dve.drain()
        dve.tensor_tensor(sel, r.eq, bc(r.best, 2, NE), ALU.is_equal)
        dve.drain()

    first_best(r.lg, r.m1, r.sel1)
    dve.scalar_tensor_tensor(r.lg2, r.sel1, NEG, r.lg, ALU.mult, ALU.add)
    dve.drain()
    first_best(r.lg2, r.m2, r.sel2)
    dve.tensor_tensor(r.sel, r.sel1, r.sel2, ALU.add).then_inc(s["r_sel"], 1)
    dve.tensor_tensor(r.ex, r.m2, r.m1, ALU.subtract).then_inc(s["r_e"], 1)
    dve.wait_ge(s["r_ed"], 1)
    dve.tensor_scalar(r.w2, r.ex, 1.0, None, ALU.add)
    dve.drain()
    dve.reciprocal(r.w1, r.w2)
    dve.drain()
    dve.tensor_tensor(r.w2, r.ex, r.w1, ALU.mult)
    dve.tensor_tensor(r.sel1, r.sel1, bc(r.w1, 2, NE), ALU.mult)
    dve.drain()
    dve.tensor_tensor(r.sel2, r.sel2, bc(r.w2, 2, NE), ALU.mult)
    dve.drain()
    dve.tensor_tensor(r.gate, r.sel1, r.sel2, ALU.add)
    dve.wait_ge(s["r_rank"], 1)
    dve.scalar_tensor_tensor(r.rk1, m.ps[1][:, 0:NT * NE].rearrange("p (t e) -> p t e", t=NT), 1.0, r.sel,
                             ALU.add, ALU.mult)
    dve.tensor_reduce(r.most, m.ps[1][:, 16:24], AX.X, ALU.max)
    dve.drain()
    for n in range(2):
        cols = slice(n * NE, (n + 1) * NE)
        dve.tensor_scalar(r.rank[:, :, cols], r.rk1, -1.0 - n * P, None, ALU.add)
        dve.tensor_copy(r.gates[:, :, cols], r.gate)
    dve.memset(r.rank[:, :, STEPS - 1:STEPS], -1.0)
    dve.memset(r.gates[:, :, STEPS - 1:STEPS], 0.0)
    dve.tensor_scalar(r.over, r.most, float(P), None, ALU.is_gt)
    dve.drain()
    dve.tensor_scalar(m.q_int[:, 0:1], r.over, float(NE), float(NE), ALU.mult, ALU.add)
    dve.tensor_scalar(m.q_int[:, 1:2], r.over, 1.0, None, ALU.add)
    dve.drain().then_inc(s["r_q"], 1)
    dve.drain().then_inc(s["r_h"], 1)
    dve.drain().then_inc(s["r_add"], 1)

    def one_hot(n):
        for t in range(NT):
            rank, gate = r.rank[:, t, bass.ds(n, 1)], r.gates[:, t, bass.ds(n, 1)]
            dve.tensor_scalar(r.oh[:, t, :], c["iota"], rank, None, ALU.is_equal)
            dve.tensor_scalar(r.ohg[:, t, :], c["iota"], rank, gate, ALU.is_equal, ALU.mult)
        dve.drain().then_inc(s["r_oh"], 1)

    def gathered(n):
        for k in range(KT):
            dve.wait_ge(s["r_xga"], 2 * n + k // 4 + 1)
            last = dve.scalar_tensor_tensor(r.xgl[:, k, :], m.ps[k // 4][:, (k % 4) * P:(k % 4 + 1) * P],
                                            m.s["g3"][:, k:k + 1], r.xgh[:, k, :], ALU.mult, ALU.subtract)
        last.then_inc(s["r_xgd"], 1)

    def lo(q, kind, c, raw, halves=(0, 1)):
        pair, places = moe_pair(kind, c)
        for half in halves:
            dve.wait_ge(s["r_hi"], 2 * (q * PAIRS + pair) + half + 1)
            dve.tensor_tensor(m.wlo[places[half]][:, :], raw[:, half * PIECE:(half + 1) * PIECE],
                              m.whi[places[half]][:, :], ALU.subtract).then_inc(s["r_lo"], 1)

    def hidden(q, c):
        dve.wait_ge(s["r_used"], moe_done(q, "up", c))
        dve.wait_ge(s["r_silu"], q * NC + c + 1)
        dve.tensor_tensor(r.h, r.silu, m.ps[1][:, :], ALU.mult).then_inc(s["r_h"], 1)

    def turned(i):
        dve.wait_ge(s["r_hT"], i + 1)
        turned_h = m.ps[2][:, :].rearrange("p (j t) -> p j t", j=FC // P)
        dve.tensor_copy(r.hh, turned_h)
        dve.drain()
        dve.tensor_tensor(r.hl, turned_h, r.hh, ALU.subtract).then_inc(s["r_hTd"], 1)

    def chunk(q, c, slot):
        lo(q, "gate", c, m.mslot[0])
        lo(q, "up", c, m.mslot[1])
        turned(q * NC + c - 1)
        lo(q, "down", c - 1, m.mslot[2 + slot])
        hidden(q, c)

    steps = moe_steps(dve, m)
    one_hot(0)
    gathered(0)
    lo(0, "gate", 0, m.mslot[0])
    with dve.Fori(0, steps) as q:
        lo(q, "up", 0, m.mslot[1])
        hidden(q, 0)
        chunk(q, 1, 0)
        dve.wait_ge(s["r_ohT"], q + 1)
        one_hot(q + 1)
        chunk(q, 2, 1)
        with dve.Fori(1, 3) as j:
            chunk(q, 2 * j + 1, 0)
            chunk(q, 2 * j + 2, 1)
        lo(q, "down", NC - 1, m.mslot[2])
        turned(q * NC + NC - 1)
        lo(q + 1, "gate", 0, m.mslot[0], halves=(0,))
        gathered(q + 1)
        lo(q + 1, "gate", 0, m.mslot[0], halves=(1,))
        dve.wait_ge(s["r_used"], moe_done(q, "down", NC - 1))
        dve.tensor_copy(r.y[:, HALF:D], m.ps[4][:, :]).then_inc(s["r_yd"], 1)
        for t in range(NT):
            for half in range(2):
                dve.wait_ge(s["r_scat"], q * 4 + 2 * t + half + 1)
                x = m.res[:, t, half * HALF:(half + 1) * HALF]
                last = dve.tensor_tensor(x, x, m.ps[(5, 6, 7, 2)[2 * t + half]][:, :], ALU.add)
        last.then_inc(s["r_add"], 1)
    dve.drain().then_inc(s["res_ready"], 1)



PAD_A, PAD_C = TAPS_A - 1, TAPS_C - 1


def second_mem(m):
    c = Place()
    c.apad = m.scr(0, AT, PAD_A + SEQ)
    c.sg = m.scr(896, AT, SEQ)
    c.acc = m.scr(1664, AT, SEQ)
    c.g = m.scr(2432, NT, 2 * DB)
    c.ccs, c.cxs, c.cbs = (m.scr(3456 + i * 768, AT, SEQ) for i in range(3))
    c.zpad = m.scr(5760, AT, PAD_C + SEQ)
    c.zt, c.zacc = m.scr(6544, AT, SEQ), m.scr(7312, AT, SEQ)
    c.xh = m.scr(8080, NT, DA)
    c.v = m.scr(8848, NT, DB)
    c.y = m.scr(9360, NT, DB)
    c.ws = m.scr(9872, HB, P)
    c.mixT = m.scr(10384, KT, SEQ)
    c.st = [m.tiny(6 * i, 6) for i in range(4)]
    c.mv = [m.tiny(24 + 2 * i, 2) for i in range(4)]
    c.var, c.sd, c.r = m.tiny(32, 4), m.tiny(36, 4), m.tiny(40, 4)
    return c


def two_banks(m, bank, x, i):
    if i == 0:
        return m.ps[bank][:, :].rearrange("p (a t) -> p a t", a=2), x[:, 0:2, :]
    return m.ps[bank + 1][:, 0:SEQ], x[:, 2, :]


def second_pe(pe, m, l):
    s, c, base = m.sig, second_mem(m), B_SECOND + 8 * l

    def project(j, bank):
        block_in(pe, m, base + j)
        for a in range(AT):
            for k in range(KT):
                last = pe.matmul(m.ps[bank + a // 2][:, (a % 2) * SEQ:(a % 2 + 1) * SEQ],
                                 mblock(m, base + j)[:, k, a * P:(a + 1) * P], m.xT[:, k, :],
                                 start=(k == 0), stop=(k == KT - 1))
        last.then_inc(s[f"m_used{j % 4}"], 1)

    project(0, 0)
    project(1, 2)
    project(2, 6)
    block_in(pe, m, base + 3)
    for t in range(NT):
        for k in range(KT):
            last = pe.matmul(m.ps[4 + t][:, :], m.xT[:, k, t * P:(t + 1) * P], mblock(m, base + 3)[:, k, :],
                             start=(k == 0), stop=(k == KT - 1))
    last.then_inc(s["m_used3"], 1)
    pe.wait_ge(s["c_apad"], l + 1)
    project(4, 0)
    pe.wait_ge(s["c_vl"], l + 1)
    for t in range(NT):
        for h in range(HB):
            at = t * DB + h * 64
            last = pe.matmul(m.ps[4][:, at:at + 64], c.ws[:, h, :], c.v[:, t, h * 64:(h + 1) * 64],
                             start=True, stop=True)
    last.then_inc(s["c_s"], 1)
    pe.wait_ge(s["c_conv"], l + 1)
    for t in range(NT):
        for a in range(AT):
            last = pe.transpose(m.ps[2 + t][:, a * P:(a + 1) * P], c.acc[:, a, t * P:(t + 1) * P], m.c["ident"])
        last.then_inc(s["c_tr"], 1)
    pe.wait_ge(s["c_cev"], 3 * l + 1)
    project(5, 6)
    pe.wait_ge(s["c_yb"], l + 1)
    for j in range(DB // P):
        for t in range(NT):
            at = j * SEQ + t * P
            last = pe.transpose(m.ps[5][:, at:at + P], c.y[:, t, j * P:(j + 1) * P], m.c["ident"])
    last.then_inc(s["c_ytr"], 1)
    pe.wait_ge(s["c_cev"], 3 * l + 2)
    for t in range(NT):
        pe.wait_ge(s["c_xh"], 2 * l + t + 1)
        for a in range(AT):
            last = pe.transpose(m.ps[t][:, a * P:(a + 1) * P], c.xh[:, t, a * P:(a + 1) * P], m.c["ident"])
        last.then_inc(s["c_tr2"], 1)
    pe.wait_ge(s["c_ya"], l + 1)
    pe.wait_ge(s["c_ybT"], l + 1)
    pe.wait_ge(s["c_yc"], l + 1)
    out_pe(pe, m, base + 6, c.mixT)


def second_act(act, m, l):
    s, c, base, p = m.sig, second_mem(m), B_SECOND + 8 * l, m.s2[l]
    block_used(act, m, base + 1)
    for i in range(2):
        src, dst = two_banks(m, 2, c.sg, i)
        last = act.activation(dst, src, ACT.Sigmoid)
    last.then_inc(s["c_sg"], 1)

    def out(j, bank, dst):
        block_used(act, m, base + j)
        for i in range(2):
            src, part = two_banks(m, bank, dst, i)
            last = act.activation(part, src, ACT.Copy)
        last.then_inc(s["c_cev"], 1)

    out(2, 6, c.ccs)
    block_used(act, m, base + 3)
    for t in range(NT):
        last = act.activation(c.g[:, t, :], m.ps[4 + t][:, :], ACT.Gelu_apprx_tanh)
    last.then_inc(s["c_gb"], 1)
    act.wait_ge(s["c_ms"], 2 * l + 1)
    act.activation(c.sd[:, 0:2], c.var[:, 0:2], ACT.Sqrt).then_inc(s["c_sd"], 1)
    out(4, 0, c.cxs)
    act.wait_ge(s["c_ms"], 2 * l + 2)
    act.activation(c.sd[:, 2:4], c.var[:, 2:4], ACT.Sqrt).then_inc(s["c_sd"], 1)
    out(5, 6, c.cbs)
    act.wait_ge(s["c_ytr"], l + 1)
    act.activation(c.mixT[:, AT:AT + 2, :], m.ps[5][:, :].rearrange("p (j t) -> p j t", j=2),
                   ACT.Copy).then_inc(s["c_ybT"], 1)
    for t in range(NT):
        act.wait_ge(s["c_tr2"], 2 * l + t + 1)
        for a in range(AT):
            last = act.activation(c.mixT[:, a, t * P:(t + 1) * P], m.ps[t][:, a * P:(a + 1) * P], ACT.Silu,
                                  scale=p["ln_a_g"][:, a:a + 1], bias=p["ln_a_b"][:, a:a + 1])
    last.then_inc(s["c_ya"], 1)


def second_dve(dve, m, l):
    s, c, base, p = m.sig, second_mem(m), B_SECOND + 8 * l, m.s2[l]
    dve.memset(c.apad[:, :, 0:PAD_A], 0.0)
    dve.tensor_tensor(c.ws, p["w_s"].rearrange("p (h t) -> p h t", h=HB), bc(m.c["upto"], 1, HB), ALU.mult)
    block_used(dve, m, base)
    dve.wait_ge(s["c_sg"], l + 1)
    for i in range(2):
        src, sg = two_banks(m, 0, c.sg, i)
        dst = c.apad[:, 0:2, PAD_A:] if i == 0 else c.apad[:, 2, PAD_A:]
        dve.tensor_tensor(dst, src, sg, ALU.mult)
    dve.drain().then_inc(s["c_apad"], 1)
    for i in range(TAPS_A):
        second_tap(dve, c, p, i)
        if i == 20:
            second_gate_norm(dve, m, c, l, p)
        if i == 24:
            second_gate_scale(dve, m, c, l, p)
    dve.drain().then_inc(s["c_conv"], 1)
    dve.wait_ge(s["c_s"], l + 1)
    for t in range(NT):
        y = c.y[:, t, :].rearrange("p (h d) -> p h d", h=HB)
        dve.tensor_tensor(y, m.ps[4][:, t * DB:(t + 1) * DB].rearrange("p (h d) -> p h d", h=HB),
                          bc(p["b_s"], 2, 64), ALU.add)
    dve.drain()
    dve.tensor_tensor(c.y, c.y, c.g[:, :, 0:DB], ALU.mult).then_inc(s["c_yb"], 1)
    for t in range(NT):
        dve.wait_ge(s["c_tr"], 2 * l + t + 1)
        dve.bn_stats(c.st[2 + t], m.ps[2 + t][:, 0:DA])
        dve.drain()
        dve.bn_aggr(c.mv[2 + t], c.st[2 + t])
        dve.drain()
        dve.tensor_scalar(c.var[:, 2 + t:3 + t], c.mv[2 + t][:, 1:2], LN_EPS, None, ALU.add)
    dve.drain().then_inc(s["c_ms"], 1)
    dve.wait_ge(s["c_sd"], 2 * l + 2)
    dve.reciprocal(c.r[:, 2:4], c.sd[:, 2:4])
    dve.drain()
    for t in range(NT):
        dve.tensor_scalar(c.xh[:, t, :], m.ps[2 + t][:, 0:DA], c.mv[2 + t][:, 0:1], c.r[:, 2 + t:3 + t],
                          ALU.subtract, ALU.mult).then_inc(s["c_xh"], 1)
    out_dve(dve, m, base + 6, 2 + l)


def second_tap(eng, c, p, i):
    w = p["conv_a_w"].rearrange("p (a i) -> p a i", a=AT)
    for a in range(AT):
        x = c.apad[:, a, i:i + SEQ]
        if i == 0:
            eng.tensor_scalar(c.acc[:, a, :], x, w[:, a, 0:1], p["conv_a_b"][:, a:a + 1], ALU.mult, ALU.add)
        else:
            eng.scalar_tensor_tensor(c.acc[:, a, :], x, w[:, a, i:i + 1], c.acc[:, a, :], ALU.mult, ALU.add)
    eng.drain()


def second_gate_norm(dve, m, c, l, p):
    dve.wait_ge(m.sig["c_gb"], l + 1)
    for t in range(NT):
        dve.bn_stats(c.st[t], c.g[:, t, DB:2 * DB])
    dve.drain()
    for t in range(NT):
        dve.bn_aggr(c.mv[t], c.st[t])
    dve.drain()
    for t in range(NT):
        dve.tensor_scalar(c.var[:, t:t + 1], c.mv[t][:, 1:2], LN_EPS, None, ALU.add)
    dve.drain().then_inc(m.sig["c_ms"], 1)


def second_gate_scale(dve, m, c, l, p):
    dve.wait_ge(m.sig["c_sd"], 2 * l + 1)
    dve.reciprocal(c.r[:, 0:2], c.sd[:, 0:2])
    dve.drain()
    for t in range(NT):
        dve.tensor_scalar(c.v[:, t, :], c.g[:, t, DB:2 * DB], c.mv[t][:, 0:1], c.r[:, t:t + 1],
                          ALU.subtract, ALU.mult)
    dve.drain()
    dve.tensor_tensor(c.v, c.v, bc(p["ln_v_g"], 1, NT), ALU.mult)
    dve.drain()
    dve.tensor_tensor(c.v, c.v, bc(p["ln_v_b"], 1, NT), ALU.add).then_inc(m.sig["c_vl"], 1)


def second_pool(pool, m, l):
    s, c, p = m.sig, second_mem(m), m.s2[l]
    pool.wait_ge(s["c_cev"], 3 * l + 2)
    pool.memset(c.zpad[:, :, 0:PAD_C], 0.0)
    pool.tensor_tensor(c.zpad[:, :, PAD_C:], c.ccs, c.cxs, ALU.mult)
    pool.drain()
    w = p["conv_c_w"].rearrange("p (a i) -> p a i", a=AT)
    for i in range(TAPS_C):
        out = c.zacc if i == 0 else c.zt
        pool.tensor_tensor(out, c.zpad[:, :, i:i + SEQ], bc(w[:, :, i], 2, SEQ), ALU.mult)
        pool.drain()
        if i:
            pool.tensor_tensor(c.zacc, c.zacc, c.zt, ALU.add)
            pool.drain()
    pool.wait_ge(s["c_cev"], 3 * l + 3)
    pool.tensor_tensor(c.mixT[:, AT + 2:KT, :], c.zacc, c.cbs, ALU.mult).then_inc(s["c_yc"], 1)



NAMES = [
    "x", "e_w_in", "e_w_out", "e_ffn_w_gate", "e_ffn_w_up", "e_ffn_w_down", "o_w_in", "o_w_out",
    "o_moe_w_gate", "o_moe_w_up", "o_moe_w_down", "ffn1_w_gate_2", "ffn1_w_up_2", "ffn1_w_down_2",
    "w_in_2", "w_out_2", "ffn2_w_gate_2", "ffn2_w_up_2", "ffn2_w_down_2",
]
STAGES = 99


def first_hi(act, m, v):
    return lambda: ffn_hi(act, m, v, "gate", 0), lambda: ffn_hi(act, m, v, "up", 0)


def first_lo(dve, m, v):
    return lambda: ffn_lo(dve, m, v, "gate", 0), lambda: ffn_lo(dve, m, v, "up", 0)


def build(nc, w, out):
    with ExitStack() as ctx:
        m = place(nc, ctx, w)
        m.blocks = mix_blocks(w)
        s = m.sig
        gain2 = [[m.s2[l][f"g{i}"] for i in range(3)] for l in range(LAYERS2)]
        block = ctx.enter_context(nc.Block())

        @block.sync
        def _(sp):
            sp.dma_start(m.res, w["x"][0].rearrange("(t p) d -> p t d", p=P)).then_inc(s["x_in"], 16)
            sp.dma_start(m.consts[:, 0:P], w["consts"][:, 0:P]).then_inc(s["ident_in"], 16)
            sp.dma_start(m.small[:, :], w["small"]).then_inc(s["small_in"], 16)
            load_block(sp, m, B_EVEN)
            sp.dma_start(m.consts[:, P:], w["consts"][:, P:]).then_inc(s["const_in"], 16)
            for i in range(B_EVEN + 1, B_EVEN + 4):
                load_block(sp, m, i)
            sp.dma_start(m.small2[:, :], w["small2"]).then_inc(s["small2_in"], 16)
            for i in range(B_EVEN + 4, B_ODD):
                load_block(sp, m, i)
            if STAGES >= 2:
                def ahead():
                    for i in range(B_ODD, B_ODD + 4):
                        load_block(sp, m, i)
                ffn_load(sp, m, 0, w["e_ffn_w_gate"][0], w["e_ffn_w_up"][0], w["e_ffn_w_down"][0], ahead)
            if STAGES >= 3:
                for i in range(B_ODD + 4, B_SECOND):
                    load_block(sp, m, i)
            if STAGES >= 4:
                moe_load(sp, m)
            if STAGES >= 5:
                for l in range(LAYERS2):
                    first = B_SECOND + 8 * l

                    def ahead(first=first):
                        for i in range(first, first + 4):
                            load_block(sp, m, i)
                    ffn_load(sp, m, 1 + 2 * l, w["ffn1_w_gate_2"][l], w["ffn1_w_up_2"][l], w["ffn1_w_down_2"][l], ahead)
                    for i in range(first + 4, first + 8):
                        load_block(sp, m, i)
                    ffn_load(sp, m, 2 + 2 * l, w["ffn2_w_gate_2"][l], w["ffn2_w_up_2"][l], w["ffn2_w_down_2"][l],
                             lambda: None)
                sp.wait_ge(s["n_xn_d"], 11)
                sp.dma_start(final_gain(m), w["final"]).then_inc(s["final_in"], 16)
                sp.wait_ge(s["out_ready"], 1)
                src = m.xn
            else:
                sp.wait_ge(s["res_ready"], STAGES)
                src = m.res
            sp.dma_start(out[0].rearrange("(t p) d -> p t d", p=P), src).then_inc(s["out_st"], 16)
            sp.wait_ge(s["out_st"], 16)

        @block.tensor
        def _(pe):
            norm_pe(pe, m, 0)
            even_pe(pe, m)
            if STAGES >= 2:
                norm_pe(pe, m, 1)
                ffn_pe(pe, m, 0)
            if STAGES >= 3:
                norm_pe(pe, m, 2)
                odd_pe(pe, m)
            if STAGES >= 4:
                norm_pe(pe, m, 3)
                moe_pe(pe, m)
            if STAGES >= 5:
                for l in range(LAYERS2):
                    norm_pe(pe, m, 4 + 3 * l)
                    ffn_pe(pe, m, 1 + 2 * l)
                    norm_pe(pe, m, 5 + 3 * l)
                    second_pe(pe, m, l)
                    norm_pe(pe, m, 6 + 3 * l)
                    ffn_pe(pe, m, 2 + 2 * l)

        @block.scalar
        def _(act):
            norm_act(act, m, 0, m.s["g0"])
            even_act(act, m)
            if STAGES >= 2:
                norm_act(act, m, 1, m.s["g1"], first_hi(act, m, 0))
                ffn_act(act, m, 0)
            if STAGES >= 3:
                norm_act(act, m, 2, m.s["g2"])
                odd_act(act, m)
            if STAGES >= 4:
                norm_act(act, m, 3, m.s["g3"])
                moe_act(act, m)
            if STAGES >= 5:
                for l in range(LAYERS2):
                    norm_act(act, m, 4 + 3 * l, gain2[l][0], first_hi(act, m, 1 + 2 * l))
                    ffn_act(act, m, 1 + 2 * l)
                    norm_act(act, m, 5 + 3 * l, gain2[l][1])
                    second_act(act, m, l)
                    norm_act(act, m, 6 + 3 * l, gain2[l][2], first_hi(act, m, 2 + 2 * l))
                    ffn_act(act, m, 2 + 2 * l)
                norm_act(act, m, 10, None)

        @block.vector
        def _(dve):
            norm_dve(dve, m, 0, m.s["g0"])
            even_dve(dve, m)
            if STAGES >= 2:
                norm_dve(dve, m, 1, m.s["g1"], first_lo(dve, m, 0))
                ffn_dve(dve, m, 0, 1.0)
            if STAGES >= 3:
                norm_dve(dve, m, 2, m.s["g2"])
                odd_dve(dve, m)
            if STAGES >= 4:
                norm_dve(dve, m, 3, m.s["g3"])
                moe_dve(dve, m)
            if STAGES >= 5:
                dve.wait_ge(s["small2_in"], 16)
                for l in range(LAYERS2):
                    norm_dve(dve, m, 4 + 3 * l, gain2[l][0], first_lo(dve, m, 1 + 2 * l))
                    ffn_dve(dve, m, 1 + 2 * l, 0.5)
                    norm_dve(dve, m, 5 + 3 * l, gain2[l][1])
                    second_dve(dve, m, l)
                    norm_dve(dve, m, 6 + 3 * l, gain2[l][2], first_lo(dve, m, 2 + 2 * l))
                    ffn_dve(dve, m, 2 + 2 * l, 0.5)
                norm_dve(dve, m, 10, None)
                dve.wait_ge(s["final_in"], 16)
                dve.wait_ge(s["n_xn_a"], 11)
                for t in range(NT):
                    last = dve.tensor_tensor(m.xn[:, t, :], m.xn[:, t, :], final_gain(m), ALU.mult)
                dve.drain().then_inc(s["out_ready"], 1)

        @block.gpsimd
        def _(pool):
            if STAGES >= 3:
                odd_pool(pool, m)
            if STAGES >= 5:
                for l in range(LAYERS2):
                    second_pool(pool, m, l)


def final_gain(m):
    return m.xT.rearrange("p k t -> p (k t)")[:, 0:D]



def constants():
    i = np.arange(P)
    f = np.float32
    half = DH // 2
    inv = (f(10000.0) ** (-np.arange(half, dtype=f) / f(half))).astype(f)
    ang = np.arange(SEQ, dtype=f)[:, None] * inv[None, :]
    turn = lambda a: a.astype(f).reshape(NT, P, half).transpose(1, 0, 2).reshape(P, NT * half)
    level = []
    for k in range(NLEV):
        level.append((((i[None, :] >> k) & 1) == 1) & ((i[:, None] >> k) == (i[None, :] >> k) - 1))
    q, k = i[:, None] + P, np.arange(2 * P)[None, :]
    parts = {
        "ident": np.eye(P, dtype=f),
        "upto": (i[:, None] <= i[None, :]).astype(f),
        "before": (i[:, None] < i[None, :]).astype(f),
        "ones": np.ones((P, P), f),
        "iota": np.broadcast_to(i.astype(f), (P, P)),
        "level": np.concatenate(level, 1).astype(f),
        "future": np.where(i[:, None] <= i[None, :], f(0), f(NEG)),
        "window": np.where((q - k >= 0) & (q - k < P), f(0), f(NEG)),
        "cos": turn(np.cos(ang)), "sin": turn(np.sin(ang)),
        "eight": np.broadcast_to(np.arange(NE, 0, -1).astype(f), (P, NE)),
    }
    return np.concatenate([parts[n] for n in CONST_COLS], 1).astype(f)


def by_partition(a):
    a = a.reshape(-1, a.shape[-1] // P, P)
    return a.transpose(2, 1, 0).reshape(P, -1)


def rows(a, times=1):
    a = np.tile(a.reshape(1, -1), (1, times))
    return np.broadcast_to(a, (P, a.shape[1]))


def block_diagonal(a):
    out = np.zeros((P, LT, P), a.dtype)
    for h in range(a.shape[0]):
        r = slice((h % 2) * 64, (h % 2 + 1) * 64)
        out[r, h // 2, r] = a[h]
    return out.reshape(P, LT * P)


def kernel(**inputs):
    import concourse.bacc as bacc
    from concourse.bass_utils import run_bass_kernel_spmd

    a = {n: np.ascontiguousarray(v) for n, v in inputs.items()}
    parts = {
        "g0": by_partition(a["ln_mix"][0]), "g1": by_partition(a["ln_ffn"][0]),
        "g2": by_partition(a["ln_mix"][1]), "g3": by_partition(a["ln_ffn"][1]),
        "lconv_w": by_partition(a["e_lru_conv_w"][0]), "lconv_b": by_partition(a["e_lru_conv_b"][0]),
        "b_a": by_partition(a["e_lru_b_a"][0]), "b_i": by_partition(a["e_lru_b_i"][0]),
        "lam": by_partition(a["e_lru_lambda"][0]),
        "qk_gain": np.concatenate([rows(a["e_q_norm"][0], HQ), rows(a["e_k_norm"][0], HKV)], 1),
        "sinks": rows(a["e_sinks"][0], NT),
        "w_a": block_diagonal(a["e_lru_w_a"][0]), "w_i": block_diagonal(a["e_lru_w_i"][0]),
        "oconv_w": by_partition(a["o_conv_w"][0]),
        "a_log": rows(a["o_a_log"][0], NT), "dt_bias": rows(a["o_dt_bias"][0], NT),
        "out_gain": rows(a["o_out_norm"][0]),
        "w_ab": a["o_w_in"][0][:, 4096:].reshape(KT, P, 2 * GH).transpose(1, 0, 2).reshape(P, -1),
        "router": a["o_router"][0].reshape(KT, P, NE).transpose(1, 0, 2).reshape(P, -1),
    }
    small = np.concatenate([parts[n] for n in SMALL_COLS], 1)
    small2 = []
    for l in range(LAYERS2):
        parts = {
            "g0": by_partition(a["ffn1_norm_2"][l]), "g1": by_partition(a["mix_norm_2"][l]),
            "g2": by_partition(a["ffn2_norm_2"][l]),
            "conv_a_w": by_partition(a["conv_a_w_2"][l]), "conv_a_b": by_partition(a["conv_a_b_2"][l]),
            "ln_a_g": by_partition(a["ln_a_g_2"][l]), "ln_a_b": by_partition(a["ln_a_b_2"][l]),
            "ln_v_g": rows(a["ln_v_g_2"][l]), "ln_v_b": rows(a["ln_v_b_2"][l]),
            "w_s": a["w_s_2"][l].transpose(2, 0, 1).reshape(P, HB * P), "b_s": a["b_s_2"][l].T,
            "conv_c_w": by_partition(a["conv_c_w_2"][l]),
        }
        small2.append(np.concatenate([parts[n] for n in SMALL2_COLS], 1))

    arrays = {n: a[n] for n in NAMES}
    arrays["small"] = np.ascontiguousarray(small)
    arrays["small2"] = np.ascontiguousarray(np.concatenate(small2, 1))
    arrays["final"] = np.ascontiguousarray(rows(a["final_norm_2"]))
    arrays["consts"] = np.ascontiguousarray(constants())

    nc = bacc.Bacc("TRN2", target_bir_lowering=False, num_devices=1)
    w = {n: nc.dram_tensor(f"in_{n}", v.shape, F32, kind="ExternalInput").ap() for n, v in arrays.items()}
    out = nc.dram_tensor("out_x", (1, SEQ, D), F32, kind="ExternalOutput").ap()
    build(nc, w, out)
    r = run_bass_kernel_spmd(nc, [{f"in_{n}": v for n, v in arrays.items()}], core_ids=[0])
    return r.results[0]["out_x"]
```
